# Optimizing a Trainium2 kernel written in Bass

```python
import math
import jax, jax.numpy as jnp
from jax import lax
import numpy as np

D_MODEL = 2048
BATCH = 1
SEQ = 256
DEPTH = 1
DEC_BATCH = 8
DEC_SEQ = 8
PAST_LEN = 2048
PAGE_SIZE = 128

PLE_DIM = 256
S5_GROUP = 16
S5_WIDTH = D_MODEL // 2
S5_GROUPS = S5_WIDTH // S5_GROUP
S5_STATE = 64
DN_HEAD_DIM = 128
DN_WIDTH = D_MODEL // 2
DN_HEADS = DN_WIDTH // DN_HEAD_DIM
CONV_WIDTH = 4
CONV_CH = 3 * DN_WIDTH
CHUNK = 64
D_FF = ((-(-(8 * D_MODEL) // 3) + 255) // 256) * 256
OFF_U = S5_WIDTH
OFF_QKV = OFF_U + CONV_CH
OFF_Z = OFF_QKV + DN_WIDTH
OFF_BETA = OFF_Z + DN_HEADS
OFF_A = OFF_BETA + DN_HEADS
OFF_GA = OFF_A + D_MODEL
N_IN = OFF_GA + D_MODEL
EPS = 1e-6

kernel_name = "hybrid_s5_gdn_parallel_decode_step"

def rms_norm(x, g):
    xf = x.astype(jnp.float32)
    y = xf * lax.rsqrt(jnp.mean(xf * xf, axis=-1, keepdims=True) + EPS)
    return (y * g.astype(jnp.float32)).astype(x.dtype)

def l2_norm(x):
    return x * lax.rsqrt(jnp.sum(x * x, axis=-1, keepdims=True) + EPS)

def causal_conv_silu(xc, buf, w):
    L = xc.shape[1]
    xp = jnp.concatenate([buf.astype(xc.dtype), xc], axis=1)
    out = xp[:, 0:L] * w[0]
    for j in range(1, CONV_WIDTH):
        out = out + xp[:, j:j + L] * w[j]
    return jax.nn.silu(out), xp[:, L:]

def s5_mixer(u, h0_re, h0_im, a_re, a_im, b_re, b_im, c_re, c_im, d, log_dt):
    f32 = jnp.float32
    Bsz, L, _ = u.shape
    uf = u.astype(f32)
    ug = uf.reshape(Bsz, L, S5_GROUPS, S5_GROUP)
    dt = jnp.exp(log_dt.astype(f32))[:, None]
    ar = a_re.astype(f32)
    ai = a_im.astype(f32)
    mag = jnp.exp(ar * dt)
    lb_re = mag * jnp.cos(ai * dt)
    lb_im = mag * jnp.sin(ai * dt)
    nr = lb_re - 1.0
    ni = lb_im
    den = ar * ar + ai * ai
    cr = (nr * ar + ni * ai) / den
    ci = (ni * ar - nr * ai) / den
    br = b_re.astype(f32)
    bi = b_im.astype(f32)
    bb_re = cr[..., None] * br - ci[..., None] * bi
    bb_im = cr[..., None] * bi + ci[..., None] * br
    bu_re = jnp.einsum('blgp,gnp->blgn', ug, bb_re)
    bu_im = jnp.einsum('blgp,gnp->blgn', ug, bb_im)
    h0r = h0_re.astype(f32)
    h0i = h0_im.astype(f32)
    bu_re = bu_re.at[:, 0].add(lb_re * h0r - lb_im * h0i)
    bu_im = bu_im.at[:, 0].add(lb_re * h0i + lb_im * h0r)
    a_r = jnp.broadcast_to(lb_re, bu_re.shape)
    a_i = jnp.broadcast_to(lb_im, bu_im.shape)

    def combine(e1, e2):
        a1r, a1i, b1r, b1i = e1
        a2r, a2i, b2r, b2i = e2
        return (a2r * a1r - a2i * a1i,
                a2r * a1i + a2i * a1r,
                a2r * b1r - a2i * b1i + b2r,
                a2r * b1i + a2i * b1r + b2i)

    _, _, hr, hi = lax.associative_scan(combine, (a_r, a_i, bu_re, bu_im), axis=1)
    y = (jnp.einsum('blgn,gpn->blgp', hr, c_re.astype(f32))
         - jnp.einsum('blgn,gpn->blgp', hi, c_im.astype(f32)))
    y = y.reshape(Bsz, L, S5_WIDTH) + d.astype(f32) * uf
    return y, hr[:, -1], hi[:, -1]

def gated_delta_rule(q, k, v, g, beta, S0):
    Bsz, L, H, DK = q.shape
    DV = v.shape[-1]
    C = min(CHUNK, L)
    n = -(-L // C)
    pad = n * C - L
    if pad:
        p4 = ((0, 0), (0, pad), (0, 0), (0, 0))
        p3 = ((0, 0), (0, pad), (0, 0))
        q = jnp.pad(q, p4)
        k = jnp.pad(k, p4)
        v = jnp.pad(v, p4)
        g = jnp.pad(g, p3)
        beta = jnp.pad(beta, p3)

    def to_chunks(t):
        t = t.reshape((Bsz, n, C) + t.shape[2:])
        return jnp.moveaxis(t, (1, 3), (0, 2))

    qc = to_chunks(q)
    kc = to_chunks(k)
    vc = to_chunks(v)
    bc = to_chunks(beta)
    gc = jnp.cumsum(to_chunks(g), axis=-1)
    idx = jnp.arange(C)
    incl = idx[:, None] >= idx[None, :]
    strict = idx[:, None] > idx[None, :]
    decay = jnp.exp(jnp.where(incl, gc[..., :, None] - gc[..., None, :], -jnp.inf))
    kk = jnp.einsum('nbhid,nbhjd->nbhij', kc, kc)
    lower = jnp.where(strict, bc[..., :, None] * kk * decay, 0.0)
    eye = jnp.eye(C, dtype=jnp.float32)
    tmat = lax.linalg.triangular_solve(eye + lower, jnp.broadcast_to(eye, lower.shape),
                                       left_side=True, lower=True)
    u = tmat @ (vc * bc[..., None])
    w = tmat @ (kc * (bc * jnp.exp(gc))[..., None])
    qk = jnp.einsum('nbhid,nbhjd->nbhij', qc, kc) * decay

    def step(S, xs):
        q_i, k_i, u_i, w_i, qk_i, g_i = xs
        v_new = u_i - jnp.einsum('bhcd,bhde->bhce', w_i, S)
        o = (jnp.einsum('bhcd,bhde->bhce', q_i * jnp.exp(g_i)[..., None], S)
             + jnp.einsum('bhij,bhje->bhie', qk_i, v_new))
        g_last = g_i[..., -1:]
        S = (S * jnp.exp(g_last)[..., None]
             + jnp.einsum('bhcd,bhce->bhde', k_i * jnp.exp(g_last - g_i)[..., None], v_new))
        return S, o

    S, o = lax.scan(step, S0, (qc, kc, u, w, qk, gc))
    o = jnp.moveaxis(o, (0, 2), (1, 3)).reshape(Bsz, n * C, H, DV)[:, :L]
    return o, S

def deltanet_mixer(qkv, z, beta_l, a_l, conv_buf, S0, conv_w, a_log, dt_bias, onorm_w):
    f32 = jnp.float32
    qkv, conv_new = causal_conv_silu(qkv, conv_buf, conv_w)
    Bsz, L, _ = qkv.shape
    qkv = qkv.astype(f32)
    q = qkv[..., :DN_WIDTH].reshape(Bsz, L, DN_HEADS, DN_HEAD_DIM)
    k = qkv[..., DN_WIDTH:2 * DN_WIDTH].reshape(Bsz, L, DN_HEADS, DN_HEAD_DIM)
    v = qkv[..., 2 * DN_WIDTH:].reshape(Bsz, L, DN_HEADS, DN_HEAD_DIM)
    q = l2_norm(q) * (DN_HEAD_DIM ** -0.5)
    k = l2_norm(k)
    beta = jax.nn.sigmoid(beta_l.astype(f32))
    g = -jnp.exp(a_log.astype(f32)) * jax.nn.softplus(a_l.astype(f32) + dt_bias.astype(f32))
    o, S_new = gated_delta_rule(q, k, v, g, beta, S0.astype(f32))
    o = o * lax.rsqrt(jnp.mean(o * o, axis=-1, keepdims=True) + EPS) * onorm_w.astype(f32)
    o = o * jax.nn.silu(z.astype(f32).reshape(Bsz, L, DN_HEADS, DN_HEAD_DIM))
    return o.reshape(Bsz, L, DN_WIDTH), conv_new, S_new

def decoder_layer(x, p, conv_buf, S0, h_re, h_im, lw):
    dtype = x.dtype
    h = rms_norm(x, lw['g_mix'])
    proj = h @ lw['w_in']
    u = proj[..., :OFF_U]
    qkv = proj[..., OFF_U:OFF_QKV]
    z = proj[..., OFF_QKV:OFF_Z]
    beta_l = proj[..., OFF_Z:OFF_BETA]
    a_l = proj[..., OFF_BETA:OFF_A]
    gate_a = proj[..., OFF_A:OFF_GA]
    gate_b = proj[..., OFF_GA:]
    y_s5, hr_new, hi_new = s5_mixer(u, h_re, h_im, lw['s5_a_re'], lw['s5_a_im'], lw['s5_b_re'],
                                    lw['s5_b_im'], lw['s5_c_re'], lw['s5_c_im'], lw['s5_d'], lw['s5_log_dt'])
    y_s5 = jax.nn.gelu(y_s5).astype(dtype)
    y_s5 = y_s5 * jax.nn.sigmoid(y_s5 @ lw['w_glu'] + lw['b_glu'])
    y_dn, conv_new, S_new = deltanet_mixer(qkv, z, beta_l, a_l, conv_buf, S0, lw['conv_w'],
                                           lw['a_log'], lw['dt_bias'], lw['onorm_w'])
    y_dn = y_dn.astype(dtype)
    mix = jax.nn.sigmoid(gate_a) * (y_s5 @ lw['w_a']) + jax.nn.sigmoid(gate_b) * (y_dn @ lw['w_b'])
    x = x + mix @ lw['w_out']
    h2 = rms_norm(x, lw['g_ffn'])
    x = x + (jax.nn.silu(h2 @ lw['w_gate']) * (h2 @ lw['w_up'])) @ lw['w_down']
    h3 = rms_norm(x, lw['g_ple'])
    x = x + (p.astype(dtype) @ lw['w_ple']) * jax.nn.sigmoid(h3 @ lw['w_ple_gate'])
    return x, conv_new.astype(dtype), S_new.astype(dtype), hr_new.astype(dtype), hi_new.astype(dtype)

def setup_inputs(seed: int = 0) -> dict:
    key = jax.random.key(seed)
    ks = list(jax.random.split(key, 48))
    f32 = jnp.float32

    def nrm(shape, scale):
        return jax.random.normal(ks.pop(), shape, f32) * scale

    def unif(shape, lo, hi):
        return jax.random.uniform(ks.pop(), shape, f32, lo, hi)

    out = {}
    out['x_prompt'] = nrm((BATCH, SEQ, D_MODEL), 1.0)
    out['x_sample'] = nrm((DEC_BATCH, DEC_SEQ, D_MODEL), 1.0)
    out['state_conv'] = nrm((DEPTH, DEC_BATCH, CONV_WIDTH - 1, CONV_CH), 1.0)
    out['state_delta'] = nrm((DEPTH, DEC_BATCH, DN_HEADS, DN_HEAD_DIM, DN_HEAD_DIM), 0.1)
    out['state_s5_re'] = nrm((DEPTH, DEC_BATCH, S5_GROUPS, S5_STATE), 0.5)
    out['state_s5_im'] = nrm((DEPTH, DEC_BATCH, S5_GROUPS, S5_STATE), 0.5)
    out['p_prompt'] = nrm((DEPTH, BATCH, SEQ, PLE_DIM), 1.0)
    out['p_sample'] = nrm((DEPTH, DEC_BATCH, DEC_SEQ, PLE_DIM), 1.0)
    out['g_mix'] = 1.0 + nrm((DEPTH, D_MODEL), 0.02)
    out['w_in'] = nrm((DEPTH, D_MODEL, N_IN), D_MODEL ** -0.5)
    out['conv_w'] = nrm((DEPTH, CONV_WIDTH, CONV_CH), CONV_WIDTH ** -0.5)
    out['a_log'] = jnp.log(unif((DEPTH, DN_HEADS), 1.0, 16.0))
    dt = jnp.exp(unif((DEPTH, DN_HEADS), math.log(1e-3), math.log(1e-1)))
    out['dt_bias'] = dt + jnp.log(-jnp.expm1(-dt))
    out['onorm_w'] = 1.0 + nrm((DEPTH, DN_HEAD_DIM), 0.02)
    out['s5_a_re'] = -0.5 + nrm((DEPTH, S5_GROUPS, S5_STATE), 0.01)
    out['s5_a_im'] = jnp.pi * jnp.arange(S5_STATE, dtype=f32) + nrm((DEPTH, S5_GROUPS, S5_STATE), 0.01)
    out['s5_b_re'] = nrm((DEPTH, S5_GROUPS, S5_STATE, S5_GROUP), (2 * S5_GROUP) ** -0.5)
    out['s5_b_im'] = nrm((DEPTH, S5_GROUPS, S5_STATE, S5_GROUP), (2 * S5_GROUP) ** -0.5)
    out['s5_c_re'] = nrm((DEPTH, S5_GROUPS, S5_GROUP, S5_STATE), (2 * S5_STATE) ** -0.5)
    out['s5_c_im'] = nrm((DEPTH, S5_GROUPS, S5_GROUP, S5_STATE), (2 * S5_STATE) ** -0.5)
    out['s5_d'] = nrm((DEPTH, S5_WIDTH), 1.0)
    out['s5_log_dt'] = unif((DEPTH, S5_GROUPS), math.log(1e-3), math.log(1e-1))
    out['w_glu'] = nrm((DEPTH, S5_WIDTH, S5_WIDTH), S5_WIDTH ** -0.5)
    out['b_glu'] = nrm((DEPTH, S5_WIDTH), 0.01)
    out['w_a'] = nrm((DEPTH, S5_WIDTH, D_MODEL), S5_WIDTH ** -0.5)
    out['w_b'] = nrm((DEPTH, DN_WIDTH, D_MODEL), DN_WIDTH ** -0.5)
    out['w_out'] = nrm((DEPTH, D_MODEL, D_MODEL), D_MODEL ** -0.5)
    out['g_ffn'] = 1.0 + nrm((DEPTH, D_MODEL), 0.02)
    out['w_gate'] = nrm((DEPTH, D_MODEL, D_FF), D_MODEL ** -0.5)
    out['w_up'] = nrm((DEPTH, D_MODEL, D_FF), D_MODEL ** -0.5)
    out['w_down'] = nrm((DEPTH, D_FF, D_MODEL), D_FF ** -0.5)
    out['g_ple'] = 1.0 + nrm((DEPTH, D_MODEL), 0.02)
    out['w_ple'] = nrm((DEPTH, PLE_DIM, D_MODEL), PLE_DIM ** -0.5)
    out['w_ple_gate'] = nrm((DEPTH, D_MODEL, D_MODEL), D_MODEL ** -0.5)
    out['g_final'] = 1.0 + nrm((D_MODEL,), 0.02)
    return out

def reference(x_prompt, x_sample, state_conv, state_delta, state_s5_re, state_s5_im, p_prompt, p_sample,
              g_mix, w_in, conv_w, a_log, dt_bias, onorm_w, s5_a_re, s5_a_im, s5_b_re, s5_b_im,
              s5_c_re, s5_c_im, s5_d, s5_log_dt, w_glu, b_glu, w_a, w_b, w_out, g_ffn, w_gate, w_up,
              w_down, g_ple, w_ple, w_ple_gate, g_final):
    dt_x = x_prompt.dtype
    zc = jnp.zeros((BATCH, CONV_WIDTH - 1, CONV_CH), dt_x)
    zd = jnp.zeros((BATCH, DN_HEADS, DN_HEAD_DIM, DN_HEAD_DIM), dt_x)
    zs = jnp.zeros((BATCH, S5_GROUPS, S5_STATE), dt_x)
    yp = x_prompt
    ys = x_sample
    pc, pd, pr, pi_ = [], [], [], []
    sc, sd, sr, si = [], [], [], []
    for i in range(DEPTH):
        lw = dict(g_mix=g_mix[i], w_in=w_in[i], conv_w=conv_w[i], a_log=a_log[i], dt_bias=dt_bias[i],
                  onorm_w=onorm_w[i], s5_a_re=s5_a_re[i], s5_a_im=s5_a_im[i], s5_b_re=s5_b_re[i],
                  s5_b_im=s5_b_im[i], s5_c_re=s5_c_re[i], s5_c_im=s5_c_im[i], s5_d=s5_d[i],
                  s5_log_dt=s5_log_dt[i], w_glu=w_glu[i], b_glu=b_glu[i], w_a=w_a[i], w_b=w_b[i],
                  w_out=w_out[i], g_ffn=g_ffn[i], w_gate=w_gate[i], w_up=w_up[i], w_down=w_down[i],
                  g_ple=g_ple[i], w_ple=w_ple[i], w_ple_gate=w_ple_gate[i])
        yp, c1, d1, r1, m1 = decoder_layer(yp, p_prompt[i], zc, zd, zs, zs, lw)
        ys, c2, d2, r2, m2 = decoder_layer(ys, p_sample[i], state_conv[i], state_delta[i],
                                           state_s5_re[i], state_s5_im[i], lw)
        pc.append(c1); pd.append(d1); pr.append(r1); pi_.append(m1)
        sc.append(c2); sd.append(d2); sr.append(r2); si.append(m2)
    y_prompt = rms_norm(yp, g_final)
    y_sample = rms_norm(ys, g_final)
    return (y_prompt, y_sample,
            jnp.stack(pc), jnp.stack(pd), jnp.stack(pr), jnp.stack(pi_),
            jnp.stack(sc), jnp.stack(sd), jnp.stack(sr), jnp.stack(si))


_drawn_inputs = setup_inputs


def setup_inputs(seed=0):
    import zlib

    import numpy as np

    out = dict(_drawn_inputs(seed))
    spreads = {}
    factors = {'onorm_w': 8.0,
     's5_a_re': 17.267,
     'b_glu': 64.0,
     'g_ffn': 4.407,
     'g_ple': 64.0,
     'g_final': 7.687}
    for name, (base, spread) in spreads.items():
        noise = np.random.default_rng([zlib.crc32(name.encode()), seed]).standard_normal(out[name].shape)
        drawn = base * np.exp(spread * noise) if base else spread * noise
        out[name] = __import__('jax').numpy.asarray(drawn.astype(out[name].dtype))
    for name, factor in factors.items():
        out[name] = (out[name] * factor).astype(out[name].dtype)
    return out
```

```python
import math
from contextlib import ExitStack

import concourse.bass as bass
from concourse import mybir

F32 = mybir.dt.float32
F32R = mybir.dt.float32r
BF16 = mybir.dt.bfloat16
ACT = mybir.ActivationFunctionType
ALU = mybir.AluOpType
AX = mybir.AxisListType

P = 128
NPR = 256
NB, NL = 8, 8
NSM = NB * NL
N = NPR + NSM
D = 2048
KD = D // P
W5 = D // 2
K5 = W5 // P
H = 8
CW = 4
CCH = 3 * W5
KC = CCH // P
SEQP = CW - 1 + NPR
SEQS = CW - 1 + NL
NPAD = SEQP + NB * SEQS
NCV = NPAD - (CW - 1)
FF = 5632
KF = FF // P
FCH = 2
KFC = KF // FCH
PLE = 256
ST = 64
NT = 32
EPS = 1e-6
OFF_U, OFF_QKV = W5, W5 + CCH
OFF_Z = OFF_QKV + W5
OFF_BETA = OFF_Z + H
OFF_A = OFF_BETA + H
OFF_GA = OFF_A + D
CHUNKS = [(0, 128), (128, 128), (256, 64)]
LEVELS = [7, 7, 3]
UK = 4
RING = 4
PW = 256
MAGIC = 1.5 * 2.0 ** 23
TWO_PI_PARTS = (6.28125, 0.0019350051879882812, 3.019916e-07)


class Steps:

    def __init__(self, eng, sem):
        self.eng, self.sem, self.n, self.off = eng, sem, 0, 0

    def step(self, ins):
        ins.then_inc(self.sem, 1)
        self.n += 1

    def settle(self):
        if self.n or not isinstance(self.off, int):
            self.eng.wait_ge(self.sem, self.off + self.n)

    def link(self, ins):
        self.step(ins)
        self.settle()


def side_fills():
    order = [("b", ("par",)), ("a", ("cst",))]
    order += [("ab"[j % 2], ("x", j)) for j in range(KD // 2)]
    order += [("a", ("norm", 0)), ("b", ("s5par",)), ("a", ("h0",)), ("b", ("bbt", 0)), ("a", ("bbt", 1)),
              ("b", ("ct", 0)), ("a", ("ct", 1)), ("b", ("ba",))]
    for hq in range(NT // 2):
        order += [("a", ("bu", hq, 0)), ("b", ("bu", hq, 1))]
        if hq:
            order += [("a", ("y", hq - 1))]
    order += [("a", ("y", NT // 2 - 1)), ("b", ("hl",))]
    order += [("ab"[j % 2], ("tail", j)) for j in range(3)]
    order += [("ba"[j % 2], ("l2", j)) for j in range(H)]
    for c in range(3):
        order += [("b", ("gcum", c)), ("a", ("grow", c)), ("b", ("brow", c)), ("a", ("kt", c)), ("b", ("vt", c)),
                  ("a", ("kk", c)), ("b", ("qk", c))]
        for k in range(LEVELS[c]):
            order += [("a", ("m1", c, k)), ("b", ("ta", c, k)), ("a", ("tb", c, k))]
        if c == 1:
            order += [("b", ("ks", 1))]
        if c == 2:
            order += [("ba"[h % 2], ("sq", h)) for h in range(H)] + [("b", ("ks", 2))]
        order += [("a", ("vn", c)), ("b", ("o", c))]
        if c < 2:
            order += [("a", ("s", c))]
        else:
            order += [("ab"[h % 2], ("su", h)) for h in range(H)]
    order += [("ab"[j % 2], ("on", j)) for j in range(H // 2)]
    order += [("a", ("norm", 1)), ("b", ("pt",)), ("a", ("norm", 2)), ("b", ("norm", 3))]
    order += [("ab"[j % 2], ("fin", j)) for j in range(6)]
    count, at = {"a": 0, "b": 0}, {}
    for region, key in order:
        at[key] = (region, count[region])
        count[region] += 1
    return at


def mixer_pairs():
    return ([("u", i, KD) for i in range(4)] + [("qkv", i, KD) for i in range(12)]
            + [("z", i, KD) for i in range(4)] + [("gate", i, KD) for i in range(16)]
            + [("glu", i, K5) for i in range(4)] + [("wa", i, K5) for i in range(8)]
            + [("wb", i, K5) for i in range(8)])


def schedule():
    pairs = mixer_pairs()
    units = [(p, j) for p, (_, _, k) in enumerate(pairs) for j in range(-(-k // UK))]
    first = {}
    for n, (p, j) in enumerate(units):
        first.setdefault(pairs[p][0], n)
    slots, at = [], 0

    def slot(sides, n):
        nonlocal at
        slots.append((sides, units[at:at + n]))
        at += n

    slot([("const",), ("par",)] + [("x", j) for j in range(KD // 2)] + [("s5prep",)], 4)
    slot([("norm", 0), ("s5par",), ("h0",), ("bmix",)], 3)
    slot([("bb",), ("ct",)], 4)
    slot([("ba",)], 4)
    for hq in range(NT // 2):
        slot([("s5", hq)], 3)
    slot([("s5y",)], 1)
    slot([], first["z"] + 4 - at)
    slot([("tailc",), ("s5out",), ("tail",)], 1)
    for h in range(H):
        slot([("conv", h)], 1)
    slot([("l2a", 0)], 1)
    for j in range(H):
        slot([("l2", j)] + [("l2a", j + 1)] * (j + 1 < H), 1)
    for c in range(3):
        slot([("dg", c)], 1)
        slot([("dkv", c)], 1)
        slot([("dkk", c)], 1)
        for k in range(LEVELS[c]):
            slot([("m1", c, k)], 1)
            slot([("tab", c, k)], 1)
        if c == 2:
            slot([("sq",)], 1)
        if c:
            slot([("ks", c)], 1)
        slot([("vn", c)], 1)
        slot([("o", c)], 1)
        if c < 2:
            slot([("s", c)], 1)
        else:
            for h in range(H):
                slot([("su", h)], 0)
    assert at <= first["glu"]
    slot([], first["glu"] + 2 - at)
    slot([("ysplit",)], 0)
    slot([], first["wa"] + 6 - at)
    slot([("ona", 0)], 0)
    for j in range(H // 2):
        slot([("on", j)] + [("ona", j + 1)] * (j + 1 < H // 2), 2)
    slot([], len(units) - at)
    uses, prev = [], None
    for sides, us in slots:
        for p, j in us:
            if j == -(-pairs[p][2] // UK) - 1:
                if prev and prev[0] in ("wa", "wb"):
                    uses.append(prev)
                prev = pairs[p][0:2]
        uses += [key for key in sides if key[0] == "on"]
    uses.append(prev)
    return pairs, units, slots, uses


class Zone:

    def __init__(self, nc, at, size):
        self.nc, self.at, self.end = nc, at, at + size

    def take(self, name, shape, dt=F32):
        size = math.prod(shape[1:]) * (2 if dt == BF16 else 4)
        size = -(-size // 32) * 32
        assert self.at + size <= self.end, (name, self.at + size - self.end)
        t = self.nc.alloc_sbuf_tensor_at(name, list(shape), dt, offset=self.at)
        self.at += size
        return t


def hybrid_layer(nc, x_prompt, x_sample, state_conv, state_delta, state_s5_re, state_s5_im, p_prompt, p_sample,
                 g_mix, w_in, conv_w, a_log, dt_bias, onorm_w, s5_a_re, s5_a_im, s5_b_re, s5_b_im,
                 s5_c_re, s5_c_im, s5_d, s5_log_dt, w_glu, b_glu, w_a, w_b, w_out, g_ffn, w_gate, w_up,
                 w_down, g_ple, w_ple, w_ple_gate, g_final,
                 y_prompt, y_sample, conv_prompt, delta_prompt, s5_re_prompt, s5_im_prompt,
                 conv_sample, delta_sample, s5_re_sample, s5_im_sample):
    pairs, units, slots, uses = schedule()
    fill_at = side_fills()
    pair_units = [-(-k // UK) for _, _, k in pairs]
    pair_first = [sum(pair_units[:p]) for p in range(len(pairs))]
    pair_of = {(kind, i): p for p, (kind, i, _) in enumerate(pairs)}
    MIX_UNITS, MIX_PAIRS = len(units), len(pairs)
    OUT_U, OUT_P = MIX_UNITS, MIX_PAIRS
    FFN_U = [OUT_U + 4 * 8, 0]
    FFN_P = [OUT_P + 8, 0]
    DOWN_U, DOWN_P = [0, 0], [0, 0]
    DU = -(-KFC // UK)
    for c in range(FCH):
        DOWN_U[c], DOWN_P[c] = FFN_U[c] + 8 * (KFC // 2), FFN_P[c] + KFC
        if c + 1 < FCH:
            FFN_U[c + 1], FFN_P[c + 1] = DOWN_U[c] + 8 * DU, DOWN_P[c] + 8
    PLE_U, PLE_P = DOWN_U[-1] + 8 * DU, DOWN_P[-1] + 8
    assert MIX_UNITS % RING == 0 and OUT_U % RING == 0 and all(u % RING == 0 for u in FFN_U + DOWN_U)

    with ExitStack() as ctx:
        sem_of = {}

        def sem(name):
            if name not in sem_of:
                sem_of[name] = ctx.enter_context(nc.semaphore(name))
            return sem_of[name]

        base = -(-nc.sbuf_base // 32) * 32
        size = nc.sbuf_usable_end - base
        zw = Zone(nc, base, RING * 12 * 1024)
        raw = zw.take("raw", [P, RING, UK, PW])
        whi = zw.take("whi", [P, RING, UK, PW], F32R)
        wlo = zw.take("wlo", [P, RING, UK, PW], F32R)
        zx = Zone(nc, zw.end, 2 * KD * N * 4)
        xhi = zx.take("xhi", [P, KD, N], F32R)
        xlo = zx.take("xlo", [P, KD, N], F32R)
        zq_at = zx.end
        zq = Zone(nc, zq_at, KC * NPAD * 4)
        qkv = zq.take("qkv", [P, KC, NPAD])
        zy = Zone(nc, zq.end, K5 * N * 4)
        yt = zy.take("yt", [P, K5, N])
        zc = Zone(nc, zy.end, 10240)
        ident = zc.take("ident", [P, P])
        ones = zc.take("ones", [P, P])
        cum = zc.take("cum", [P, P])
        cums = zc.take("cums", [NSM, NSM])
        strict = zc.take("strict", [P, P], BF16)
        stricts = zc.take("stricts", [NSM, NSM], BF16)
        lvl = zc.take("lvl", [P, 7, P], BF16)
        inv = zc.take("inv", [P, N])
        start = zc.take("start", [P, N])
        par1 = zc.take("par1", [P, 81])
        par2 = zc.take("par2", [P, CW * KC])
        half = zc.take("half", [P, 2])
        cst = zc.take("cst", [P, 4])
        seqm = zc.take("seqm", [NSM, NB])
        invt = zc.take("invt", [P, 4])
        gab = zc.take("gab", [P, 2 * H])
        bet = zc.take("bet", [P, 3, H])
        gt = zc.take("gt", [P, 3, H])
        gc = zc.take("gc", [P, 3, H])
        nbe = zc.take("nbe", [P, 3, H])
        ba = zc.take("ba", [P, 3, 2 * H])
        egl = zc.take("egl", [P, H, NB])
        dl = zc.take("dl", [P, H])
        egc = zc.take("egc", [P, H])
        sp3 = zc.take("sp3", [P, 3, H])
        G_MIX, G_FFN, G_PLE, G_FINAL, D5, BGLU, ONW = 0, 16, 32, 48, 64, 72, 80
        arena_at = zc.end
        arena = base + size - arena_at

        zs = Zone(nc, arena_at, arena)
        sq = zs.take("sq", [P, 2, N])
        acc = zs.take("acc", [P, N])
        arena_at, arena = zs.at, arena - (zs.at - arena_at)
        zt = Zone(nc, arena_at, arena)
        xtok = zt.take("xtok", [P, 3, D])
        xt0 = Zone(nc, zq_at, KC * NPAD * 4).take("xt0", [P, KD, N])

        z5 = Zone(nc, arena_at, arena)
        uu = z5.take("uu", [P, 2, 2, 2, N])
        gg = z5.take("gg", [P, 2, 2, 2, N])
        tt = z5.take("tt", [P, 2, 2, N])
        bbt = z5.take("bbt", [P, 2, K5, P])
        ct = z5.take("ct", [P, 2, K5, P])
        tb = z5.take("tb", [P, 2, NT, 16])
        bu = z5.take("bu", [P, 2, 2, N])
        mm = z5.take("mm", [P, 2, N])
        ta = z5.take("ta", [P, 2, NT, 16])
        a0 = z5.take("a0", [P, 2, NT, NB])
        sp5 = z5.take("sp5", [P, 7, NT])
        pt5 = z5.take("pt5", [P, 2, 2, 256])
        hl = Zone(nc, arena_at - 3 * N * 4, 2 * N * 4).take("hl", [P, 2, NB + 1, NT])
        zpre = Zone(nc, zq_at + KD * N * 4, (KC * NPAD - KD * N) * 4)
        spar = zpre.take("spar", [NT, 3, P])
        sc5 = zpre.take("sc5", [NT, 16, P])
        wba = zpre.take("wba", [P, KD, 2 * H])
        zpre2 = Zone(nc, arena_at, 5 * 2 * 2 * N * 4)
        bnat = zpre2.take("bnat", [P, 2, NT, 16])
        bmix = zpre2.take("bmix", [P, 2, NT, 2, 16])
        bt1 = zpre2.take("bt1", [P, NT, 16])
        bt2 = zpre2.take("bt2", [P, NT, 16])
        cnat = zpre2.take("cnat", [P, 2, K5, 2, ST])
        sc5w = zpre2.take("sc5w", [P, 8, NT])
        bu_at = arena_at + 5 * 2 * 2 * N * 4 + (2 * 2 * K5 * P + 2 * NT * 16) * 4
        zpre3 = Zone(nc, bu_at, 2 * 2 * N * 4)
        h0n = zpre3.take("h0n", [P, 2, 2, P])
        h0s = zpre3.take("h0s", [P, 2, NT, NB])
        cstt = Zone(nc, bu_at + 2 * 2 * N * 4, 2 * N * 4).take("cstt", [P, KC, 3 * NB])
        hlo = Zone(nc, arena_at + 16384, 3072).take("hlo", [P, 2, 3, P])
        zpar = Zone(nc, arena_at + 3 * D * 4 + 32, 2048 + CCH * 4)
        par1n = zpar.take("par1n", [81, P])
        par2n = zpar.take("par2n", [CW * KC, P])
        csn = zpar.take("csn", [3 * NB, CCH])

        zd = Zone(nc, arena_at, arena)
        kt = zd.take("kt", [P, H, N])
        qt = zd.take("qt", [P, H, N])
        s_ = zd.take("s_", [P, H, P])
        ktok = zd.take("ktok", [P, H, P])
        vb = zd.take("vb", [P, H, P])
        vn = zd.take("vn", [P, H, P])
        eg = zd.take("eg", [P, H, P])
        dt_ = zd.take("dt_", [P, H, P])
        qkd = zd.take("qkd", [P, H, P])
        stg = zd.take("stg", [P, 2, 2, N])
        g1 = zd.take("g1", [P, 2, N])
        gr = zd.take("gr", [P, 2, 2, N])
        vsm = zd.take("vsm", [P, H, NSM])
        zl = Zone(nc, zq_at, 2 * H * NPAD * 4)
        lt = zl.take("lt", [P, H, P])
        ltm = zl.take("ltm", [P, H, P])
        m1 = zl.take("m1", [P, H, P])
        tm = zl.take("tm", [P, H, P])
        tmt = zl.take("tmt", [P, H, P])
        kb = m1
        zc2 = Zone(nc, arena_at + 2 * K5 * N * 4, 6 * 4096)
        cacc = zc2.take("cacc", [P, 2, 3, NPAD])
        sql = zc2.take("sql", [P, 2, NPAD])
        rl = zc2.take("rl", [P, 2, NPAD])
        zt2 = Zone(nc, arena_at, 2 * K5 * N * 4)
        tail = zt2.take("tail", [P, KC, 3 + 3 * NB])
        ttok = zt2.take("ttok", [27, CCH])
        zs2 = Zone(nc, arena_at + 2 * K5 * N * 4, 16384)
        sqt = zs2.take("sqt", [P, H, P])
        zst = Zone(nc, zq_at, 4 * 4096)
        st1 = zst.take("st1", [P, NB, P])
        st2 = zst.take("st2", [P, NB, P])
        vnb = zst.take("vnb", [NSM, 2, NB, P])
        st_ring = [st1, st2]

        x_at, half_x = zx.at - 2 * KD * N * 4, K5 * N * 4
        yhi = Zone(nc, x_at, half_x).take("yhi", [P, K5, N], F32R)
        ylo = Zone(nc, x_at + half_x, half_x).take("ylo", [P, K5, N], F32R)
        dhi = Zone(nc, x_at, half_x).take("dhi", [P, K5, N], F32R)
        dlo = Zone(nc, x_at + half_x, half_x).take("dlo", [P, K5, N], F32R)
        ghi = Zone(nc, x_at + 2 * half_x, half_x).take("ghi", [P, K5, N], F32R)
        glo = Zone(nc, x_at + 3 * half_x, half_x).take("glo", [P, K5, N], F32R)
        mxhi = Zone(nc, arena_at, KD * N * 4).take("mxhi", [P, KD, N], F32R)
        zm = Zone(nc, arena_at + KD * N * 4, KD * N * 4 + 2560)
        mixa = zm.take("mixa", [P, KD, N])
        t1 = zm.take("t1", [P, 2, N])
        mxlo = Zone(nc, arena_at + KD * N * 4, KD * N * 4).take("mxlo", [P, KD, N], F32R)

        xt = Zone(nc, zq_at, KD * N * 4).take("xt", [P, KD, N])
        zf2 = Zone(nc, zq_at + KD * N * 4, (KC * NPAD - KD * N) * 4)
        fg1 = zf2.take("fg1", [P, 2, N])
        fsg = zf2.take("fsg", [P, 2, N])
        fsi = zf2.take("fsi", [P, 2, N])
        fmd = zf2.take("fmd", [P, 2, N])
        pf = zf2.take("pf", [P, 2, N])
        zp = Zone(nc, zy.at - K5 * N * 4, K5 * N * 4)
        phi = zp.take("phi", [P, 2, N], F32R)
        plo = zp.take("plo", [P, 2, N], F32R)
        ptok = zp.take("ptok", [P, 3, PLE])
        zmid = Zone(nc, arena_at, arena)
        mhi = zmid.take("mhi", [P, KFC, N], F32R)
        mlo = zmid.take("mlo", [P, KFC, N], F32R)
        zo = Zone(nc, arena_at, arena)
        yo = zo.take("yo", [P, 2, D])
        xg = zo.take("xg", [P, KD, N])

        scr_x = nc.dram_tensor("scratch_x", [P, KD, N], F32, kind="Internal").ap()
        scr_g = nc.dram_tensor("scratch_gates", [P, 40, N], F32, kind="Internal").ap()

        pg = ctx.enter_context(nc.psum_tensor("pg", [P, 2, 2, 512], F32))
        side_ps = {r: ctx.enter_context(nc.psum_tensor(f"side_{r}", [P, 2, 512], F32)) for r in "ab"}
        filled = {r: sem(f"side_{r}_filled") for r in "ab"}
        drained = {r: sem(f"side_{r}_drained") for r in "ab"}

        def ps(key):
            return side_ps[fill_at[key][0]]

        def wait_filled(eng, key):
            r, i = fill_at[key]
            eng.wait_ge(filled[r], i + 1)

        def wait_drained(eng, key):
            r, i = fill_at[key]
            eng.wait_ge(drained[r], i + 1)

        def drain(ins, key):
            ins.then_inc(drained[fill_at[key][0]], 1)

        def heads(t, c):
            return t[:, :, 0:CHUNKS[c][1]]

        def hview(key, c, n=None, rows=P):
            n = n or CHUNKS[c][1]
            return ps(key)[0:rows, :, 0:4 * n].rearrange("p k (h c) -> p k h c", h=4)

        def hsplit(ap):
            return ap.rearrange("p (k h) c -> p k h c", k=2)

        raw_landed = [sem(f"raw_landed_{r}") for r in range(RING)]
        w_hi, w_lo, multiplied = sem("w_hi_ready"), sem("w_lo_ready"), sem("units_multiplied")
        evacuated = sem("pair_evacuated")

        def rows_of(w, k0, nk, cols):
            return w[0, k0 * P:(k0 + nk) * P, cols].rearrange("(k p) c -> p k c", p=P)

        mixer_w = {"u": (w_in, 0), "qkv": (w_in, OFF_U), "z": (w_in, OFF_QKV), "gate": (w_in, OFF_A),
                   "glu": (w_glu, 0), "wa": (w_a, 0), "wb": (w_b, 0)}

        block = ctx.enter_context(nc.Block())

        @block.sync
        def _(sp):
            def load_unit(u, r, src, nk, first_lap=False):
                if not first_lap:
                    sp.wait_ge(w_hi, u - RING + 1)
                    sp.wait_ge(w_lo, u - RING + 1)
                sp.dma_start(raw[:, r, 0:nk, :], src).then_inc(raw_landed[r], 16)

            tokens = [(x_prompt[0, 0:P], P), (x_prompt[0, P:2 * P], P), (x_sample.rearrange("b l d -> (b l) d"), NSM)]
            for c, (src, n) in enumerate(tokens):
                sp.dma_start(xtok[0:n, c, :], src).then_inc(sem("x_landed"), 16)

            def load_mixer(n):
                p, j = units[n]
                kind, i, k = pairs[p]
                w, off = mixer_w[kind]
                nk = min(UK, k - UK * j)
                load_unit(n, n % RING, rows_of(w, UK * j, nk, slice(off + PW * i, off + PW * (i + 1))), nk, n < RING)

            def spill(n):
                sp.wait_ge(sem("stage_written"), n + 1)
                sp.dma_start(scr_g[:, 2 * n:2 * n + 2, :], stg[:, n % 2]).then_inc(sem(f"stage_stored_{n % 2}"), 16)

            spilled = 0
            for _, us in slots:
                for p, j in us:
                    load_mixer(units.index((p, j)))
                    if j == pair_units[p] - 1 and p >= 2 and pairs[p - 2][0] in ("z", "gate"):
                        spill(spilled)
                        spilled += 1

            sp.wait_ge(sem("x_stored"), 16)
            sp.wait_ge(sem("on_ready"), H // 2)
            for s in range(2):
                sp.wait_ge(sem(f"st_stored_{s}"), 16 * (H // 2))
            sp.dma_start(xt[:], scr_x).then_inc(sem("xt_landed"), 16)

            with sp.Fori(0, 4) as it:
                for b in range(2):
                    for j in range(4):
                        load_unit(OUT_U + it * 8 + 4 * b + j, j,
                                  rows_of(w_out, UK * j, UK, bass.ds((it * 2 + b) * PW, PW)), UK)
            for c, (src, n) in enumerate([(p_prompt[0, 0, 0:P], P), (p_prompt[0, 0, P:2 * P], P),
                                          (p_sample[0].rearrange("b l d -> (b l) d"), NSM)]):
                sp.dma_start(ptok[0:n, c, :], src).then_inc(sem("p_landed"), 16)
            for c in range(FCH):
                with sp.Fori(0, KFC // 2) as it:
                    for b, w in enumerate((w_gate, w_up)):
                        for j in range(4):
                            load_unit(FFN_U[c] + it * 8 + 4 * b + j, j,
                                      rows_of(w, UK * j, UK, bass.ds(it * PW + c * KFC * P, PW)), UK)
                with sp.Fori(0, 4) as it:
                    for b in range(2):
                        for j in range(DU):
                            nk = min(UK, KFC - UK * j)
                            load_unit(DOWN_U[c] + it * 2 * DU + DU * b + j, (DU * b + j) % RING,
                                      rows_of(w_down, c * KFC + UK * j, nk, bass.ds((it * 2 + b) * PW, PW)), nk)
            with sp.Fori(0, 2) as it:
                for b in range(4):
                    for j in range(5):
                        w, k0, nk = (w_ple_gate, UK * j, UK) if j < 4 else (w_ple, 0, 2)
                        load_unit(PLE_U + it * 20 + 5 * b + j, (5 * b + j) % RING,
                                  rows_of(w, k0, nk, bass.ds((it * 4 + b) * PW, PW)), nk)

            for t in range(3):
                dst, n = [(y_prompt[0, 0:P], P), (y_prompt[0, P:2 * P], P),
                          (y_sample.rearrange("b l d -> (b l) d"), NSM)][t]
                for f in (2 * t, 2 * t + 1):
                    wait_drained(sp, ("fin", f))
                sp.dma_start(dst, yo[0:n, t % 2, :]).then_inc(sem(f"y_stored_{t % 2}"), 16)
            sp.wait_ge(sem("y_stored_0"), 32)
            sp.wait_ge(sem("y_stored_1"), 16)
            sp.wait_ge(sem("tail_stored"), 32)
            sp.wait_ge(sem("hl_stored"), 16 * 4)
            sp.wait_ge(sem("s_stored"), 16)
            sp.wait_ge(sem("st_stored_0"), 16 * 4)
            sp.wait_ge(sem("st_stored_1"), 16 * 4)

        @block.gpsimd
        def _(pool):
            o = Steps(pool, sem("pool_steps"))

            def tensor(out, a, b, op, link=True):
                ins = pool.tensor_tensor(out, a, b, op)
                o.link(ins) if link else o.step(ins)

            def select(t, pattern, op, base, cm, fill=0.0):
                o.link(pool.affine_select(t, t, pattern=pattern, compare_op=op, fill=fill, base=base,
                                          channel_multiplier=cm))

            def const():
                for at, w in ((G_MIX, g_mix), (G_FFN, g_ffn), (G_PLE, g_ple), (G_FINAL, g_final)):
                    src = w if w is g_final else w[0]
                    pool.dma_start(par1n[at:at + KD, :], src.rearrange("(k p) -> k p", p=P)).then_inc(sem("par_landed"), 16)
                for at, w in ((D5, s5_d), (BGLU, b_glu)):
                    pool.dma_start(par1n[at:at + K5, :], w[0].rearrange("(k p) -> k p", p=P)).then_inc(sem("par_landed"), 16)
                pool.dma_start(par1n[ONW:ONW + 1, :], onorm_w).then_inc(sem("par_landed"), 16)
                pool.dma_start(par2n[:], conv_w[0].rearrange("j (k p) -> (j k) p", p=P)).then_inc(sem("par_landed"), 16)
                o.step(pool.memset(ones[:], 1.0))
                o.link(pool.memset(ident[:], 0.0))
                pool.affine_select(ident[:], ident[:], pattern=[[-1, P]], compare_op=ALU.not_equal, fill=1.0, base=0,
                                   channel_multiplier=1).then_inc(sem("ident_ready"), 1)
                o.step(pool.memset(acc[:], 0.0))
                for k, w in enumerate((s5_a_re, s5_a_im)):
                    pool.dma_start(spar[:, k, :], w[0].rearrange("(t g) n -> t (g n)", g=2)).then_inc(sem("spar_landed"), 16)
                pool.dma_start(spar[:, 2, 0:2], s5_log_dt[0].rearrange("(t g) -> t g", g=2)).then_inc(sem("spar_landed"), 16)
                pool.dma_start(gab[:, 0:H], a_log.broadcast_to([P, H])).then_inc(sem("gab_landed"), 16)
                pool.dma_start(gab[:, H:2 * H], dt_bias.broadcast_to([P, H])).then_inc(sem("gab_landed"), 16)
                pool.dma_start(wba[:], w_in[0, :, OFF_Z:OFF_A].rearrange("(k p) c -> p k c", p=P)).then_inc(sem("wba_landed"), 16)
                pool.dma_start(csn[:], state_conv[0].rearrange("b j c -> (b j) c")).then_inc(sem("csn_landed"), 16)
                for t, n in ((cum, P), (cums, NSM)):
                    o.link(pool.memset(t[:], 1.0))
                    select(t[:], [[1, n]], ALU.is_ge, 0, -1)
                for t, n in ((strict, P), (stricts, NSM)):
                    o.link(pool.memset(t[:], 1.0))
                    select(t[:], [[1, n]], ALU.is_gt, 0, -1)
                for t in (cums, stricts):
                    v = t[:].rearrange("p (b l) -> p b l", l=NL)
                    select(v, [[-NL, NB], [0, NL]], ALU.is_ge, 0, 1)
                    select(v, [[NL, NB], [0, NL]], ALU.is_ge, NL - 1, -1)
                o.link(pool.memset(lvl[:], 0.0))
                for k in range(7):
                    s = 1 << k
                    v = lvl[:, k, :].rearrange("p (b h s) -> p b h s", h=2, s=s)[:, :, 1, :]
                    o.link(pool.memset(v, 1.0))
                    select(v, [[-2 * s, P // (2 * s)], [0, s]], ALU.is_ge, 0, 1)
                    select(v, [[2 * s, P // (2 * s)], [0, s]], ALU.is_ge, s - 1, -1)
                o.link(pool.memset(seqm[:], 1.0))
                select(seqm[:], [[-NL, NB]], ALU.is_ge, 0, 1)
                select(seqm[:], [[NL, NB]], ALU.is_ge, NL - 1, -1)
                o.link(pool.memset(half[:], 1.0))
                select(half[:, 0:1], [[0, 1]], ALU.is_ge, 63, -1)
                select(half[:, 1:2], [[0, 1]], ALU.is_ge, -64, 1)
                o.link(pool.memset(start[:], 1.0))
                o.step(pool.memset(start[:, 0:1], 0.0))
                o.step(pool.memset(start[:, NPR:N:NL], 0.0))
                o.step(pool.memset(cst[:, 0:1], EPS))
                o.step(pool.memset(cst[:, 1:2], P * EPS))
                pool.memset(cst[:, 2:3], math.pi / 2).then_inc(sem("masks_ready"), 1)

            def add_squares(n, r=None):
                pool.wait_ge(sem("sq_ready"), n + 1)
                o.settle()
                o.link(pool.tensor_tensor(acc[:], acc[:], sq[:, 0, :], ALU.add))
                pool.tensor_tensor(acc[:], acc[:], sq[:, 1, :], ALU.add).then_inc(sem("acc_added"), 1)
                pool.wait_ge(sem("acc_added"), n + 1)

            def clear_sum(n):
                wait_filled(pool, ("norm", n))
                o.link(pool.memset(acc[:], 0.0))

            def square(r, i, ar, ai, t):
                tensor(t[0], ar, ar, ALU.mult, False)
                tensor(t[1], ai, ai, ALU.mult, False)
                tensor(t[2], ar, ai, ALU.mult)
                tensor(r, t[0], t[1], ALU.subtract, False)
                tensor(i, t[2], t[2], ALU.add)

            def product(r, i, ar, ai, br, bi, t0, t1, last=None):
                tensor(t0, ar, br, ALU.mult, False)
                tensor(t1, ai, bi, ALU.mult)
                tensor(r, t0, t1, ALU.subtract)
                tensor(t0, ar, bi, ALU.mult, False)
                tensor(t1, ai, br, ALU.mult)
                tensor(i, t0, t1, ALU.add)

            def powers(t, sr, si):
                o.step(pool.memset(t[:, 0, :, 0:1], 1.0))
                o.step(pool.memset(t[:, 1, :, 0:1], 0.0))
                o.step(pool.tensor_copy(t[:, 0, :, 1:2], sr.unsqueeze(2)))
                o.link(pool.tensor_copy(t[:, 1, :, 1:2], si.unsqueeze(2)))
                w = sc5w
                cur = (sr, si)
                for k in range(1, 5):
                    nxt = (w[:, 2 * (k % 2), :], w[:, 2 * (k % 2) + 1, :])
                    square(nxt[0], nxt[1], cur[0], cur[1], [w[:, 4 + e, :] for e in range(3)])
                    cur = nxt
                    n = 1 << k
                    if n < 16:
                        def bc(v):
                            return v.unsqueeze(2).broadcast_to([P, NT, n])
                        product(t[:, 0, :, n:2 * n], t[:, 1, :, n:2 * n], t[:, 0, :, 0:n], t[:, 1, :, 0:n],
                                bc(cur[0]), bc(cur[1]), pt5[:, 0, 0, :].rearrange("p (t n) -> p t n", n=8)[:, :, 0:n],
                                pt5[:, 0, 1, :].rearrange("p (t n) -> p t n", n=8)[:, :, 0:n])
                return cur

            def tables():
                wait_drained(pool, ("s5par",))
                cur = powers(tb, sp5[:, 1, :], sp5[:, 2, :])
                powers(ta, *cur)

            def h0_terms():
                wait_drained(pool, ("h0",))
                lr = sp5[:, 3, :].unsqueeze(2).broadcast_to([P, NT, NB])
                li = sp5[:, 4, :].unsqueeze(2).broadcast_to([P, NT, NB])
                hr, hi = h0s[:, 0], h0s[:, 1]
                t0 = pt5[:, 0, 0, :].rearrange("p (t b) -> p t b", b=NB)
                t1 = pt5[:, 0, 1, :].rearrange("p (t b) -> p t b", b=NB)
                product(a0[:, 0], a0[:, 1], lr, li, hr, hi, t0, t1)

            def phases(hq):
                s = hq % 2
                if hq >= 2:
                    pool.wait_ge(sem("states_ready"), hq - 1)
                elif hq == 0:
                    wait_filled(pool, ("ct", 1))
                shape = [P, 2, 16, 16]
                ar = ta[:, 0, 2 * hq:2 * hq + 2, :].unsqueeze(3).broadcast_to(shape)
                ai = ta[:, 1, 2 * hq:2 * hq + 2, :].unsqueeze(3).broadcast_to(shape)
                br = tb[:, 0, 2 * hq:2 * hq + 2, :].unsqueeze(2).broadcast_to(shape)
                bi = tb[:, 1, 2 * hq:2 * hq + 2, :].unsqueeze(2).broadcast_to(shape)

                def v(t):
                    return t.rearrange("p t (a b) -> p t a b", b=16)
                product(v(uu[:, s, 0, :, 0:NPR]), v(uu[:, s, 1, :, 0:NPR]), ar, ai, br, bi, v(pt5[:, 0]), v(pt5[:, 1]))
                src = uu[:, s, :, :, 0:NL].rearrange("p r t l -> p (r t) l").unsqueeze(2).broadcast_to([P, 4, NB, NL])
                dst = uu[:, s, :, :, NPR:N].rearrange("p r t (b l) -> p (r t) b l", l=NL)
                pool.tensor_copy(dst, src).then_inc(sem("phases_ready"), 1)

            def inverse_start(c):
                n = CHUNKS[c][1]
                if c:
                    wait_filled(pool, ("vn", c - 1))
                else:
                    pool.wait_ge(sem("qk_normed"), 2 * H)
                src = ident[0:n, 0:n].unsqueeze(1).broadcast_to([n, H, n])
                o.step(pool.tensor_copy(tm[0:n, :, 0:n], src))
                pool.tensor_copy(tmt[0:n, :, 0:n], src).then_inc(sem("t_started"), 1)

            def strict_lt(c):
                n = CHUNKS[c][1]
                m = (strict if c < 2 else stricts)[0:n, 0:n].unsqueeze(1).broadcast_to([n, H, n])
                wait_drained(pool, ("kk", c))
                pool.tensor_tensor(lt[0:n, :, 0:n], lt[0:n, :, 0:n], m, ALU.mult).then_inc(sem("lt_ready"), 1)

            def block_values(h):
                if h == 0:
                    wait_drained(pool, ("vn", 2))
                    wait_filled(pool, ("o", 2))
                if h >= 2:
                    wait_filled(pool, ("su", h - 2))
                src = vn[0:NSM, h, :].unsqueeze(1).broadcast_to([NSM, NB, P])
                m = seqm[:].unsqueeze(2).broadcast_to([NSM, NB, P])
                pool.tensor_tensor(vnb[:, h % 2], src, m, ALU.mult).then_inc(sem("vnb_ready"), 1)

            def load_state(n):
                if n >= H + 2:
                    pool.wait_ge(sem(f"st_stored_{n % 2}"), 16 * ((n - H) // 2))
                elif n >= 2:
                    wait_filled(pool, ("sq", n - 2))
                else:
                    wait_drained(pool, ("tb", 2, LEVELS[2] - 1))
                src = state_delta[0, :, n % H].rearrange("b d e -> d b e")
                pool.dma_start(st_ring[n % 2][:], src).then_inc(sem(f"st_landed_{n % 2}"), 16)

            def store_state(h):
                wait_drained(pool, ("su", h))
                pool.dma_start(delta_sample[0, :, h].rearrange("b d e -> d b e"),
                               st_ring[h % 2][:]).then_inc(sem(f"st_stored_{h % 2}"), 16)

            for sides, us in slots:
                for key in sides:
                    what, a = key[0], key[1:]
                    if what == "const":
                        const()
                    elif what == "x":
                        add_squares(a[0])
                    elif what == "norm":
                        clear_sum(0)
                        wait_filled(pool, ("x", KD // 2 - 1))
                        for r, (wb_, wc_, h_) in enumerate(((s5_b_re, s5_c_re, state_s5_re), (s5_b_im, s5_c_im, state_s5_im))):
                            pool.dma_start(bnat[:, r], wb_[0].rearrange("(t g) n c -> (g n) t c", g=2)).then_inc(sem("bnat_landed"), 16)
                            src = wc_[0].rearrange("(k g) c n -> (g c) k n", g=8)
                            for h in range(2):
                                pool.dma_start(cnat[:, r, :, h, :], src).then_inc(sem("cnat_landed"), 16)
                            src = h_[0].rearrange("b (t g) n -> (b t) (g n)", g=2).rearrange("(k r) c -> r k c", k=2)
                            pool.dma_start(h0n[:, r], src).then_inc(sem("h0_landed"), 16)
                    elif what == "h0":
                        tables()
                        h0_terms()
                    elif what == "ba":
                        phases(0)
                    elif what == "s5" and a[0] + 1 < NT // 2:
                        phases(a[0] + 1)
                    elif what == "tail":
                        for j in range(3):
                            wait_drained(pool, ("tail", j))
                        pool.dma_start(conv_prompt[0, 0], ttok[0:3, :]).then_inc(sem("tail_stored"), 16)
                        pool.dma_start(conv_sample[0].rearrange("b j c -> (b j) c"), ttok[3:27, :]).then_inc(sem("tail_stored"), 16)
                    elif what == "s5out":
                        wait_drained(pool, ("hl",))
                        for r, (op_, os_) in enumerate(((s5_re_prompt, s5_re_sample), (s5_im_prompt, s5_im_sample))):
                            pool.dma_start(op_[0, 0].rearrange("(t g) n -> t (g n)", g=2), hlo[0:NT, r, 0, :]).then_inc(sem("hl_stored"), 16)
                            pool.dma_start(os_[0].rearrange("b (t g) n -> (b t) (g n)", g=2).rearrange("(k r) c -> r k c", k=2),
                                           hlo[:, r, 1:3, :]).then_inc(sem("hl_stored"), 16)
                    elif what == "dkk":
                        inverse_start(*a)
                        strict_lt(*a)
                    elif what == "s" and a[0] == 1:
                        wait_drained(pool, key)
                        pool.dma_start(delta_prompt[0, 0].rearrange("h d e -> d h e"), s_[:]).then_inc(sem("s_stored"), 16)
                    elif what == "sq":
                        for n in range(H + 1):
                            load_state(n)
                    elif what == "su":
                        h = a[0]
                        block_values(h)
                        if h:
                            store_state(h - 1)
                        if h + 1 < H:
                            load_state(H + h + 1)
                        else:
                            store_state(h)
                    elif what == "ysplit":
                        for s in range(2):
                            pool.wait_ge(sem(f"stage_stored_{s}"), 16 * 10)
                        for n, (kind, i) in enumerate(uses):
                            if n >= 2:
                                k_, i_ = uses[n - 2]
                                if k_ == "on":
                                    pool.wait_ge(sem("on_ready"), i_ + 1)
                                else:
                                    pool.wait_ge(evacuated, pair_of[k_, i_] + 1)
                            src = {"wa": 4 + i, "on": i, "wb": 12 + i}[kind]
                            pool.dma_start(gr[:, n % 2], scr_g[:, 2 * src:2 * src + 2, :]).then_inc(sem(f"gate_landed_{n % 2}"), 16)

            def add_loop(first, last):
                n0 = o.n
                with pool.Fori(0, last - first) as it:
                    pool.wait_ge(sem("sq_ready"), it + (first + 1))
                    pool.wait_ge(sem("pool_steps"), it + n0)
                    pool.tensor_tensor(acc[:], acc[:], sq[:, 0, :], ALU.add).then_inc(sem("pool_steps"), 1)
                    pool.wait_ge(sem("pool_steps"), it + (n0 + 1))
                    pool.tensor_tensor(acc[:], acc[:], sq[:, 1, :], ALU.add).then_inc(sem("acc_added"), 1)
                    pool.wait_ge(sem("acc_added"), it + (first + 1))
                o.n = n0 + last - first

            add_loop(8, 16)
            clear_sum(1)
            for c in range(FCH):
                with pool.Fori(0, KFC // 2) as it:
                    pool.wait_ge(sem("silu_ready"), it + (c * (KFC // 2) + 1))
                    pool.tensor_tensor(fsi[:], fsg[:], inv[:].unsqueeze(1).broadcast_to([P, 2, N]),
                                       ALU.mult).then_inc(sem("fsi_ready"), 1)
            add_loop(16, 24)
            clear_sum(2)
            add_loop(24, 32)

        @block.scalar
        def _(act):
            o = Steps(act, sem("scalar_steps"))

            def split_hi(u, r, nk, lap0=False):
                act.wait_ge(raw_landed[r], 16 * (u // RING + 1) if isinstance(u, int) else u * 4 + (16 - 4 * r))
                if not lap0:
                    act.wait_ge(multiplied, u - RING + 1)
                act.activation(whi[:, r, 0:nk, :], raw[:, r, 0:nk, :], ACT.Copy).then_inc(w_hi, 1)

            def copy(out, in_, scale=1.0):
                return act.activation(out, in_, ACT.Copy, scale=scale)

            def finish(x, n, j, gcol):
                if not (isinstance(n, int) and n == 0):
                    act.wait_ge(sem("acc_added"), n)
                act.activation(sq[:], x[:, bass.ds(j * 2, 2), :], ACT.Square).then_inc(sem("sq_ready"), 1)
                if gcol is None:
                    return
                for m in range(2):
                    act.activation(xhi[:, bass.ds(j * 2 + m, 1), :], x[:, bass.ds(j * 2 + m, 1), :], ACT.Copy,
                                   scale=par1[:, bass.ds(j * 2 + (m + gcol), 1)]).then_inc(sem("xhi_ready"), 1)

            def root(n):
                wait_drained(act, ("norm", n))
                if n < 3:
                    act.activation(inv[:], inv[:], ACT.Sqrt).then_inc(sem("root_ready"), 1)
                if n in (0, 3):
                    act.activation(invt[:, 0:2], invt[:, 0:2], ACT.Sqrt).then_inc(sem("root_ready"), 1)
                    act.activation(invt[0:NSM, 2:3], invt[0:NSM, 2:3], ACT.Sqrt).then_inc(sem("root_ready"), 1)

            gates = 0

            def evac(p):
                nonlocal gates
                kind, i, _ = pairs[p]
                if kind in ("z", "gate"):
                    n = gates
                    gates += 1
                    act.wait_ge(evacuated, p + 1)
                    if n >= 2:
                        act.wait_ge(sem(f"stage_stored_{n % 2}"), 16 * (n // 2))
                    act.activation(stg[:, n % 2], g1[:], ACT.Silu if kind == "z" else ACT.Sigmoid).then_inc(sem("stage_written"), 1)
                elif kind == "glu":
                    act.wait_ge(evacuated, p + 1)
                    act.activation(g1[:], g1[:], ACT.Sigmoid).then_inc(sem("glu_sig"), 1)

            def silu_tile(n, t, a):
                act.wait_ge(sem("conv_ready"), n + 1)
                act.activation(qkv[:, t, 0:NCV], a, ACT.Silu).then_inc(sem("silu_done"), 1)

            def side(key):
                what, a = key[0], key[1:]
                if what == "par":
                    wait_filled(act, key)
                    o.step(copy(par1[:], ps(key)[:, 0, 0:81]))
                    drain(copy(par2[:], ps(key)[:, 1, 0:CW * KC]), key)
                    wait_filled(act, ("cst",))
                    drain(copy(cstt[:].rearrange("p (k t) c -> p k (t c)", k=2), ps(("cst",))[:, :, 0:12 * 3 * NB]), ("cst",))
                    wait_drained(act, ("par",))
                elif what == "x":
                    j = a[0]
                    wait_filled(act, key)
                    drain(copy(xt0[:, 2 * j:2 * j + 2, :], ps(key)[:, :, 0:N]), key)
                    wait_drained(act, key)
                    finish(xt0, j, j, G_MIX)
                    if j == KD // 2 - 1:
                        act.dma_start(scr_x, xt0[:]).then_inc(sem("x_stored"), 16)
                elif what == "s5prep":
                    act.wait_ge(sem("spar_landed"), 48)
                    act.wait_ge(sem("masks_ready"), 1)
                    act.activation(sc5[:, 0, 0:2], spar[:, 2, 0:2], ACT.Exp).then_inc(sem("s5_scalar"), 1)
                    act.wait_ge(sem("s5_vector"), 1)
                    act.activation(sc5[:, 3, :], sc5[:, 1, :], ACT.Exp).then_inc(sem("s5_scalar"), 1)
                    act.wait_ge(sem("s5_vector"), 2)
                    act.activation(sc5[:, 7, :], sc5[:, 5, :], ACT.Sin).then_inc(sem("s5_scalar"), 1)
                    act.activation(sc5[:, 8, :], sc5[:, 6, :], ACT.Sin, scale=-1.0, bias=cst[0:NT, 2:3]).then_inc(sem("s5_scalar"), 1)
                elif what == "norm":
                    root(a[0])
                elif what == "s5par":
                    wait_filled(act, key)
                    drain(copy(sp5[:].rearrange("p a t -> p (a t)"), ps(key)[:, 0, 0:7 * NT]), key)
                elif what == "h0":
                    wait_filled(act, key)
                    drain(copy(h0s[:].rearrange("p r t b -> p r b t"), ps(key)[:, :, 0:NT * NB].rearrange("p r (b t) -> p r b t", b=NB)), key)
                elif what == "bb":
                    for r in range(2):
                        wait_filled(act, ("bbt", r))
                        drain(copy(bbt[:, r].rearrange("p (k t) c -> p k (t c)", k=2), ps(("bbt", r))[:]), ("bbt", r))
                elif what == "ba":
                    act.wait_ge(sem("gab_landed"), 32)
                    o.step(act.activation(gab[:, 0:H], gab[:, 0:H], ACT.Exp))
                    act.wait_ge(sem("ba_vector"), 1)
                    act.activation(sp3[:], sp3[:], ACT.Exp, scale=-1.0).then_inc(sem("ba_scalar"), 1)
                    act.wait_ge(sem("ba_scalar"), 1)
                    act.activation(sp3[:], sp3[:], ACT.Ln, bias=ones[:, 0:1]).then_inc(sem("ba_scalar"), 1)
                    act.activation(bet[:], ba[:, :, 0:H], ACT.Sigmoid).then_inc(sem("ba_scalar"), 1)
                elif what == "s5":
                    hq = a[0]
                    if hq == 0:
                        act.wait_ge(sem("phases_ready"), 1)
                        act.wait_ge(sem("pads_done"), 1)
                    else:
                        act.wait_ge(sem("states_ready"), hq)
                        last_states(hq - 1)
                    for t in range(2):
                        k = 2 * hq + t
                        copy(mm[:, t, :], start[:], scale=sp5[:, 0, k:k + 1]).then_inc(sem("decay_ready"), 1)
                    for t in range(2):
                        wait_filled(act, ("bu", hq, t))
                        drain(copy(bu[:, :, t, :], ps(("bu", hq, t))[:, :, 0:N]), ("bu", hq, t))
                    if hq % 2 and hq >= 3:
                        gelu((hq - 3) // 2)
                elif what == "s5y":
                    act.wait_ge(sem("states_ready"), NT // 2)
                    last_states(NT // 2 - 1)
                    gelu(K5 - 1)
                elif what == "s5out":
                    wait_filled(act, ("hl",))
                    o.step(act.activation(hlo[0:NT, :, 0, :], ps(("hl",))[0:NT, :, 0:P], ACT.Copy))
                    drain(copy(hlo[:, :, 1:3, :], ps(("hl",))[:, :, P:3 * P].rearrange("p r (k c) -> p r k c", k=2)), ("hl",))
                elif what == "tail":
                    for j in range(3):
                        wait_filled(act, ("tail", j))
                        drain(copy(ttok[:, j * 1024:(j + 1) * 1024].rearrange("p (k c) -> p k c", k=2),
                                   ps(("tail", j))[0:27, :, :]), ("tail", j))
                elif what == "conv":
                    h = a[0]
                    for g in range(3):
                        silu_tile(3 * h + g, h + H * g, cacc[:, h % 2, g, 0:NCV])
                elif what == "l2a":
                    j = a[0]
                    act.wait_ge(sem("silu_done"), 3 * H)
                    if j == 0:
                        src = qkv[:, 2 * H:3 * H, SEQP:NPAD].rearrange("p h (b l) -> p h b l", l=SEQS)[:, :, :, 0:NL]
                        copy(vsm[:].rearrange("p h (b l) -> p h b l", l=NL), src).then_inc(sem("vsm_ready"), 1)
                    if j:
                        wait_filled(act, ("l2", j - 1))
                    act.activation(sql[:, :, 0:NCV], qkv[:, 2 * j:2 * j + 2, 0:NCV], ACT.Square).then_inc(sem("l2sq_ready"), 1)
                elif what == "l2":
                    j = a[0]
                    wait_filled(act, key)
                    if j:
                        act.wait_ge(sem("qk_normed"), 2 * j)
                    q = j < H // 2
                    drain(act.activation(rl[:, :, 0:NCV], ps(key)[:, :, 0:NCV], ACT.Sqrt, scale=float(P) if q else 1.0,
                                         bias=cst[:, 1:2] if q else cst[:, 0:1]), key)
                elif what == "dg":
                    c = a[0]
                    n = CHUNKS[c][1]
                    act.wait_ge(sem("gdiff_ready"), H * (c + 1))
                    if c:
                        wait_filled(act, ("o", c - 1))
                    drain(act.activation(hsplit(eg[:, :, 0:n]), hview(("grow", c), c), ACT.Exp), ("grow", c))
                    act.activation(dt_[0:n, :, 0:n], dt_[0:n, :, 0:n], ACT.Exp).then_inc(sem("decay_exp"), 1)
                    act.activation(egc[0:n, :], gc[0:n, c, :], ACT.Exp).then_inc(sem("decay_exp"), 1)
                elif what == "dkv":
                    c = a[0]
                    n = CHUNKS[c][1]
                    wait_filled(act, ("kt", c))
                    drain(act.activation(hsplit(ktok[0:n]), ps(("kt", c))[0:n].rearrange("p k (h c) -> p k h c", h=4), ACT.Copy), ("kt", c))
                    wait_filled(act, ("vt", c))
                    for h in range(H):
                        ins = copy(vb[0:n, h, :], ps(("vt", c))[0:n, h // 4, (h % 4) * P:(h % 4 + 1) * P], scale=bet[0:n, c, h:h + 1])
                        o.step(ins) if h < H - 1 else drain(ins, ("vt", c))
                elif what == "m1":
                    c, k = a
                    n = CHUNKS[c][1]
                    wait_filled(act, key)
                    drain(act.activation(hsplit(m1[0:n, :, 0:n]), hview(key, c, rows=n), ACT.Copy), key)
                elif what == "vn":
                    n = CHUNKS[a[0]][1]
                    wait_filled(act, key)
                    drain(act.activation(hsplit(vn[0:n]), ps(key)[0:n].rearrange("p k (h c) -> p k h c", h=4), ACT.Copy), key)
                elif what == "o" and a[0] < 2:
                    c0, n = CHUNKS[a[0]]
                    wait_filled(act, key)
                    drain(act.activation(hsplit(qt[:, :, c0:c0 + n]), hview(key, a[0]), ACT.Copy), key)
                elif what == "sq":
                    act.wait_ge(sem("s_stored"), 16)
                    for h in range(H):
                        key = ("sq", h)
                        wait_filled(act, key)
                        drain(act.activation(sqt[:, h, :], ps(key)[:, 0, 0:P], ACT.Copy), key)
                elif what == "ysplit":
                    act.wait_ge(multiplied, pair_first[pair_of["gate", 15]] + 4)
                    act.wait_ge(sem("gelu_done"), K5)
                    act.activation(yhi[:], yt[:], ACT.Copy).then_inc(sem("yhi_ready"), 1)
                elif what == "ona":
                    j = a[0]
                    wait_drained(act, ("o", 2))
                    if j:
                        wait_filled(act, ("on", j - 1))
                    act.activation(sq[:], qt[:, 2 * j:2 * j + 2, :], ACT.Square).then_inc(sem("osq_ready"), 1)
                elif what == "on":
                    j = a[0]
                    wait_filled(act, key)
                    if j:
                        act.wait_ge(sem("on_ready"), j)
                    else:
                        act.wait_ge(sem("glu_done"), 4)
                    drain(act.activation(g1[:], ps(key)[:, :, 0:N], ACT.Sqrt, scale=1.0 / P, bias=cst[:, 0:1]), key)

            def last_states(hq):
                s = hq % 2
                o.step(copy(hl[:, :, 0, 2 * hq:2 * hq + 2], gg[:, s, :, :, NPR - 1]))
                copy(hl[:, :, 1:NB + 1, 2 * hq:2 * hq + 2].rearrange("p r b t -> p r t b"),
                     gg[:, s, :, :, NPR + NL - 1:N:NL]).then_inc(sem("last_states"), 1)

            def gelu(c):
                wait_drained(act, ("y", 2 * c + 1))
                act.activation(yt[:, c, :], yt[:, c, :], ACT.Gelu_apprx_tanh).then_inc(sem("gelu_done"), 1)

            prev = None
            for sides, us in slots:
                for n in [units.index(u) for u in us]:
                    p, j = units[n]
                    split_hi(n, n % RING, min(UK, pairs[p][2] - UK * j), n < RING)
                    if j == pair_units[p] - 1:
                        if prev is not None:
                            evac(prev)
                        prev = p
                for key in sides:
                    side(key)

            def finish_out(n, j, gcol):
                act.wait_ge(evacuated, n + (OUT_P - 7))
                finish(xt, n, j, gcol)

            def units_of(u0, js, nk=lambda j: UK):
                for j in js:
                    split_hi(u0 + j, j % RING, nk(j))

            units_of(OUT_U, range(4))
            evac(prev)
            with act.Fori(0, 3) as it:
                for b in range(2):
                    for j in range(4):
                        split_hi(OUT_U + 4 + 4 * b + it * 8 + j, j, UK)
                    finish_out(it * 2 + (8 + b), it * 2 + b, G_FFN)
            units_of(OUT_U + 28, range(4))
            finish_out(14, 6, G_FFN)

            def silu(c, i):
                act.wait_ge(evacuated, i * 2 + (FFN_P[c] + 1))
                act.activation(fsg[:], fg1[:], ACT.Silu).then_inc(sem("silu_ready"), 1)

            def hidden(c, i):
                act.wait_ge(evacuated, i * 2 + (FFN_P[c] + 2))
                act.activation(mhi[:, bass.ds(i * 2, 2), :], fmd[:], ACT.Copy).then_inc(sem("mhi_ready"), 1)

            nk_down = lambda j: min(UK, KFC - UK * (j % DU))
            HF = KFC // 2
            for c in range(FCH):
                units_of(FFN_U[c], range(4))
                if c == 0:
                    finish_out(15, 7, G_FFN)
                units_of(FFN_U[c] + 4, range(4))
                if c == 0:
                    root(1)
                silu(c, 0)
                units_of(FFN_U[c] + 8, range(4))
                hidden(c, 0)
                with act.Fori(0, HF - 2) as it:
                    for j in range(4):
                        split_hi(FFN_U[c] + 12 + it * 8 + j, j, UK)
                    silu(c, it + 1)
                    for j in range(4):
                        split_hi(FFN_U[c] + 16 + it * 8 + j, j, UK)
                    hidden(c, it + 1)
                units_of(FFN_U[c] + 8 * HF - 4, range(4))
                silu(c, HF - 1)
                units_of(DOWN_U[c], range(DU), nk_down)
                hidden(c, HF - 1)
                n0 = 16

                def down_pair(it, b):
                    for j in range(DU):
                        jj = DU + b * DU + j
                        split_hi(DOWN_U[c] + jj + it * 2 * DU, jj % RING, nk_down(j))
                    if c == FCH - 1:
                        act.wait_ge(evacuated, it * 2 + (DOWN_P[c] + 1 + b))
                        finish(xt, it * 2 + (n0 + b), it * 2 + b, G_PLE)

                with act.Fori(0, 3) as it:
                    for b in range(2):
                        down_pair(it, b)
                for j in range(DU):
                    jj = 7 * DU + j
                    split_hi(DOWN_U[c] + jj, jj % RING, nk_down(j))
                if c == FCH - 1:
                    act.wait_ge(evacuated, DOWN_P[c] + 7)
                    finish(xt, 22, 6, G_PLE)

            def gate_sig(i):
                act.wait_ge(evacuated, PLE_P + 2 * i + 1)
                act.activation(fsg[:], fg1[:], ACT.Sigmoid).then_inc(sem("psig_ready"), 1)

            def final_x(i):
                act.wait_ge(sem("xf_ready"), i + 1)
                finish(xt, i + 24, i, None)
                for m in range(2):
                    act.activation(xg[:, bass.ds(i * 2 + m, 1), :], xt[:, bass.ds(i * 2 + m, 1), :], ACT.Copy,
                                   scale=par1[:, bass.ds(i * 2 + (m + G_FINAL), 1)]).then_inc(sem("xg_ready"), 1)

            wait_drained(act, ("pt",))
            act.activation(phi[:], pf[:], ACT.Copy).then_inc(sem("phi_ready"), 1)
            for i in range(8):
                u = PLE_U + 5 * i
                for j in range(3):
                    split_hi(u + j, (5 * i + j) % RING, UK)
                if i:
                    gate_sig(i - 1)
                split_hi(u + 3, (5 * i + 3) % RING, UK)
                if i:
                    final_x(i - 1)
                else:
                    act.wait_ge(evacuated, PLE_P)
                    finish(xt, 23, 7, G_PLE)
                split_hi(u + 4, (5 * i + 4) % RING, 2)
                if i == 0:
                    root(2)
            gate_sig(7)
            final_x(7)
            root(3)
            act.wait_ge(sem("invt_ready"), 2)
            for t in range(3):
                n = CHUNKS[t][1]
                key = ("fin", 2 * t)
                wait_filled(act, key)
                if t == 2:
                    act.wait_ge(sem("y_stored_0"), 16)
                drain(act.activation(yo[0:n, t % 2, 0:D // 2].rearrange("p (k c) -> p k c", k=2), ps(key)[0:n], ACT.Copy,
                                     scale=invt[0:n, t:t + 1]), key)

        @block.vector
        def _(dve):
            o = Steps(dve, sem("vector_steps"))

            def both(t):
                return t[:].unsqueeze(1).broadcast_to([P, 2, N])

            def split_lo(u, r, nk):
                dve.wait_ge(w_hi, u + 1)
                dve.tensor_tensor(wlo[:, r, 0:nk, :], raw[:, r, 0:nk, :], whi[:, r, 0:nk, :].bitcast(F32),
                                  ALU.subtract).then_inc(w_lo, 1)

            def lows(x, n, j, gcol):
                for m in range(2):
                    dve.wait_ge(sem("xhi_ready"), n * 2 + (m + 1))
                    dve.scalar_tensor_tensor(out=xlo[:, bass.ds(j * 2 + m, 1), :], in0=x[:, bass.ds(j * 2 + m, 1), :],
                                             scalar=par1[:, bass.ds(j * 2 + (m + gcol), 1)],
                                             in1=xhi[:, bass.ds(j * 2 + m, 1), :].bitcast(F32),
                                             op0=ALU.mult, op1=ALU.subtract).then_inc(sem("xlo_ready"), 1)

            def norm(n):
                key = ("norm", n)
                wait_filled(dve, key)
                o.settle()
                both_forms = n in (0, 3)
                if n < 3:
                    ins = dve.tensor_scalar(inv[:], ps(key)[:, 0, 0:N], 1.0 / D, EPS, ALU.mult, ALU.add)
                    o.step(ins) if both_forms else drain(ins, key)
                if both_forms:
                    o.step(dve.tensor_scalar(invt[:, 0:2], ps(key)[:, 1, 0:2], 1.0 / D, EPS, ALU.mult, ALU.add))
                    drain(dve.tensor_scalar(invt[0:NSM, 2:3], ps(key)[0:NSM, 1, 2:3], 1.0 / D, EPS, ALU.mult, ALU.add), key)
                dve.wait_ge(sem("root_ready"), {0: 3, 1: 4, 2: 5, 3: 7}[n])
                if both_forms:
                    o.step(dve.reciprocal(invt[:, 0:2], invt[:, 0:2]))
                    dve.reciprocal(invt[0:NSM, 2:3], invt[0:NSM, 2:3]).then_inc(sem("invt_ready"), 1)
                    dve.wait_ge(sem("invt_ready"), 1 + (n == 3))
                if n < 3:
                    dve.reciprocal(inv[:], inv[:]).then_inc(sem("inv_ready"), 1)
                    dve.wait_ge(sem("inv_ready"), n + 1)

            gates = 0

            def stored_gate(kind, i):
                n = uses.index((kind, i))
                dve.wait_ge(sem(f"gate_landed_{n % 2}"), 16 * (n // 2 + 1))
                return gr[:, n % 2]

            def evac(p):
                nonlocal gates
                kind, i, _ = pairs[p]
                dve.wait_ge(multiplied, pair_first[p] + pair_units[p])
                src = pg[:, p % 2, :, 0:N]
                if kind == "u":
                    dve.tensor_tensor(yt[:, 2 * i:2 * i + 2, :], src, both(inv), ALU.mult).then_inc(evacuated, 1)
                elif kind == "qkv":
                    if i == 0:
                        dve.wait_ge(sem("x_stored"), 16)
                    t = slice(2 * i, 2 * i + 2)
                    o.step(dve.tensor_tensor(qkv[:, t, CW - 1:SEQP], pg[:, p % 2, :, 0:NPR],
                                             inv[:, 0:NPR].unsqueeze(1).broadcast_to([P, 2, NPR]), ALU.mult))
                    dst = qkv[:, t, SEQP:NPAD].rearrange("p t (b l) -> p t b l", l=SEQS)[:, :, :, CW - 1:SEQS]
                    dve.tensor_tensor(dst, pg[:, p % 2, :, NPR:N].rearrange("p t (b l) -> p t b l", l=NL),
                                      inv[:, NPR:N].rearrange("p (b l) -> p b l", l=NL).unsqueeze(1).broadcast_to([P, 2, NB, NL]),
                                      ALU.mult).then_inc(evacuated, 1)
                elif kind in ("z", "gate"):
                    if gates:
                        dve.wait_ge(sem("stage_written"), gates)
                    gates += 1
                    dve.tensor_tensor(g1[:], src, both(inv), ALU.mult).then_inc(evacuated, 1)
                elif kind == "glu":
                    dve.wait_ge(sem("stage_written"), 20)
                    o.settle()
                    for m in range(2):
                        k = BGLU + 2 * i + m
                        ins = dve.tensor_scalar(g1[:, m, :], src[:, m, :], par1[:, k:k + 1], None, ALU.add)
                        o.step(ins) if m == 0 else ins.then_inc(evacuated, 1)
                elif kind == "wa":
                    dve.tensor_tensor(mixa[:, 2 * i:2 * i + 2, :], src, stored_gate("wa", i), ALU.mult).then_inc(evacuated, 1)
                elif kind == "wb":
                    o.settle()
                    dve.tensor_tensor(t1[:], src, stored_gate("wb", i), ALU.mult).then_inc(evacuated, 1)
                    dve.wait_ge(evacuated, p + 1)
                    t = slice(2 * i, 2 * i + 2)
                    o.link(dve.tensor_tensor(t1[:], t1[:], mixa[:, t, :], ALU.add))
                    o.link(dve.tensor_copy(mxhi[:, t, :], t1[:]))
                    dve.tensor_tensor(mxlo[:, t, :], t1[:], mxhi[:, t, :].bitcast(F32), ALU.subtract).then_inc(sem("mix_ready"), 1)
                    dve.wait_ge(sem("mix_ready"), i + 1)

            def late(p):
                kind, i, _ = pairs[p]
                if kind == "glu":
                    t = slice(2 * i, 2 * i + 2)
                    dve.wait_ge(sem("glu_sig"), i + 1)
                    o.settle()
                    o.link(dve.tensor_tensor(t1[:], yt[:, t, :], g1[:], ALU.mult))
                    o.link(dve.tensor_copy(ghi[:, t, :], t1[:]))
                    dve.tensor_tensor(glo[:, t, :], t1[:], ghi[:, t, :].bitcast(F32), ALU.subtract).then_inc(sem("glu_done"), 1)
                    dve.wait_ge(sem("glu_done"), i + 1)

            def s5_scalars():
                dve.wait_ge(sem("s5_scalar"), 1)
                ar, ai = spar[:, 0, :], spar[:, 1, :]
                row = [sc5[:, k, :] for k in range(16)]
                dtb = sc5[:, 0, 0:2].unsqueeze(2).broadcast_to([NT, 2, ST])

                def g(v):
                    return v.rearrange("t (g n) -> t g n", g=2)
                o.step(dve.tensor_tensor(g(row[2]), g(ai), dtb, ALU.mult))
                dve.tensor_tensor(g(row[1]), g(ar), dtb, ALU.mult).then_inc(sem("s5_vector"), 1)
                dve.wait_ge(sem("s5_vector"), 1)
                o.link(dve.tensor_scalar(row[4], row[2], 1.0 / (2 * math.pi), MAGIC, ALU.mult, ALU.add))
                o.link(dve.tensor_scalar(row[4], row[4], MAGIC, None, ALU.subtract))
                cur = row[2]
                for k, part in enumerate(TWO_PI_PARTS):
                    dst = row[12 + k % 2]
                    o.link(dve.scalar_tensor_tensor(out=dst, in0=row[4], scalar=-part, in1=cur, op0=ALU.mult, op1=ALU.add))
                    cur = dst
                o.link(dve.tensor_scalar(row[5], cur, 3.1415925, -3.1415925, ALU.min, ALU.max))
                dve.scalar_tensor_tensor(out=row[6], in0=row[5], scalar=-1.0, in1=row[5], op0=ALU.mult, op1=ALU.max).then_inc(sem("s5_vector"), 1)
                dve.wait_ge(sem("s5_scalar"), 4)
                o.step(dve.tensor_tensor(row[9], row[3], row[8], ALU.mult))
                o.step(dve.tensor_tensor(row[10], row[3], row[7], ALU.mult))
                o.step(dve.tensor_tensor(row[13], ar, ar, ALU.mult))
                o.link(dve.tensor_tensor(row[14], ai, ai, ALU.mult))
                o.step(dve.tensor_tensor(row[13], row[13], row[14], ALU.add))
                o.link(dve.tensor_scalar(row[15], row[9], -1.0, None, ALU.add))
                o.step(dve.reciprocal(row[13], row[13]))
                o.step(dve.tensor_tensor(row[1], row[15], ar, ALU.mult))
                o.step(dve.tensor_tensor(row[2], row[10], ai, ALU.mult))
                o.step(dve.tensor_tensor(row[4], row[10], ar, ALU.mult))
                o.link(dve.tensor_tensor(row[14], row[15], ai, ALU.mult))
                o.step(dve.tensor_tensor(row[1], row[1], row[2], ALU.add))
                o.link(dve.tensor_tensor(row[4], row[4], row[14], ALU.subtract))
                o.step(dve.tensor_tensor(row[11], row[1], row[13], ALU.mult))
                dve.tensor_tensor(row[12], row[4], row[13], ALU.mult).then_inc(sem("s5_vector"), 1)

            def b_discrete():
                dve.wait_ge(sem("bnat_landed"), 32)
                wait_drained(dve, ("s5par",))
                cr = sp5[:, 5, :].unsqueeze(2).broadcast_to([P, NT, 16])
                ci = sp5[:, 6, :].unsqueeze(2).broadcast_to([P, NT, 16])
                br, bi = bnat[:, 0], bnat[:, 1]
                t3 = bmix[:, 0].rearrange("p t h c -> p (t h c)")[:, 0:NT * 16].rearrange("p (t c) -> p t c", c=16)
                o.step(dve.tensor_tensor(bt1[:], br, cr, ALU.mult))
                o.step(dve.tensor_tensor(bt2[:], bi, ci, ALU.mult))
                o.link(dve.tensor_tensor(t3, br, ci, ALU.mult))
                o.link(dve.tensor_tensor(bt1[:], bt1[:], bt2[:], ALU.subtract))
                o.link(dve.tensor_tensor(bt2[:], bi, cr, ALU.mult))
                o.link(dve.tensor_tensor(bt2[:], bt2[:], t3, ALU.add))
                for r, b in enumerate((bt1, bt2)):
                    for h in range(2):
                        ins = dve.tensor_scalar(bmix[:, r, :, h, :], b[:], half[:, h:h + 1], None, ALU.mult)
                        o.step(ins) if (r, h) != (1, 1) else ins.then_inc(sem("bmix_ready"), 1)

            def s5_tiles(hq):
                s = hq % 2
                ur, ui = uu[:, s, 0], uu[:, s, 1]
                u, g_, b_ = uu[:, s], gg[:, s], bu[:]
                dve.wait_ge(sem("phases_ready"), hq + 1)
                for t in range(2):
                    wait_drained(dve, ("bu", hq, t))
                o.settle()
                o.link(dve.tensor_tensor(bu[:, :, :, NPR:N:NL], bu[:, :, :, NPR:N:NL], a0[:, :, 2 * hq:2 * hq + 2, :], ALU.add))
                o.link(dve.tensor_tensor(tt[:], u, b_, ALU.mult))
                if hq >= 2:
                    wait_filled(dve, ("y", hq - 2))
                    dve.wait_ge(sem("last_states"), hq - 1)
                o.link(dve.tensor_tensor(g_[:, 0], tt[:, 0], tt[:, 1], ALU.add))
                o.step(dve.tensor_tensor(tt[:, 0], ur, b_[:, 1], ALU.mult))
                o.link(dve.tensor_tensor(tt[:, 1], ui, b_[:, 0], ALU.mult))
                o.link(dve.tensor_tensor(g_[:, 1], tt[:, 0], tt[:, 1], ALU.subtract))
                dve.wait_ge(sem("decay_ready"), 2 * hq + 2)
                for r in range(2):
                    o.step(dve.tensor_tensor_scan(b_[:, r].rearrange("p t n -> p (t n)"), mm[:].rearrange("p t n -> p (t n)"),
                                                  g_[:, r].rearrange("p t n -> p (t n)"), 0.0, ALU.mult, ALU.add))
                o.settle()
                o.link(dve.tensor_tensor(tt[:], u, b_, ALU.mult))
                o.link(dve.tensor_tensor(g_[:, 0], tt[:, 0], tt[:, 1], ALU.subtract))
                o.step(dve.tensor_tensor(tt[:, 0], ur, b_[:, 1], ALU.mult))
                o.link(dve.tensor_tensor(tt[:, 1], ui, b_[:, 0], ALU.mult))
                dve.tensor_tensor(g_[:, 1], tt[:, 0], tt[:, 1], ALU.add).then_inc(sem("states_ready"), 1)
                dve.wait_ge(sem("states_ready"), hq + 1)

            def y_half(hq):
                c, r = hq // 2, slice(64 * (hq % 2), 64 * (hq % 2) + 64)
                wait_filled(dve, ("y", hq))
                ins = dve.scalar_tensor_tensor(out=yt[r, c, :], in0=yt[r, c, :], scalar=par1[r, D5 + c:D5 + c + 1],
                                               in1=ps(("y", hq))[r, 0, 0:N], op0=ALU.mult, op1=ALU.add)
                drain(ins, ("y", hq))

            def level_mask(c, k):
                n = CHUNKS[c][1]
                m = lvl[0:n, k, 0:n].unsqueeze(1).broadcast_to([n, H, n])
                dve.tensor_tensor(ltm[0:n, :, 0:n], lt[0:n, :, 0:n], m, ALU.mult).then_inc(sem("ltm_ready"), 1)

            def side(key):
                what, a = key[0], key[1:]
                if what == "x":
                    lows(xt0, a[0], a[0], G_MIX)
                elif what == "norm":
                    norm(0)
                elif what == "s5prep":
                    s5_scalars()
                elif what == "bmix":
                    b_discrete()
                elif what == "ct":
                    for r in range(2):
                        key = ("ct", r)
                        wait_filled(dve, key)
                        dst = ct[:, r].rearrange("p k (g h c) -> p (k g) h c", h=2, c=16)
                        src = ps(key)[:].rearrange("p k (g h c) -> p (k g) h c", h=2, c=16)
                        for h in range(2):
                            ins = dve.tensor_scalar(dst[:, :, h, :], src[:, :, h, :], half[:, h:h + 1], -1.0 if r else 1.0,
                                                    ALU.mult, ALU.mult)
                            o.step(ins) if h == 0 else drain(ins, key)
                elif what == "ba":
                    o.link(dve.memset(ba[:], 0.0))
                    wait_filled(dve, key)
                    for c in range(3):
                        n = CHUNKS[c][1]
                        ins = dve.tensor_scalar(ba[0:n, c, :], ps(key)[0:n, 0, 16 * c:16 * c + 16], invt[0:n, c:c + 1], None, ALU.mult)
                        o.step(ins) if c < 2 else drain(ins, key)
                    wait_drained(dve, key)
                    dve.wait_ge(sem("gab_landed"), 32)
                    av = ba[:, :, H:2 * H]
                    o.link(dve.tensor_tensor(av, av, gab[:, H:2 * H].unsqueeze(1).broadcast_to([P, 3, H]), ALU.add))
                    dve.scalar_tensor_tensor(out=sp3[:], in0=av, scalar=-1.0, in1=av, op0=ALU.mult, op1=ALU.max).then_inc(sem("ba_vector"), 1)
                    dve.wait_ge(sem("ba_scalar"), 3)
                    o.link(dve.scalar_tensor_tensor(out=sp3[:], in0=av, scalar=0.0, in1=sp3[:], op0=ALU.max, op1=ALU.add))
                    dve.scalar_tensor_tensor(out=gt[:], in0=sp3[:], scalar=-1.0, in1=gab[:, 0:H].unsqueeze(1).broadcast_to([P, 3, H]),
                                             op0=ALU.mult, op1=ALU.mult).then_inc(sem("g_ready"), 1)
                    dve.wait_ge(sem("x_stored"), 16)
                    wait_filled(dve, ("ba",))
                    wait_drained(dve, ("cst",))
                    o.step(dve.memset(qkv[:, :, 0:CW - 1], 0.0))
                    dst = qkv[:, :, SEQP:NPAD].rearrange("p t (b l) -> p t b l", l=SEQS)[:, :, :, 0:CW - 1]
                    dve.tensor_copy(dst, cstt[:].rearrange("p t (b j) -> p t b j", j=CW - 1)).then_inc(sem("pads_done"), 1)
                    dve.wait_ge(sem("pads_done"), 1)
                elif what == "s5":
                    s5_tiles(a[0])
                    if a[0]:
                        y_half(a[0] - 1)
                elif what == "s5y":
                    y_half(NT // 2 - 1)
                elif what == "tailc":
                    dve.wait_ge(evacuated, pair_of["qkv", 11] + 1)
                    wait_filled(dve, ("y", NT // 2 - 1))
                    dve.wait_ge(sem("last_states"), NT // 2)
                    o.settle()
                    o.step(dve.tensor_copy(tail[:, :, 0:3], qkv[:, :, SEQP - 3:SEQP]))
                    src = qkv[:, :, SEQP:NPAD].rearrange("p t (b l) -> p t b l", l=SEQS)[:, :, :, NL:SEQS]
                    dve.tensor_copy(tail[:, :, 3:27].rearrange("p t (b j) -> p t b j", j=3), src).then_inc(sem("tails_ready"), 1)
                elif what == "conv":
                    h = a[0]
                    if h == 0:
                        dve.wait_ge(sem("tails_ready"), 1)
                    for g in range(3):
                        t, s = h + H * g, cacc[:, h % 2, g, 0:NCV]
                        if h >= 2:
                            dve.wait_ge(sem("silu_done"), 3 * (h - 2) + g + 1)
                        o.link(dve.tensor_scalar(s, qkv[:, t, 0:NCV], par2[:, t:t + 1], None, ALU.mult))
                        for j in range(1, CW):
                            ins = dve.scalar_tensor_tensor(out=s, in0=qkv[:, t, j:j + NCV], scalar=par2[:, j * KC + t:j * KC + t + 1],
                                                           in1=s, op0=ALU.mult, op1=ALU.add)
                            o.link(ins) if j < CW - 1 else ins.then_inc(sem("conv_ready"), 1)
                elif what == "l2":
                    j = a[0]
                    wait_drained(dve, key)
                    if j == 0:
                        dve.wait_ge(sem("tail_stored"), 32)
                        dve.wait_ge(sem("hl_stored"), 64)
                    o.link(dve.reciprocal(rl[:, :, 0:NCV], rl[:, :, 0:NCV]))
                    dst = qt if j < H // 2 else kt
                    t = slice(2 * (j % 4), 2 * (j % 4) + 2)
                    dve.tensor_tensor(dst[:, t, 0:NPR], qkv[:, 2 * j:2 * j + 2, 0:NPR], rl[:, :, 0:NPR], ALU.mult).then_inc(sem("qk_normed"), 1)

                    def v(x):
                        return x.rearrange("p t (b l) -> p t b l", l=SEQS)[:, :, :, 0:NL]
                    q11 = qkv[:, 2 * j:2 * j + 2, SEQP:NPAD]
                    r11 = rl[:, :, SEQP:NPAD]
                    dve.tensor_tensor(dst[:, t, NPR:N].rearrange("p t (b l) -> p t b l", l=NL), v(q11), v(r11),
                                      ALU.mult).then_inc(sem("qk_normed"), 1)
                elif what == "dg":
                    c = a[0]
                    c0, n = CHUNKS[c]
                    wait_filled(dve, ("gcum", c))
                    drain(dve.tensor_copy(gc[0:n, c, :], ps(("gcum", c))[0:n, 0, 0:H]), ("gcum", c))
                    wait_drained(dve, ("gcum", c))
                    wait_filled(dve, ("grow", c))
                    if c:
                        wait_drained(dve, ("qk", c - 1))
                    for h in range(H):
                        dve.tensor_scalar(dt_[0:n, h, 0:n], ps(("grow", c))[0:n, h // 4, (h % 4) * n:(h % 4) * n + n],
                                          gc[0:n, c, h:h + 1], 0.0, ALU.subtract, ALU.min).then_inc(sem("gdiff_ready"), 1)
                    wait_filled(dve, ("brow", c))
                    if c:
                        wait_drained(dve, ("tb", c - 1, LEVELS[c - 1] - 1))
                    drain(dve.tensor_tensor(hsplit(kb[:, :, 0:n]), hsplit(kt[:, :, c0:c0 + n]), hview(("brow", c), c), ALU.mult),
                          ("brow", c))
                    dve.wait_ge(sem("decay_exp"), 2 * (c + 1))
                    m = (cum if c < 2 else cums)[0:n, 0:n].unsqueeze(1).broadcast_to([n, H, n])
                    o.link(dve.tensor_tensor(dt_[0:n, :, 0:n], dt_[0:n, :, 0:n], m, ALU.mult))
                    o.step(dve.scalar_tensor_tensor(out=nbe[0:n, c, :], in0=egc[0:n, :], scalar=-1.0, in1=bet[0:n, c, :],
                                                    op0=ALU.mult, op1=ALU.mult))
                    if c < 2:
                        o.step(dve.tensor_copy(dl[0:n, :], dt_[0:n, :, n - 1]))
                        o.step(dve.tensor_copy(egl[:, :, 0], eg[:, :, n - 1]))
                    else:
                        o.step(dve.tensor_reduce(dl[0:n, :], dt_[0:n, :, NL - 1:n:NL], AX.X, ALU.add))
                        o.step(dve.tensor_copy(egl[:], eg[:, :, NL - 1:n:NL]))
                    o.settle()
                elif what == "dkk":
                    c = a[0]
                    c0, n = CHUNKS[c]
                    wait_filled(dve, ("kk", c))
                    drain(dve.tensor_tensor(hsplit(lt[0:n, :, 0:n]), hview(("kk", c), c, rows=n), hsplit(dt_[0:n, :, 0:n]), ALU.mult), ("kk", c))
                    wait_filled(dve, ("qk", c))
                    if c:
                        wait_drained(dve, ("o", c - 1))
                    drain(dve.tensor_tensor(hsplit(qkd[0:n, :, 0:n]), hview(("qk", c), c, rows=n), hsplit(dt_[0:n, :, 0:n]), ALU.mult), ("qk", c))
                    dve.tensor_tensor(eg[:, :, 0:n], eg[:, :, 0:n], qt[:, :, c0:c0 + n], ALU.mult).then_inc(sem("qg_ready"), 1)
                    wait_drained(dve, ("kt", c))
                    dve.tensor_tensor(ktok[0:n], ktok[0:n], dl[0:n, :].unsqueeze(2).broadcast_to([n, H, P]), ALU.mult).then_inc(sem("kd_ready"), 1)
                    dve.wait_ge(sem("lt_ready"), c + 1)
                    level_mask(c, 0)
                elif what == "tab":
                    c, k = a
                    n = CHUNKS[c][1]
                    for nm, t in (("ta", tm), ("tb", tmt)):
                        kk = (nm, c, k)
                        wait_filled(dve, kk)
                        drain(dve.tensor_tensor(hsplit(t[0:n, :, 0:n]), hsplit(t[0:n, :, 0:n]), hview(kk, c, rows=n), ALU.subtract), kk)
                    if k + 1 < LEVELS[c]:
                        level_mask(c, k + 1)
                elif what == "ks":
                    c = a[0]
                    n = CHUNKS[c][1]
                    wait_filled(dve, key)
                    for h in range(H):
                        ins = dve.scalar_tensor_tensor(out=vb[0:n, h, :], in0=ps(key)[0:n, h // 4, (h % 4) * P:(h % 4 + 1) * P],
                                                       scalar=nbe[0:n, c, h:h + 1], in1=vb[0:n, h, :], op0=ALU.mult, op1=ALU.add)
                        o.step(ins) if h < H - 1 else drain(ins, key)
                elif what == "o" and a[0] == 2:
                    wait_filled(dve, key)
                    v = sqt[:].rearrange("p h (k c) -> p h k c", k=2)[:, :, 1, :]
                    drain(dve.tensor_tensor(hsplit(qt[:, :, NPR:N]), hview(key, 2), hsplit(v), ALU.add), key)
                elif what == "s":
                    c = a[0]
                    wait_filled(dve, key)
                    if c == 0:
                        drain(dve.tensor_copy(hsplit(s_[:]), ps(key)[:].rearrange("p k (h e) -> p k h e", h=4)), key)
                    else:
                        for h in range(H):
                            ins = dve.scalar_tensor_tensor(out=s_[:, h, :], in0=s_[:, h, :], scalar=egl[:, h, 0:1],
                                                           in1=ps(key)[:, h // 4, (h % 4) * P:(h % 4 + 1) * P], op0=ALU.mult, op1=ALU.add)
                            o.step(ins) if h < H - 1 else drain(ins, key)
                elif what == "su":
                    h = a[0]
                    st = st_ring[h % 2]
                    dve.wait_ge(sem(f"st_landed_{h % 2}"), 16 * (4 + h // 2 + 1))
                    o.link(dve.tensor_tensor(st[:], st[:], egl[:, h, :].unsqueeze(2).broadcast_to([P, NB, P]), ALU.mult))
                    wait_filled(dve, key)
                    drain(dve.tensor_tensor(hsplit(st[:]), hsplit(st[:]), ps(key)[:].rearrange("p k (b e) -> p k b e", b=4), ALU.add), key)
                elif what == "ysplit":
                    dve.wait_ge(sem("yhi_ready"), 1)
                    dve.tensor_tensor(ylo[:], yt[:], yhi[:].bitcast(F32), ALU.subtract).then_inc(sem("ylo_ready"), 1)
                elif what == "on":
                    j = a[0]
                    wait_drained(dve, key)
                    o.link(dve.reciprocal(g1[:], g1[:]))
                    for m in range(2):
                        o.step(dve.scalar_tensor_tensor(out=t1[:, m, :], in0=qt[:, 2 * j + m, :], scalar=par1[:, ONW:ONW + 1],
                                                        in1=g1[:, m, :], op0=ALU.mult, op1=ALU.mult))
                    z = stored_gate("on", j)
                    o.settle()
                    o.link(dve.tensor_tensor(t1[:], t1[:], z, ALU.mult))
                    t = slice(2 * j, 2 * j + 2)
                    o.link(dve.tensor_copy(dhi[:, t, :], t1[:]))
                    dve.tensor_tensor(dlo[:, t, :], t1[:], dhi[:, t, :].bitcast(F32), ALU.subtract).then_inc(sem("on_ready"), 1)
                    dve.wait_ge(sem("on_ready"), j + 1)

            prev = None
            for sides, us in slots:
                for n in [units.index(u) for u in us]:
                    p, j = units[n]
                    nk, last = min(UK, pairs[p][2] - UK * j), pair_units[p] - 1
                    if j == last and last >= 3 and prev is not None:
                        evac(prev)
                    split_lo(n, n % RING, nk)
                    if j == 0 and p >= 2:
                        late(p - 2)
                    if j == last:
                        if last < 3 and prev is not None:
                            evac(prev)
                        prev = p
                for key in sides:
                    side(key)

            def add_x(gp, par, j):
                xs = xt[:, bass.ds(j * 2, 2), :]
                dve.tensor_tensor(xs, xs, pg[:, par, :, 0:N], ALU.add).then_inc(evacuated, 1)

            def splits(u0, js, nk=lambda j: UK):
                for j in js:
                    split_lo(u0 + j, j % RING, nk(j))

            splits(OUT_U, range(3))
            evac(prev)
            splits(OUT_U, [3])
            dve.wait_ge(sem("xt_landed"), 16)
            splits(OUT_U + 4, range(3))
            dve.wait_ge(multiplied, OUT_U + 4)
            add_x(OUT_P, 0, 0)
            splits(OUT_U + 4, [3])
            with dve.Fori(0, 3) as it:
                for b in range(2):
                    split_lo(OUT_U + 8 + 4 * b + it * 8, 0, UK)
                    lows(xt, it * 2 + (8 + b), it * 2 + b, G_FFN)
                    split_lo(OUT_U + 9 + 4 * b + it * 8, 1, UK)
                    split_lo(OUT_U + 10 + 4 * b + it * 8, 2, UK)
                    dve.wait_ge(multiplied, OUT_U + 8 + 4 * b + it * 8)
                    add_x(None, 1 - b, it * 2 + (1 + b))
                    split_lo(OUT_U + 11 + 4 * b + it * 8, 3, UK)

            HF = KFC // 2
            both_inv = both(inv)

            def gate_out(k):
                dve.wait_ge(multiplied, k)
                dve.tensor_tensor(fg1[:], pg[:, 0, :, 0:N], both_inv, ALU.mult).then_inc(evacuated, 1)

            def up_out(k, n):
                dve.wait_ge(multiplied, k)
                dve.wait_ge(sem("fsi_ready"), n)
                dve.tensor_tensor(fmd[:], pg[:, 1, :, 0:N], fsi[:], ALU.mult).then_inc(evacuated, 1)

            def hidden_lo(n, i):
                dve.wait_ge(sem("mhi_ready"), n)
                dve.tensor_tensor(mlo[:, bass.ds(i * 2, 2), :], fmd[:], mhi[:, bass.ds(i * 2, 2), :].bitcast(F32),
                                  ALU.subtract).then_inc(sem("mlo_ready"), 1)

            nk_down = lambda j: min(UK, KFC - UK * (j % DU))
            for c in range(FCH):
                U, n0 = FFN_U[c], c * HF
                if c == 0:
                    split_lo(U, 0, UK)
                    lows(xt, 14, 6, G_FFN)
                    splits(U, [1, 2])
                    dve.wait_ge(multiplied, OUT_U + 32)
                    add_x(None, 1, 7)
                    splits(U, [3])
                    split_lo(U + 4, 0, UK)
                    lows(xt, 15, 7, G_FFN)
                    splits(U + 4, [1, 2])
                    norm(1)
                else:
                    splits(U, range(3))
                    dve.wait_ge(multiplied, U)
                    add_x(None, 1, 7)
                    splits(U, [3])
                    splits(U + 4, range(3))
                gate_out(U + 4)
                splits(U + 4, [3])
                with dve.Fori(0, HF - 1) as it:
                    k = it * 8
                    split_lo(k + (U + 8), 0, UK)
                    split_lo(k + (U + 9), 1, UK)
                    split_lo(k + (U + 10), 2, UK)
                    up_out(k + (U + 8), it + (n0 + 1))
                    split_lo(k + (U + 11), 3, UK)
                    split_lo(k + (U + 12), 0, UK)
                    hidden_lo(it + (n0 + 1), it)
                    split_lo(k + (U + 13), 1, UK)
                    split_lo(k + (U + 14), 2, UK)
                    gate_out(k + (U + 12))
                    split_lo(k + (U + 15), 3, UK)
                W = DOWN_U[c]
                splits(W, range(3))
                up_out(W, n0 + HF)
                splits(W, [3])
                hidden_lo(n0 + HF, HF - 1)
                splits(W, range(4, DU), nk_down)
                if c == 0:
                    wait_filled(dve, ("pt",))
                    drain(dve.tensor_copy(pf[:], ps(("pt",))[:, :, 0:N]), ("pt",))
                    wait_drained(dve, ("pt",))

                def down_pair(it, b):
                    for j in range(DU):
                        jj = DU + b * DU + j
                        if c == FCH - 1 and j == 1 and b == 1:
                            lows(xt, it * 2 + 16, it * 2, G_PLE)
                        if j == 3:
                            dve.wait_ge(multiplied, it * (2 * DU) + (W + DU + b * DU))
                            add_x(None, b, it * 2 + b)
                        split_lo(it * (2 * DU) + (W + jj), jj % RING, nk_down(j))

                with dve.Fori(0, 3) as it:
                    down_pair(it, 0)
                    down_pair(it, 1)
                    if c == FCH - 1:
                        lows(xt, it * 2 + 17, it * 2 + 1, G_PLE)
                for j in range(DU):
                    jj = 7 * DU + j
                    if j == 3:
                        dve.wait_ge(multiplied, W + 7 * DU)
                        add_x(None, 0, 6)
                    split_lo(W + jj, jj % RING, nk_down(j))

            def ple_gate_out(i):
                dve.wait_ge(multiplied, PLE_U + 5 * i + 4)
                dve.tensor_tensor(fg1[:], pg[:, 0, :, 0:N], both_inv, ALU.mult).then_inc(evacuated, 1)

            def ple_out(i):
                dve.wait_ge(multiplied, PLE_U + 5 * i + 5)
                dve.wait_ge(sem("psig_ready"), i + 1)
                o.settle()
                dve.tensor_tensor(fmd[:], pg[:, 1, :, 0:N], fsg[:], ALU.mult).then_inc(evacuated, 1)
                dve.wait_ge(evacuated, PLE_P + 2 * i + 2)
                xs = xt[:, 2 * i:2 * i + 2, :]
                dve.tensor_tensor(xs, xs, fmd[:], ALU.add).then_inc(sem("xf_ready"), 1)
                dve.wait_ge(sem("xf_ready"), i + 1)

            dve.wait_ge(sem("phi_ready"), 1)
            dve.tensor_tensor(plo[:], pf[:], phi[:].bitcast(F32), ALU.subtract).then_inc(sem("plo_ready"), 1)
            for i in range(8):
                u = PLE_U + 5 * i

                def s(j):
                    split_lo(u + j, (5 * i + j) % RING, UK if j < 4 else 2)
                s(0)
                if i == 0:
                    lows(xt, 22, 6, G_PLE)
                s(1)
                s(2) if i == 0 else None
                if i == 0:
                    dve.wait_ge(multiplied, PLE_U)
                    add_x(None, 1, 7)
                    s(3)
                    lows(xt, 23, 7, G_PLE)
                    s(4)
                    norm(2)
                else:
                    ple_gate_out(i - 1)
                    s(2)
                    ple_out(i - 1)
                    s(3)
                    s(4)
            ple_gate_out(7)
            ple_out(7)
            norm(3)
            for t in range(3):
                n = CHUNKS[t][1]
                key = ("fin", 2 * t + 1)
                wait_filled(dve, key)
                if t == 2:
                    dve.wait_ge(sem("y_stored_0"), 16)
                drain(dve.tensor_scalar(yo[0:n, t % 2, 1024:2048].rearrange("p (k c) -> p k c", k=2), ps(key)[0:n],
                                        invt[0:n, t:t + 1], None, ALU.mult), key)

        @block.tensor
        def _(pe):
            def begin(key):
                r, i = fill_at[key]
                if i:
                    pe.wait_ge(drained[r], i)
                return ps(key)

            def end(ins, key):
                ins.then_inc(filled[fill_at[key][0]], 1)

            def unit(u, r, par, k0, nk, first, last, hi, lo):
                pe.wait_ge(w_lo, u + 1)
                for m in range(2):
                    for k in range(nk):
                        wh, wl = whi[:, r, k, m * P:(m + 1) * P], wlo[:, r, k, m * P:(m + 1) * P]
                        a_hi, a_lo = hi[:, k0 + k, :], lo[:, k0 + k, :]
                        for part, (w, a) in enumerate(((wh, a_hi), (wh, a_lo), (wl, a_hi))):
                            ins = pe.matmul(pg[:, par, m, 0:N], w, a, start=first and k == 0 and part == 0,
                                            stop=last and k == nk - 1 and part == 2)
                ins.then_inc(multiplied, 1)

            def token_transposes(out, cols, src):
                for c, (c0, n) in enumerate(CHUNKS):
                    ins = pe.transpose(out[:, c0:c0 + n], src[0:n, c, cols], ident[0:n, 0:n])
                return ins

            def norm(i):
                pe.wait_ge(sem("acc_added"), 8 * (i + 1))
                key = ("norm", i)
                out = begin(key)
                if i < 3:
                    ins = pe.matmul(out[:, 0, 0:N], ones[:], acc[:], start=True, stop=True)
                if i in (0, 3):
                    for c, (c0, n) in enumerate(CHUNKS):
                        ins = pe.matmul(out[0:n, 1, c:c + 1], acc[:, c0:c0 + n], ones[:, 0:1], start=True, stop=True)
                end(ins, key)

            def per_head(key, n, lhs, rhs, rows=None):
                out = begin(key)
                for h in range(H):
                    ins = pe.matmul(out[0:rows or P, h // 4, (h % 4) * n:(h % 4) * n + n], lhs(h), rhs(h), start=True, stop=True)
                end(ins, key)

            def side(key):
                what, a = key[0], key[1:]
                if what == "par":
                    pe.wait_ge(sem("par_landed"), 16 * 8)
                    pe.wait_ge(sem("ident_ready"), 1)
                    out = begin(key)
                    pe.transpose(out[:, 0, 0:81], par1n[:], ident[0:81, 0:81])
                    end(pe.transpose(out[:, 1, 0:CW * KC], par2n[:], ident[0:CW * KC, 0:CW * KC]), key)
                    pe.wait_ge(sem("csn_landed"), 16)
                    key = ("cst",)
                    out = begin(key)
                    for t in range(KC):
                        c = (t % 12) * 3 * NB
                        ins = pe.transpose(out[:, t // 12, c:c + 3 * NB], csn[:, t * P:(t + 1) * P], ident[0:3 * NB, 0:3 * NB])
                    end(ins, key)
                elif what == "x":
                    if a[0] == 0:
                        pe.wait_ge(sem("x_landed"), 48)
                    out = begin(key)
                    for m in range(2):
                        t = 2 * a[0] + m
                        ins = token_transposes(out[:, m], slice(t * P, (t + 1) * P), xtok)
                    end(ins, key)
                elif what == "norm":
                    norm(0)
                elif what == "s5par":
                    pe.wait_ge(sem("s5_vector"), 3)
                    out = begin(key)
                    for i, k in enumerate((3, 8, 7, 9, 10, 11, 12)):
                        ins = pe.transpose(out[:, 0, i * NT:(i + 1) * NT], sc5[:, k, :], ident[0:NT, 0:NT])
                    end(ins, key)
                elif what == "h0":
                    pe.wait_ge(sem("h0_landed"), 32)
                    out = begin(key)
                    for r in range(2):
                        for k in range(2):
                            ins = pe.transpose(out[:, r, k * P:(k + 1) * P], h0n[:, r, k, :], ident[:])
                    end(ins, key)
                elif what == "bb":
                    pe.wait_ge(sem("bmix_ready"), 1)
                    for r in range(2):
                        key = ("bbt", r)
                        out = begin(key)
                        for k in range(K5):
                            ins = pe.transpose(out[:, k // 4, (k % 4) * P:(k % 4 + 1) * P],
                                               bmix[:, r, 4 * k:4 * k + 4].rearrange("p t h c -> p (t h c)"), ident[:])
                        end(ins, key)
                elif what == "ct":
                    pe.wait_ge(sem("cnat_landed"), 64)
                    for r in range(2):
                        key = ("ct", r)
                        out = begin(key)
                        for k in range(K5):
                            ins = pe.transpose(out[:, k // 4, (k % 4) * P:(k % 4 + 1) * P],
                                               cnat[:, r, k].rearrange("p h n -> p (h n)"), ident[:])
                        end(ins, key)
                elif what == "ba":
                    pe.wait_ge(sem("wba_landed"), 16)
                    pe.wait_ge(sem("xlo_ready"), KD)
                    out = begin(key)
                    for c, (c0, n) in enumerate(CHUNKS):
                        for k in range(KD):
                            for part, x in enumerate((xhi, xlo)):
                                ins = pe.matmul(out[0:n, 0, 16 * c:16 * c + 16], x[:, k, c0:c0 + n].bitcast(F32), wba[:, k, :],
                                                start=k == 0 and part == 0, stop=k == KD - 1 and part == 1)
                    end(ins, key)
                elif what == "s5":
                    hq = a[0]
                    pe.wait_ge(evacuated, hq // 4 + 1)
                    if hq == 0:
                        wait_drained(pe, ("ct", 1))
                    for t in range(2):
                        key = ("bu", hq, t)
                        c, q = (2 * hq + t) // 4, (2 * hq + t) % 4
                        rows = slice(32 * q, 32 * q + 32)
                        out = begin(key)
                        for r in range(2):
                            ins = pe.matmul(out[:, r, 0:N], bbt[rows, r, c, :], yt[rows, c, :], start=True, stop=True)
                        end(ins, key)
                    if hq:
                        readout(hq - 1)
                elif what == "s5y":
                    readout(NT // 2 - 1)
                elif what == "s5out":
                    pe.wait_ge(sem("last_states"), NT // 2)
                    key = ("hl",)
                    out = begin(key)
                    for r in range(2):
                        pe.transpose(out[0:NT, r, 0:P], hl[:, r, 0, :], ident[:])
                        for k in range(2):
                            ins = pe.transpose(out[:, r, (k + 1) * P:(k + 2) * P],
                                               hl[:, r, 1 + 4 * k:5 + 4 * k, :].rearrange("p b t -> p (b t)"), ident[:])
                    end(ins, key)
                elif what == "tail":
                    pe.wait_ge(sem("tails_ready"), 1)
                    for j in range(3):
                        key = ("tail", j)
                        out = begin(key)
                        for t in range(8):
                            ins = pe.transpose(out[0:27, t // 4, (t % 4) * P:(t % 4 + 1) * P], tail[:, 8 * j + t, :], ident[:])
                        end(ins, key)
                elif what == "l2":
                    j = a[0]
                    pe.wait_ge(sem("l2sq_ready"), j + 1)
                    out = begin(key)
                    for m in range(2):
                        ins = pe.matmul(out[:, m, 0:NCV], ones[:], sql[:, m, 0:NCV], start=True, stop=True)
                    end(ins, key)
                elif what == "dg":
                    c = a[0]
                    n = CHUNKS[c][1]
                    tri = (cum if c < 2 else cums)[0:n, 0:n]
                    pe.wait_ge(sem("g_ready"), 1)
                    key = ("gcum", c)
                    end(pe.matmul(begin(key)[0:n, 0, 0:H], tri, gt[0:n, c, :], start=True, stop=True), key)
                    per_head(("grow", c), n, lambda h: gt[0:n, c, h:h + 1].to_broadcast([n, P]), lambda h: tri)
                    per_head(("brow", c), n, lambda h: bet[0:n, c, h:h + 1].to_broadcast([n, P]), lambda h: ident[0:n, 0:n])
                elif what == "dkv":
                    c = a[0]
                    c0, n = CHUNKS[c]
                    pe.wait_ge(sem("qk_normed"), 2 * H)
                    pe.wait_ge(sem("vsm_ready"), 1)
                    for nm in ("kt", "vt"):
                        key = (nm, c)
                        out = begin(key)
                        for h in range(H):
                            if nm == "kt":
                                src = kt[:, h, c0:c0 + n]
                            elif c < 2:
                                src = qkv[:, 2 * H + h, c0:c0 + n]
                            else:
                                src = vsm[:, h, :]
                            ins = pe.transpose(out[0:n, h // 4, (h % 4) * P:(h % 4 + 1) * P], src, ident[:])
                        end(ins, key)
                elif what == "dkk":
                    c = a[0]
                    c0, n = CHUNKS[c]
                    wait_drained(pe, ("brow", c))
                    per_head(("kk", c), n, lambda h: kt[:, h, c0:c0 + n], lambda h: kb[:, h, 0:n], n)
                    per_head(("qk", c), n, lambda h: kt[:, h, c0:c0 + n], lambda h: qt[:, h, c0:c0 + n], n)
                elif what == "m1":
                    c, k = a
                    n = CHUNKS[c][1]
                    pe.wait_ge(sem("ltm_ready"), sum(LEVELS[:c]) + k + 1)
                    if k:
                        wait_drained(pe, ("ta", c, k - 1))
                    else:
                        pe.wait_ge(sem("t_started"), c + 1)
                    per_head(key, n, lambda h: ltm[0:n, h, 0:n], lambda h: tm[0:n, h, 0:n], n)
                elif what == "tab":
                    c, k = a
                    n = CHUNKS[c][1]
                    wait_drained(pe, ("m1", c, k))
                    if k:
                        wait_drained(pe, ("tb", c, k - 1))
                    per_head(("ta", c, k), n, lambda h: tmt[0:n, h, 0:n], lambda h: m1[0:n, h, 0:n], n)
                    per_head(("tb", c, k), n, lambda h: m1[0:n, h, 0:n], lambda h: tmt[0:n, h, 0:n], n)
                elif what == "sq":
                    pe.wait_ge(sem("qg_ready"), 3)
                    for h in range(H):
                        key = ("sq", h)
                        pe.wait_ge(sem(f"st_landed_{h % 2}"), 16 * (h // 2 + 1))
                        out = begin(key)
                        for b in range(NB):
                            t = slice(NPR + b * NL, NPR + (b + 1) * NL)
                            pe.matmul(out[:, 0, b * NL:(b + 1) * NL], st_ring[h % 2][:, b, :], kt[:, h, t], start=True, stop=True)
                            ins = pe.matmul(out[:, 0, NSM + b * NL:NSM + (b + 1) * NL], st_ring[h % 2][:, b, :],
                                            eg[:, h, b * NL:(b + 1) * NL], start=True, stop=True)
                        end(ins, key)
                elif what == "ks":
                    c = a[0]
                    c0, n = CHUNKS[c]
                    if c == 1:
                        wait_drained(pe, ("s", 0))
                        out = begin(key)
                        for h in range(H):
                            ins = pe.matmul(out[0:n, h // 4, (h % 4) * P:(h % 4 + 1) * P], kt[:, h, c0:c0 + n], s_[:, h, :], start=True, stop=True)
                        end(ins, key)
                    else:
                        wait_drained(pe, ("sq", H - 1))
                        wait_drained(pe, ("sq", H - 2))
                        out = begin(key)
                        for h in range(H):
                            ins = pe.transpose(out[0:n, h // 4, (h % 4) * P:(h % 4 + 1) * P], sqt[:, h, 0:NSM], ident[:])
                        end(ins, key)
                elif what == "vn":
                    c = a[0]
                    n = CHUNKS[c][1]
                    wait_drained(pe, ("tb", c, LEVELS[c] - 1))
                    wait_drained(pe, ("vt", c))
                    if c:
                        wait_drained(pe, ("ks", c))
                    per_head(key, P, lambda h: tmt[0:n, h, 0:n], lambda h: vb[0:n, h, :], n)
                elif what == "o":
                    c = a[0]
                    n = CHUNKS[c][1]
                    wait_drained(pe, ("vn", c))
                    wait_drained(pe, ("qk", c))
                    pe.wait_ge(sem("qg_ready"), c + 1)
                    out = begin(key)
                    for h in range(H):
                        cols = slice((h % 4) * n, (h % 4) * n + n)
                        ins = pe.matmul(out[:, h // 4, cols], vn[0:n, h, :], qkd[0:n, h, 0:n], start=True, stop=c != 1)
                        if c == 1:
                            ins = pe.matmul(out[:, h // 4, cols], s_[:, h, :], eg[:, h, 0:n], start=False, stop=True)
                    end(ins, key)
                elif what == "s":
                    c = a[0]
                    pe.wait_ge(sem("kd_ready"), c + 1)
                    n = CHUNKS[c][1]
                    per_head(key, P, lambda h: ktok[0:n, h, :], lambda h: vn[0:n, h, :])
                elif what == "su":
                    h = a[0]
                    pe.wait_ge(sem("kd_ready"), 3)
                    pe.wait_ge(sem("vnb_ready"), h + 1)
                    out = begin(key)
                    for k in range(2):
                        ins = pe.matmul(out[:, k, :], ktok[0:NSM, h, :],
                                        vnb[:, h % 2, 4 * k:4 * k + 4, :].rearrange("j b e -> j (b e)"), start=True, stop=True)
                    end(ins, key)
                elif what == "on":
                    j = a[0]
                    pe.wait_ge(sem("osq_ready"), j + 1)
                    out = begin(key)
                    for m in range(2):
                        ins = pe.matmul(out[:, m, 0:N], ones[:], sq[:, m, :], start=True, stop=True)
                    end(ins, key)

            def readout(hq):
                key = ("y", hq)
                pe.wait_ge(sem("states_ready"), hq + 1)
                out = begin(key)
                for t in range(2):
                    c, q = (2 * hq + t) // 4, (2 * hq + t) % 4
                    for r in range(2):
                        ins = pe.matmul(out[32 * q:32 * q + 32, 0, 0:N], ct[:, r, c, 32 * q:32 * q + 32], gg[:, hq % 2, r, t, :],
                                        start=r == 0, stop=r == 1)
                end(ins, key)

            operands = {"u": (xhi, xlo), "qkv": (xhi, xlo), "z": (xhi, xlo), "gate": (xhi, xlo), "glu": (yhi, ylo),
                        "wa": (ghi, glo), "wb": (dhi, dlo)}
            for sides, us in slots:
                for key in sides:
                    side(key)
                for n in [units.index(u) for u in us]:
                    p, j = units[n]
                    kind, i, kts = pairs[p]
                    nk = min(UK, kts - UK * j)
                    if j == 0 and p >= 2:
                        pe.wait_ge(evacuated, p - 1)
                    if p == 0:
                        pe.wait_ge(sem("xlo_ready"), UK * (j + 1))
                    if kind == "glu" and i == 0 and j == 0:
                        pe.wait_ge(sem("ylo_ready"), 1)
                    if kind == "wa" and i == 0:
                        pe.wait_ge(sem("glu_done"), 2 * (j + 1))
                    if kind == "wb" and i == 0:
                        pe.wait_ge(sem("on_ready"), 2 * (j + 1))
                    unit(n, n % RING, p % 2, UK * j, nk, j == 0, j == pair_units[p] - 1, *operands[kind])

            def pair(u0, p0, du, kts, b, it, hi, lo, par, ready=None):
                pe.wait_ge(evacuated, p0 - 1)
                nu = -(-kts // UK)
                for j in range(nu):
                    if ready is not None:
                        ready(j)
                    jj = du + j
                    unit(u0 + j, jj % RING, par, UK * j, min(UK, kts - UK * j), j == 0, j == nu - 1, hi, lo)

            def out_pair(it, b, ready=None):
                pair(it * 8 + (OUT_U + 4 * b), it * 2 + (OUT_P + b), 4 * b, KD, b, it, mxhi, mxlo, b, ready)

            out_pair(0, 0, lambda j: pe.wait_ge(sem("mix_ready"), 2 * (j + 1)))
            out_pair(0, 1)
            with pe.Fori(1, 4) as it:
                out_pair(it, 0)
                out_pair(it, 1)
            for c in range(FCH):
                def gate_up(it, b, ready=None):
                    pair(it * 8 + (FFN_U[c] + 4 * b), it * 2 + (FFN_P[c] + b), 4 * b, KD, b, it, xhi, xlo, b, ready)

                def ffn_in(j):
                    pe.wait_ge(sem("xlo_ready"), KD + 4 * (j + 1))
                gate_up(0, 0, ffn_in if c == 0 else None)
                if c == 0:
                    norm(1)
                gate_up(0, 1)
                with pe.Fori(1, KFC // 2) as it:
                    gate_up(it, 0)
                    gate_up(it, 1)

                def down(it, b, ready=None):
                    pair(it * (2 * DU) + (DOWN_U[c] + DU * b), it * 2 + (DOWN_P[c] + b), DU * b, KFC, b, it, mhi, mlo, b, ready)
                down(0, 0, lambda j: pe.wait_ge(sem("mlo_ready"), c * (KFC // 2) + min(2 * (j + 1), KFC // 2)))
                if c == 0:
                    pe.wait_ge(sem("p_landed"), 48)
                    key = ("pt",)
                    out = begin(key)
                    for m in range(2):
                        ins = token_transposes(out[:, m], slice(m * P, (m + 1) * P), ptok)
                    end(ins, key)
                down(0, 1)
                with pe.Fori(1, 4) as it:
                    down(it, 0)
                    down(it, 1)

            def ple(it, b, ready=None, ready_p=None):
                pair(it * 20 + (PLE_U + 5 * b), it * 8 + (PLE_P + 2 * b), 5 * b, KD, b, it, xhi, xlo, 0, ready)
                pair(it * 20 + (PLE_U + 5 * b + 4), it * 8 + (PLE_P + 2 * b + 1), 5 * b + 4, 2, b, it, phi, plo, 1, ready_p)

            ple(0, 0, lambda j: pe.wait_ge(sem("xlo_ready"), 2 * KD + 4 * (j + 1)), lambda j: pe.wait_ge(sem("plo_ready"), 1))
            norm(2)
            for b in range(1, 4):
                ple(0, b)
            with pe.Fori(1, 2) as it:
                for b in range(4):
                    ple(it, b)
            pe.wait_ge(sem("xg_ready"), KD)
            norm(3)
            for f in range(6):
                key = ("fin", f)
                c0, n = CHUNKS[f // 2]
                out = begin(key)
                for t in range(8):
                    ins = pe.transpose(out[0:n, t // 4, (t % 4) * P:(t % 4 + 1) * P], xg[:, 8 * (f % 2) + t, c0:c0 + n], ident[:])
                end(ins, key)


_INS = ["x_prompt", "x_sample", "state_conv", "state_delta", "state_s5_re", "state_s5_im", "p_prompt", "p_sample",
        "g_mix", "w_in", "conv_w", "a_log", "dt_bias", "onorm_w", "s5_a_re", "s5_a_im", "s5_b_re", "s5_b_im",
        "s5_c_re", "s5_c_im", "s5_d", "s5_log_dt", "w_glu", "b_glu", "w_a", "w_b", "w_out", "g_ffn", "w_gate",
        "w_up", "w_down", "g_ple", "w_ple", "w_ple_gate", "g_final"]
_OUTS = [("y_prompt", (1, NPR, D)), ("y_sample", (NB, NL, D)), ("conv_prompt", (1, 1, CW - 1, CCH)),
         ("delta_prompt", (1, 1, H, P, P)), ("s5_re_prompt", (1, 1, 64, ST)), ("s5_im_prompt", (1, 1, 64, ST)),
         ("conv_sample", (1, NB, CW - 1, CCH)), ("delta_sample", (1, NB, H, P, P)),
         ("s5_re_sample", (1, NB, 64, ST)), ("s5_im_sample", (1, NB, 64, ST))]


def kernel(**inputs):
    import numpy as np
    import concourse.bacc as bacc
    from concourse.bass_utils import run_bass_kernel_spmd

    nc = bacc.Bacc("TRN2", target_bir_lowering=False, num_devices=1)
    arrays, args = {}, []
    for name in _INS:
        a = np.ascontiguousarray(inputs[name])
        arrays[f"in_{name}"] = a
        args.append(nc.dram_tensor(f"in_{name}", a.shape, mybir.dt.from_np(a.dtype), kind="ExternalInput").ap())
    for name, shape in _OUTS:
        args.append(nc.dram_tensor(f"out_{name}", shape, F32, kind="ExternalOutput").ap())
    hybrid_layer(nc, *args)
    r = run_bass_kernel_spmd(nc, [arrays], core_ids=[0])
    return tuple(r.results[0][f"out_{name}"] for name, _ in _OUTS)
```

```python
import math
from contextlib import ExitStack

import concourse.bass as bass
from concourse import mybir

F32 = mybir.dt.float32
F32R = mybir.dt.float32r
BF16 = mybir.dt.bfloat16
ACT = mybir.ActivationFunctionType
ALU = mybir.AluOpType
AX = mybir.AxisListType

P = 128
NPR = 256
NB, NL = 8, 8
NSM = NB * NL
N = NPR + NSM
D = 2048
KD = D // P
W5 = D // 2
K5 = W5 // P
H = 8
CW = 4
CCH = 3 * W5
KC = CCH // P
SEQP = CW - 1 + NPR
SEQS = CW - 1 + NL
NPAD = SEQP + NB * SEQS
NCV = NPAD - (CW - 1)
FF = 5632
KF = FF // P
FCH = 2
KFC = KF // FCH
PLE = 256
ST = 64
NT = 32
EPS = 1e-6
OFF_U, OFF_QKV = W5, W5 + CCH
OFF_Z = OFF_QKV + W5
OFF_BETA = OFF_Z + H
OFF_A = OFF_BETA + H
OFF_GA = OFF_A + D
CHUNKS = [(0, 128), (128, 128), (256, 64)]
LEVELS = [7, 7, 3]
UK = 4
RING = 4
PW = 256
MAGIC = 1.5 * 2.0 ** 23
TWO_PI_PARTS = (6.28125, 0.0019350051879882812, 3.019916e-07)


class Steps:

    def __init__(self, eng, sem):
        self.eng, self.sem, self.n = eng, sem, 0

    def step(self, ins):
        ins.then_inc(self.sem, 1)
        self.n += 1

    def settle(self, but=0):
        if self.n > but:
            self.eng.wait_ge(self.sem, self.n - but)

    def link(self, ins):
        self.step(ins)
        self.settle()


def side_fills():
    keys = [("par",), ("cst",), ("x", 0), ("x", 1), ("s5par",), ("h0",)] + [("x", j) for j in range(2, KD // 2)]
    keys += [("norm", 0), ("bbt", 0), ("bbt", 1), ("ct", 0), ("ct", 1), ("ba",), ("bat",)]
    order = [("ba"[i % 2], key) for i, key in enumerate(keys)]
    for hq in range(NT // 2):
        order += [("a", ("bu", hq, 0)), ("b", ("bu", hq, 1))]
        if hq:
            order += [("a", ("y", hq - 1))]
    order += [("a", ("y", NT // 2 - 1)), ("b", ("hl",))]
    order += [("ab"[j % 2], ("tail", j)) for j in range(3)]
    order += [("ba"[j % 2], ("l2", j)) for j in range(H)]
    for c in range(3):
        order += [("b", ("gcum", c)), ("a", ("grow", c)), ("b", ("brow", c)), ("a", ("kt", c)), ("b", ("vt", c)),
                  ("a", ("kk", c)), ("b", ("qk", c))]
        for k in range(LEVELS[c]):
            order += [("a", ("m1", c, k))]
            order += [("b", ("ta", c, k))] * (0 < k < LEVELS[c] - 1) + [("ab"[k == LEVELS[c] - 1], ("tb", c, k))] * (k > 0)
        if c == 1:
            order += [("b", ("ks", 1))]
        if c == 2:
            order += [("ab"[h % 2], ("sq", h)) for h in range(H)] + [("b", ("ks", 2))]
        order += [("a", ("vn", c)), ("b", ("o", c))]
        if c < 2:
            order += [("a", ("s", c))]
        else:
            order += [("ab"[h % 2], ("su", h)) for h in range(H)]
    order += [("ab"[j % 2], ("on", j)) for j in range(H // 2)]
    order += [("a", ("norm", 1)), ("b", ("pt",)), ("a", ("emb", 0)), ("b", ("norm", 2))]
    order += [("ba"[i % 2], ("emb", i)) for i in range(1, KD // 2)] + [("b", ("norm", 3))]
    order += [("ab"[j % 2], ("fin", j)) for j in range(6)]
    count, signals, at = {"a": 0, "b": 0}, {"a": 0, "b": 0}, {}
    for region, key in order:
        at[key] = (region, count[region], signals[region])
        count[region] += 1
        signals[region] += key[0] != "emb"
    return at


def mixer_pairs():
    return ([("u", i, KD) for i in range(4)] + [("qkv", i, KD) for i in range(12)]
            + [("z", i, KD) for i in range(4)] + [("gate", i, KD) for i in range(16)]
            + [("glu", i, K5) for i in range(4)] + [("wa", i, K5) for i in range(8)]
            + [("wb", i, K5) for i in range(8)])


def schedule():
    pairs = mixer_pairs()
    units = [(p, j) for p, (_, _, k) in enumerate(pairs) for j in range(-(-k // UK))]
    first = {}
    for n, (p, j) in enumerate(units):
        first.setdefault(pairs[p][0], n)
    slots, at = [], 0

    def slot(sides, n):
        nonlocal at
        slots.append((sides, units[at:at + n]))
        at += n
        if first["glu"] < at <= first["glu"] + n:
            slots.append(([("ysplit",)], []))

    slot([("const",), ("par",), ("s5a",), ("x", 0), ("s5b",), ("x", 1), ("s5par",), ("h0",)], 0)
    for j in range(2, KD // 2, 2):
        slot([("x", j), ("x", j + 1)], 1)
    slot([("norm", 0), ("bmix",)], 4)
    slot([("bb",), ("ct",)], 4)
    slot([("ba",)], 4)
    for hq in range(NT // 2):
        slot([("s5", hq)], 3 + (hq % 2 and hq > 1))
    slot([("s5y",)], 1)
    assert first["z"] + 4 <= at < first["z"] + 8
    slot([("tailc",), ("s5out",), ("tail",)], 1)
    for h in range(H):
        slot([("conv", h)], 2)
    slot([("l2a", 0)], 1)
    for j in range(H):
        slot([("l2", j)] + [("l2a", j + 1)] * (j + 1 < H), 1)
    slot([("l2e", 0), ("l2e", 1)], 1)
    for c in range(3):
        slot([("dg", c)], 1)
        slot([("dkv", c)], 1)
        slot([("dkk", c)], 1)
        for k in range(LEVELS[c]):
            slot([("m1", c, k)], 0 if c < 2 and k in (2, 4) else 1)
            if k:
                slot([("tab", c, k)], 1)
        if c == 2:
            for h in range(H):
                slot([("sq", h)], 1)
        if c:
            slot([("ks", c)], 1)
        slot([("vn", c)], 1)
        slot([("o", c)], 1)
        if c < 2:
            slot([("s", c)], 1)
        else:
            for i in range(H):
                slot([("su", i)], 1)
    slot([("ona", 0)], 1)
    for j in range(H // 2):
        slot([("on", j)] + [("ona", j + 1)] * (j + 1 < H // 2), 2)
    slot([], len(units) - at)
    uses, prev, n = [], None, 0
    for sides, us in slots:
        for p, j in us:
            n += 1
            if j == -(-pairs[p][2] // UK) - 1:
                if prev and prev[0] in ("wa", "wb"):
                    uses.append((prev, n))
                prev = pairs[p][0:2]
        uses += [(key, n) for key in sides if key[0] == "on"]
    uses.append((prev, n))
    return pairs, units, slots, uses


class Zone:

    def __init__(self, nc, at, size):
        self.nc, self.at, self.end = nc, at, at + size

    def take(self, name, shape, dt=F32):
        size = math.prod(shape[1:]) * (2 if dt == BF16 else 4)
        size = -(-size // 32) * 32
        assert self.at + size <= self.end, (name, self.at + size - self.end)
        t = self.nc.alloc_sbuf_tensor_at(name, list(shape), dt, offset=self.at)
        self.at += size
        return t


def hybrid_layer(nc, x_prompt, x_sample, state_conv, state_delta, state_s5_re, state_s5_im, p_prompt, p_sample,
                 g_mix, w_in, conv_w, a_log, dt_bias, onorm_w, s5_a_re, s5_a_im, s5_b_re, s5_b_im,
                 s5_c_re, s5_c_im, s5_d, s5_log_dt, w_glu, b_glu, w_a, w_b, w_out, g_ffn, w_gate, w_up,
                 w_down, g_ple, w_ple, w_ple_gate, g_final,
                 y_prompt, y_sample, conv_prompt, delta_prompt, s5_re_prompt, s5_im_prompt,
                 conv_sample, delta_sample, s5_re_sample, s5_im_sample):
    pairs, units, slots, uses = schedule()
    fill_at = side_fills()
    pair_units = [-(-k // UK) for _, _, k in pairs]
    pair_first = [sum(pair_units[:p]) for p in range(len(pairs))]
    pair_of = {(kind, i): p for p, (kind, i, _) in enumerate(pairs)}
    MIX_UNITS, MIX_PAIRS = len(units), len(pairs)
    OUT_U, OUT_P = MIX_UNITS, MIX_PAIRS
    first_wa = pair_first[pair_of["wa", 0]]
    FFN_U = [OUT_U + 4 * 8, 0]
    FFN_P = [OUT_P + 8, 0]
    DOWN_U, DOWN_P = [0, 0], [0, 0]
    DU = -(-KFC // UK)
    for c in range(FCH):
        DOWN_U[c], DOWN_P[c] = FFN_U[c] + 8 * (KFC // 2), FFN_P[c] + KFC
        if c + 1 < FCH:
            FFN_U[c + 1], FFN_P[c + 1] = DOWN_U[c] + 8 * DU, DOWN_P[c] + 8
    PLE_U, PLE_P = DOWN_U[-1] + 8 * DU, DOWN_P[-1] + 8
    assert MIX_UNITS % RING == 0 and OUT_U % RING == 0 and all(u % RING == 0 for u in FFN_U + DOWN_U)

    with ExitStack() as ctx:
        sem_of = {}

        def sem(name):
            if name not in sem_of:
                sem_of[name] = ctx.enter_context(nc.semaphore(name))
            return sem_of[name]

        base = -(-nc.sbuf_base // 32) * 32
        size = nc.sbuf_usable_end - base
        zw = Zone(nc, base, RING * 12 * 1024)
        raw = zw.take("raw", [P, RING, UK, PW])
        whi = zw.take("whi", [P, RING, UK, PW], F32R)
        wlo = zw.take("wlo", [P, RING, UK, PW], F32R)
        zx = Zone(nc, zw.end, 2 * KD * N * 4)
        xhi = zx.take("xhi", [P, KD, N], F32R)
        xlo = zx.take("xlo", [P, KD, N], F32R)
        zq_at = zx.end
        zq = Zone(nc, zq_at, KC * NPAD * 4)
        qkv = zq.take("qkv", [P, KC, NPAD])
        zy = Zone(nc, zq.end, K5 * N * 4)
        yt = zy.take("yt", [P, K5, N])
        zc = Zone(nc, zy.end, 10240)
        ident = zc.take("ident", [P, P])
        ones = zc.take("ones", [P, P])
        cum = zc.take("cum", [P, P])
        cums = zc.take("cums", [NSM, NSM])
        strict = zc.take("strict", [P, P], BF16)
        stricts = zc.take("stricts", [NSM, NSM], BF16)
        lvl = zc.take("lvl", [P, 7, P], BF16)
        inv = zc.take("inv", [P, N])
        start = zc.take("start", [P, N])
        par1 = zc.take("par1", [P, 81])
        par2 = zc.take("par2", [P, CW * KC])
        half = zc.take("half", [P, 2])
        cst = zc.take("cst", [P, 4])
        seqm = zc.take("seqm", [NSM, NB])
        invt = zc.take("invt", [P, 4])
        gab = zc.take("gab", [P, 2 * H])
        bet = zc.take("bet", [P, 3, H])
        gt = zc.take("gt", [P, 3, H])
        gc = zc.take("gc", [P, 3, H])
        nbe = zc.take("nbe", [P, 3, H])
        ba = zc.take("ba", [P, 3, 2 * H])
        egl = zc.take("egl", [P, H, NB])
        dl = zc.take("dl", [P, H])
        egc = zc.take("egc", [P, H])
        sp3 = zc.take("sp3", [P, 3, H])
        G_MIX, G_FFN, G_PLE, G_FINAL, D5, BGLU, ONW = 0, 16, 32, 48, 64, 72, 80
        arena_at = zc.end
        arena = base + size - arena_at

        zs = Zone(nc, arena_at, arena)
        sq = zs.take("sq", [P, 2, N])
        acc = zs.take("acc", [P, N])
        arena_at, arena = zs.at, arena - (zs.at - arena_at)
        zt = Zone(nc, arena_at, arena)
        xtok = zt.take("xtok", [P, 3, D])
        xt0 = Zone(nc, zq_at, KC * NPAD * 4).take("xt0", [P, KD, N])

        z5 = Zone(nc, arena_at, arena)
        uu = z5.take("uu", [P, 2, 2, 2, N])
        gg = z5.take("gg", [P, 2, 2, 2, N])
        tt = z5.take("tt", [P, 2, 2, N])
        bbt = z5.take("bbt", [P, 2, K5, P])
        ct = z5.take("ct", [P, 2, K5, P])
        tb = z5.take("tb", [P, 2, NT, 16])
        bu = z5.take("bu", [P, 2, 2, N])
        mm = z5.take("mm", [P, 2, N])
        ta = z5.take("ta", [P, 2, NT, 16])
        a0 = z5.take("a0", [P, 2, NT, NB])
        sp5 = z5.take("sp5", [P, 7, NT])
        pt5 = z5.take("pt5", [P, 2, 2, 256])
        hl = Zone(nc, arena_at - 3 * N * 4, 2 * N * 4).take("hl", [P, 2, NB + 1, NT])
        zpre = Zone(nc, zq_at + KD * N * 4, (KC * NPAD - KD * N) * 4)
        spar = zpre.take("spar", [NT, 3, P])
        sc5 = zpre.take("sc5", [NT, 16, P])
        wba = zpre.take("wba", [P, KD, 2 * H])
        wbhi = zpre.take("wbhi", [P, KD, 2 * H], F32R)
        zpre2 = Zone(nc, arena_at, 3 * D * 4)
        bmix = zpre2.take("bmix", [P, 2, NT, 2, 16])
        bt1 = zpre2.take("bt1", [P, NT, 16])
        bt2 = zpre2.take("bt2", [P, NT, 16])
        cnat = zpre2.take("cnat", [P, 2, K5, 2, ST])
        bu_at = arena_at + 5 * 2 * 2 * N * 4 + (2 * 2 * K5 * P + 2 * NT * 16) * 4
        zpre3 = Zone(nc, bu_at, 2 * 2 * N * 4)
        h0n = zpre3.take("h0n", [P, 2, 2, P])
        h0s = zpre3.take("h0s", [P, 2, NT, NB])
        cstt = Zone(nc, bu_at + 2 * 2 * N * 4, 2 * N * 4).take("cstt", [P, KC, 3 * NB])
        hlo = Zone(nc, arena_at + 16384, 3072).take("hlo", [P, 2, 3, P])
        sc5w = Zone(nc, z5.at - 2048, 2048).take("sc5w", [P, 8, NT])
        zpar = Zone(nc, arena_at + 3 * D * 4, 1024 + CCH * 4 + 4096)
        par1n = zpar.take("par1n", [81, P])
        par2n = zpar.take("par2n", [CW * KC, P])
        csn = zpar.take("csn", [3 * NB, CCH])
        bnat = zpar.take("bnat", [P, 2, NT, 16])
        zba = Zone(nc, arena_at - 3 * N * 4, 3 * N * 4)
        wblo = zba.take("wblo", [P, KD, 2 * H], F32R)
        bafm = zba.take("bafm", [2 * H, N])

        zd = Zone(nc, arena_at, arena)
        kt = zd.take("kt", [P, H, N])
        qt = zd.take("qt", [P, H, N])
        s_ = zd.take("s_", [P, H, P])
        ktok = zd.take("ktok", [P, H, P])
        vb = zd.take("vb", [P, H, P])
        vn = zd.take("vn", [P, H, P])
        eg = zd.take("eg", [P, H, P])
        dt_ = zd.take("dt_", [P, H, P])
        qkd = zd.take("qkd", [P, H, P])
        stg = zd.take("stg", [P, 2, 2, N])
        g1 = zd.take("g1", [P, 2, N])
        gr = zd.take("gr", [P, 2, 2, N])
        kq = Zone(nc, zd.at - 5120, 4096).take("kq", [P, H, NB, 2 * NL])
        vsm = zd.take("vsm", [P, H, NSM])
        zl = Zone(nc, zq_at, 2 * H * NPAD * 4)
        lt = zl.take("lt", [P, H, P])
        ltm = zl.take("ltm", [P, H, P])
        m1 = zl.take("m1", [P, H, P])
        tm = zl.take("tm", [P, H, P])
        tmt = zl.take("tmt", [P, H, P])
        kb = m1
        zc2 = Zone(nc, arena_at + 2 * K5 * N * 4, 6 * 4096)
        cacc = zc2.take("cacc", [P, 2, 3, NPAD])
        sql = zc2.take("sql", [P, 2, NPAD])
        zt2 = Zone(nc, arena_at, 2 * K5 * N * 4)
        tail = zt2.take("tail", [P, KC, 3 + 3 * NB])
        ttok = zt2.take("ttok", [27, CCH])
        zs2 = Zone(nc, arena_at + 2 * K5 * N * 4, 16384)
        sqt = zs2.take("sqt", [P, H, P])
        zst = Zone(nc, zq_at, 4 * 4096)
        st_ring = [zst.take("st2", [P, NB, P]), zst.take("st3", [P, NB, P])]
        vnb = zst.take("vnb", [NSM, 2, NB, P])
        zst2 = Zone(nc, zq_at + 2 * H * NPAD * 4, H * NPAD * 4)
        st_ring = [zst2.take("st0", [P, NB, P]), zst2.take("st1", [P, NB, P])] + st_ring
        x_at, half_x = zx.at - 2 * KD * N * 4, K5 * N * 4
        yhi = Zone(nc, x_at, half_x).take("yhi", [P, K5, N], F32R)
        ylo = Zone(nc, x_at + half_x, half_x).take("ylo", [P, K5, N], F32R)
        ghi = Zone(nc, x_at + 2 * half_x, half_x).take("ghi", [P, K5, N], F32R)
        glo = Zone(nc, x_at + 3 * half_x, half_x).take("glo", [P, K5, N], F32R)
        tg = Zone(nc, arena_at - 3 * N * 4, 2 * N * 4).take("tg", [P, 2, N])
        mixa = Zone(nc, x_at, KD * N * 4).take("mixa", [P, KD, N])
        mxlo = Zone(nc, zq_at + KD * N * 4, KD * N * 4).take("mxlo", [P, KD, N], F32R)
        dhi = Zone(nc, arena_at, half_x).take("dhi", [P, K5, N], F32R)
        dlo = Zone(nc, arena_at + half_x, half_x).take("dlo", [P, K5, N], F32R)
        zm = Zone(nc, arena_at + 2 * half_x, KD * N * 4 + 2560)
        mxhi = zm.take("mxhi", [P, KD, N], F32R)
        t1 = zm.take("t1", [P, 2, N])

        xt = Zone(nc, zq_at, KD * N * 4).take("xt", [P, KD, N])
        zf2 = Zone(nc, zq_at + KD * N * 4, (KC * NPAD - KD * N) * 4)
        fg1 = zf2.take("fg1", [P, 2, N])
        fsg = zf2.take("fsg", [P, 2, N])
        fsi = zf2.take("fsi", [P, 2, N])
        fmd = zf2.take("fmd", [P, 2, N])
        pf = zf2.take("pf", [P, 2, N])
        zp = Zone(nc, zy.at - K5 * N * 4, K5 * N * 4)
        phi = zp.take("phi", [P, 2, N], F32R)
        plo = zp.take("plo", [P, 2, N], F32R)
        ptok = zp.take("ptok", [P, 3, PLE])
        zmid = Zone(nc, arena_at, arena)
        mhi = zmid.take("mhi", [P, KFC, N], F32R)
        mlo = zmid.take("mlo", [P, KFC, N], F32R)
        zo = Zone(nc, arena_at, arena)
        yo = zo.take("yo", [P, 2, D])
        xg = zo.take("xg", [P, KD, N])

        scr_x = nc.dram_tensor("scratch_x", [P, KD, N], F32, kind="Internal").ap()
        scr_g = nc.dram_tensor("scratch_gates", [P, 40, N], F32, kind="Internal").ap()

        pg = ctx.enter_context(nc.psum_tensor("pg", [P, 2, 2, 512], F32))
        side_ps = {r: ctx.enter_context(nc.psum_tensor(f"side_{r}", [P, 2, 512], F32)) for r in "ab"}
        filled = {r: sem(f"side_{r}_filled") for r in "ab"}
        drained = {r: sem(f"side_{r}_drained") for r in "ab"}

        def ps(key):
            return side_ps[fill_at[key][0]]

        def wait_filled(eng, key):
            r, _, i = fill_at[key]
            eng.wait_ge(filled[r], i + 1)

        def wait_drained(eng, key):
            r, i, _ = fill_at[key]
            eng.wait_ge(drained[r], i + 1)

        def drain(ins, key):
            ins.then_inc(drained[fill_at[key][0]], 1)

        def heads(t, c):
            return t[:, :, 0:CHUNKS[c][1]]

        def hview(key, c, n=None, rows=P):
            n = n or CHUNKS[c][1]
            return ps(key)[0:rows, :, 0:4 * n].rearrange("p k (h c) -> p k h c", h=4)

        def hsplit(ap):
            return ap.rearrange("p (k h) c -> p k h c", k=2)

        raw_landed = [sem(f"raw_landed_{r}") for r in range(RING)]
        w_hi, w_lo, multiplied = sem("w_hi_ready"), sem("w_lo_ready"), sem("units_multiplied")
        evacuated = sem("pair_evacuated")

        def rows_of(w, k0, nk, cols):
            return w[0, k0 * P:(k0 + nk) * P, cols].rearrange("(k p) c -> p k c", p=P)

        mixer_w = {"u": (w_in, 0), "qkv": (w_in, OFF_U), "z": (w_in, OFF_QKV), "gate": (w_in, OFF_A),
                   "glu": (w_glu, 0), "wa": (w_a, 0), "wb": (w_b, 0)}

        block = ctx.enter_context(nc.Block())

        @block.sync
        def _(sp):
            def load_unit(u, r, src, nk, first_lap=False):
                if not first_lap:
                    sp.wait_ge(w_hi, u - RING + 1)
                    sp.wait_ge(w_lo, u - RING + 1)
                sp.dma_start(raw[:, r, 0:nk, :], src).then_inc(raw_landed[r], 16)

            tokens = [(x_prompt[0, 0:P], P), (x_prompt[0, P:2 * P], P), (x_sample.rearrange("b l d -> (b l) d"), NSM)]
            for c, (src, n) in enumerate(tokens):
                sp.dma_start(xtok[0:n, c, :], src).then_inc(sem("x_landed"), 16)
            sp.wait_ge(sem("spar_landed"), 48)

            def load_mixer(n):
                p, j = units[n]
                kind, i, k = pairs[p]
                w, off = mixer_w[kind]
                nk = min(UK, k - UK * j)
                load_unit(n, n % RING, rows_of(w, UK * j, nk, slice(off + PW * i, off + PW * (i + 1))), nk, n < RING)

            def spill(n):
                sp.wait_ge(sem("stage_written"), n + 1)
                sp.dma_start(scr_g[:, 2 * n:2 * n + 2, :], stg[:, n % 2]).then_inc(sem(f"stage_stored_{n % 2}"), 16)

            due = [first_wa - 2] * 2 + [min(uses[n - 2][1] + 3, MIX_UNITS) for n in range(2, 20)]

            def fetch(n):
                if n == 0:
                    wait_filled(sp, ("sq", H - 1))
                    for s in range(2):
                        sp.wait_ge(sem(f"stage_stored_{s}"), 16 * 10)
                if n >= 2:
                    kind, i = uses[n - 2][0]
                    if kind == "on":
                        sp.wait_ge(sem("on_ready"), i + 1)
                    else:
                        sp.wait_ge(evacuated, pair_of[kind, i] + 1)
                kind, i = uses[n][0]
                src = {"wa": 4 + i, "on": i, "wb": 12 + i}[kind]
                sp.dma_start(gr[:, n % 2], scr_g[:, 2 * src:2 * src + 2, :]).then_inc(sem(f"gate_landed_{n % 2}"), 16)

            spilled = fetched = 0
            for n, (p, j) in enumerate(units):
                load_mixer(n)
                if j == pair_units[p] - 1 and p >= 2 and pairs[p - 2][0] in ("z", "gate"):
                    spill(spilled)
                    spilled += 1
                while fetched < 20 and due[fetched] == n + 1:
                    fetch(fetched)
                    fetched += 1

            sp.wait_ge(sem("x_stored"), 16)
            sp.wait_ge(sem("on_ready"), H // 2)
            for s in range(4):
                sp.wait_ge(sem(f"st_stored_{s}"), 16 * (H // 4))
            sp.dma_start(xt[:], scr_x).then_inc(sem("xt_landed"), 16)

            with sp.Fori(0, 4) as it:
                for b in range(2):
                    for j in range(4):
                        load_unit(OUT_U + it * 8 + 4 * b + j, j,
                                  rows_of(w_out, UK * j, UK, bass.ds((it * 2 + b) * PW, PW)), UK)
            for c in range(FCH):
                with sp.Fori(0, KFC // 2) as it:
                    for b, w in enumerate((w_gate, w_up)):
                        for j in range(4):
                            load_unit(FFN_U[c] + it * 8 + 4 * b + j, j,
                                      rows_of(w, UK * j, UK, bass.ds(it * PW + c * KFC * P, PW)), UK)
                if c == 0:
                    for t, (src, n) in enumerate([(p_prompt[0, 0, 0:P], P), (p_prompt[0, 0, P:2 * P], P),
                                                  (p_sample[0].rearrange("b l d -> (b l) d"), NSM)]):
                        sp.dma_start(ptok[0:n, t, :], src).then_inc(sem("p_landed"), 16)
                with sp.Fori(0, 4) as it:
                    for b in range(2):
                        for j in range(DU):
                            nk = min(UK, KFC - UK * j)
                            load_unit(DOWN_U[c] + it * 2 * DU + DU * b + j, (DU * b + j) % RING,
                                      rows_of(w_down, c * KFC + UK * j, nk, bass.ds((it * 2 + b) * PW, PW)), nk)
            with sp.Fori(0, 2) as it:
                for b in range(4):
                    for j in range(5):
                        w, k0, nk = (w_ple_gate, UK * j, UK) if j < 4 else (w_ple, 0, 2)
                        load_unit(PLE_U + it * 20 + 5 * b + j, (5 * b + j) % RING,
                                  rows_of(w, k0, nk, bass.ds((it * 4 + b) * PW, PW)), nk)

            for t in range(3):
                dst, n = [(y_prompt[0, 0:P], P), (y_prompt[0, P:2 * P], P),
                          (y_sample.rearrange("b l d -> (b l) d"), NSM)][t]
                for f in (2 * t, 2 * t + 1):
                    wait_drained(sp, ("fin", f))
                sp.dma_start(dst, yo[0:n, t % 2, :]).then_inc(sem(f"y_stored_{t % 2}"), 16)
            sp.wait_ge(sem("y_stored_0"), 32)
            sp.wait_ge(sem("y_stored_1"), 16)
            sp.wait_ge(sem("tail_stored"), 32)
            sp.wait_ge(sem("hl_stored"), 16 * 4)
            sp.wait_ge(sem("s_stored"), 16)

        @block.gpsimd
        def _(pool):
            o = Steps(pool, sem("pool_steps"))

            def tensor(out, a, b, op, link=True):
                ins = pool.tensor_tensor(out, a, b, op)
                o.link(ins) if link else o.step(ins)

            def select(t, pattern, op, base, cm, fill=0.0):
                o.link(pool.affine_select(t, t, pattern=pattern, compare_op=op, fill=fill, base=base,
                                          channel_multiplier=cm))

            def const():
                o.step(pool.memset(ones[:], 1.0))
                o.link(pool.memset(ident[:], 0.0))
                pool.affine_select(ident[:], ident[:], pattern=[[-1, P]], compare_op=ALU.not_equal, fill=1.0, base=0,
                                   channel_multiplier=1).then_inc(sem("ident_ready"), 1)
                o.step(pool.memset(cst[:, 0:1], EPS))
                o.step(pool.memset(cst[:, 1:2], P * EPS))
                pool.memset(cst[:, 2:3], math.pi / 2).then_inc(sem("cst_ready"), 1)
                o.link(pool.memset(half[:], 1.0))
                select(half[:, 0:1], [[0, 1]], ALU.is_ge, 63, -1)
                o.step(pool.affine_select(half[:, 1:2], half[:, 1:2], pattern=[[0, 1]], compare_op=ALU.is_ge, fill=0.0,
                                          base=-64, channel_multiplier=1))
                o.step(pool.memset(start[:], 1.0))
                o.settle()
                o.step(pool.memset(start[:, 0:1], 0.0))
                pool.memset(start[:, NPR:N:NL], 0.0).then_inc(sem("start_ready"), 1)

            def masks():
                for t, n in ((cum, P), (cums, NSM)):
                    o.link(pool.memset(t[:], 1.0))
                    select(t[:], [[1, n]], ALU.is_ge, 0, -1)
                for t, n in ((strict, P), (stricts, NSM)):
                    o.link(pool.memset(t[:], 1.0))
                    select(t[:], [[1, n]], ALU.is_gt, 0, -1)
                for t in (cums, stricts):
                    v = t[:].rearrange("p (b l) -> p b l", l=NL)
                    select(v, [[-NL, NB], [0, NL]], ALU.is_ge, 0, 1)
                    select(v, [[NL, NB], [0, NL]], ALU.is_ge, NL - 1, -1)
                o.link(pool.memset(lvl[:], 0.0))
                for k in range(7):
                    s = 1 << k
                    v = lvl[:, k, :].rearrange("p (b h s) -> p b h s", h=2, s=s)[:, :, 1, :]
                    o.link(pool.memset(v, 1.0))
                    select(v, [[-2 * s, P // (2 * s)], [0, s]], ALU.is_ge, 0, 1)
                    select(v, [[2 * s, P // (2 * s)], [0, s]], ALU.is_ge, s - 1, -1)
                o.link(pool.memset(seqm[:], 1.0))
                select(seqm[:], [[-NL, NB]], ALU.is_ge, 0, 1)
                pool.affine_select(seqm[:], seqm[:], pattern=[[NL, NB]], compare_op=ALU.is_ge, fill=0.0, base=NL - 1,
                                   channel_multiplier=-1).then_inc(sem("masks_ready"), 1)

            def clear_sum(n):
                wait_filled(pool, ("norm", n))
                o.link(pool.memset(acc[:], 0.0))

            def square(r, i, ar, ai, t):
                tensor(t[0], ar, ar, ALU.mult, False)
                tensor(t[1], ai, ai, ALU.mult, False)
                tensor(t[2], ar, ai, ALU.mult)
                tensor(r, t[0], t[1], ALU.subtract, False)
                tensor(i, t[2], t[2], ALU.add)

            def product(r, i, ar, ai, br, bi, t0, t1, last=None):
                tensor(t0, ar, br, ALU.mult, False)
                tensor(t1, ai, bi, ALU.mult)
                tensor(r, t0, t1, ALU.subtract)
                tensor(t0, ar, bi, ALU.mult, False)
                tensor(t1, ai, br, ALU.mult)
                tensor(i, t0, t1, ALU.add)

            def powers(t, sr, si):
                o.step(pool.memset(t[:, 0, :, 0:1], 1.0))
                o.step(pool.memset(t[:, 1, :, 0:1], 0.0))
                o.step(pool.tensor_copy(t[:, 0, :, 1:2], sr.unsqueeze(2)))
                o.link(pool.tensor_copy(t[:, 1, :, 1:2], si.unsqueeze(2)))
                w = sc5w
                cur = (sr, si)
                for k in range(1, 5):
                    nxt = (w[:, 2 * (k % 2), :], w[:, 2 * (k % 2) + 1, :])
                    square(nxt[0], nxt[1], cur[0], cur[1], [w[:, 4 + e, :] for e in range(3)])
                    cur = nxt
                    n = 1 << k
                    if n < 16:
                        def bc(v):
                            return v.unsqueeze(2).broadcast_to([P, NT, n])
                        product(t[:, 0, :, n:2 * n], t[:, 1, :, n:2 * n], t[:, 0, :, 0:n], t[:, 1, :, 0:n],
                                bc(cur[0]), bc(cur[1]), pt5[:, 0, 0, :].rearrange("p (t n) -> p t n", n=8)[:, :, 0:n],
                                pt5[:, 0, 1, :].rearrange("p (t n) -> p t n", n=8)[:, :, 0:n])
                return cur

            def tables():
                wait_drained(pool, ("s5par",))
                cur = powers(tb, sp5[:, 1, :], sp5[:, 2, :])
                powers(ta, *cur)

            def h0_terms():
                wait_drained(pool, ("h0",))
                lr = sp5[:, 3, :].unsqueeze(2).broadcast_to([P, NT, NB])
                li = sp5[:, 4, :].unsqueeze(2).broadcast_to([P, NT, NB])
                hr, hi = h0s[:, 0], h0s[:, 1]
                t0 = pt5[:, 0, 0, :].rearrange("p (t b) -> p t b", b=NB)
                t1 = pt5[:, 0, 1, :].rearrange("p (t b) -> p t b", b=NB)
                product(a0[:, 0], a0[:, 1], lr, li, hr, hi, t0, t1)

            def phases(hq):
                s = hq % 2
                if hq >= 2:
                    pool.wait_ge(sem("states_ready"), hq - 1)
                elif hq == 0:
                    wait_filled(pool, ("ct", 1))
                shape = [P, 2, 16, 16]
                ar = ta[:, 0, 2 * hq:2 * hq + 2, :].unsqueeze(3).broadcast_to(shape)
                ai = ta[:, 1, 2 * hq:2 * hq + 2, :].unsqueeze(3).broadcast_to(shape)
                br = tb[:, 0, 2 * hq:2 * hq + 2, :].unsqueeze(2).broadcast_to(shape)
                bi = tb[:, 1, 2 * hq:2 * hq + 2, :].unsqueeze(2).broadcast_to(shape)

                def v(t):
                    return t.rearrange("p t (a b) -> p t a b", b=16)
                product(v(uu[:, s, 0, :, 0:NPR]), v(uu[:, s, 1, :, 0:NPR]), ar, ai, br, bi, v(pt5[:, 0]), v(pt5[:, 1]))
                src = uu[:, s, :, :, 0:NL].rearrange("p r t l -> p (r t) l").unsqueeze(2).broadcast_to([P, 4, NB, NL])
                dst = uu[:, s, :, :, NPR:N].rearrange("p r t (b l) -> p (r t) b l", l=NL)
                pool.tensor_copy(dst, src).then_inc(sem("phases_ready"), 1)

            def inverse_start(c):
                n = CHUNKS[c][1]
                if c:
                    wait_filled(pool, ("vn", c - 1))
                else:
                    pool.wait_ge(sem("qk_normed"), 4)
                src = ident[0:n, 0:n].unsqueeze(1).broadcast_to([n, H, n])
                o.step(pool.tensor_copy(tm[0:n, :, 0:n], src))
                pool.tensor_copy(tmt[0:n, :, 0:n], src).then_inc(sem("t_started"), 1)

            def strict_lt(c):
                n = CHUNKS[c][1]
                m = (strict if c < 2 else stricts)[0:n, 0:n].unsqueeze(1).broadcast_to([n, H, n])
                if c == 2:
                    v = kq[:].rearrange("p h b (s l) -> p h b s l", s=2)
                    o.step(pool.tensor_copy(v[:, :, :, 0, :], kt[:, :, NPR:N].rearrange("p h (b l) -> p h b l", l=NL)))
                wait_drained(pool, ("kk", c))
                pool.tensor_tensor(lt[0:n, :, 0:n], lt[0:n, :, 0:n], m, ALU.mult).then_inc(sem("lt_ready"), 1)

            def block_values(i):
                if i == 0:
                    wait_drained(pool, ("vn", 2))
                    wait_filled(pool, ("o", 2))
                if i >= 2:
                    wait_filled(pool, ("su", i - 2))
                src = vn[0:NSM, (i + 4) % H, :].unsqueeze(1).broadcast_to([NSM, NB, P])
                m = seqm[:].unsqueeze(2).broadcast_to([NSM, NB, P])
                pool.tensor_tensor(vnb[:, i % 2], src, m, ALU.mult).then_inc(sem("vnb_ready"), 1)

            def load_state(n):
                if n >= H:
                    pool.wait_ge(sem(f"st_stored_{n % 4}"), 16)
                elif n >= 4:
                    wait_filled(pool, ("sq", n - 4))
                elif n >= 2:
                    wait_drained(pool, ("tb", 2, LEVELS[2] - 1))
                else:
                    wait_filled(pool, ("vt", 2))
                src = state_delta[0, :, n % H].rearrange("b d e -> d b e")
                pool.dma_start(st_ring[n % 4][:], src).then_inc(sem(f"st_landed_{n % 4}"), 16)

            def store_state(i):
                wait_drained(pool, ("su", i))
                pool.dma_start(delta_sample[0, :, (i + 4) % H].rearrange("b d e -> d b e"),
                               st_ring[i % 4][:]).then_inc(sem(f"st_stored_{i % 4}"), 16)

            for sides, us in slots:
                for key in sides:
                    what, a = key[0], key[1:]
                    if what == "const":
                        const()
                    elif what == "s5y":
                        masks()
                    elif what == "h0":
                        tables()
                        h0_terms()
                    elif what == "ct":
                        phases(0)
                    elif what == "s5" and a[0] + 1 < NT // 2:
                        phases(a[0] + 1)
                    elif what == "tail":
                        for j in range(3):
                            wait_drained(pool, ("tail", j))
                        pool.dma_start(conv_prompt[0, 0], ttok[0:3, :]).then_inc(sem("tail_stored"), 16)
                        pool.dma_start(conv_sample[0].rearrange("b j c -> (b j) c"), ttok[3:27, :]).then_inc(sem("tail_stored"), 16)
                    elif what == "s5out":
                        wait_drained(pool, ("hl",))
                        for r, (op_, os_) in enumerate(((s5_re_prompt, s5_re_sample), (s5_im_prompt, s5_im_sample))):
                            pool.dma_start(op_[0, 0].rearrange("(t g) n -> t (g n)", g=2), hlo[0:NT, r, 0, :]).then_inc(sem("hl_stored"), 16)
                            pool.dma_start(os_[0].rearrange("b (t g) n -> (b t) (g n)", g=2).rearrange("(k r) c -> r k c", k=2),
                                           hlo[:, r, 1:3, :]).then_inc(sem("hl_stored"), 16)
                    elif what == "dkk":
                        inverse_start(*a)
                        strict_lt(*a)
                    elif what == "s" and a[0] == 1:
                        wait_drained(pool, key)
                        pool.dma_start(delta_prompt[0, 0].rearrange("h d e -> d h e"), s_[:]).then_inc(sem("s_stored"), 16)
                    elif what == "dkv" and a[0] == 2:
                        load_state(0)
                        load_state(1)
                    elif what == "sq":
                        if a[0] == 0:
                            load_state(2)
                            load_state(3)
                        if a[0] + 4 < H:
                            load_state(a[0] + 4)
                    elif what == "su":
                        i = a[0]
                        block_values(i)
                        if i:
                            store_state(i - 1)
                        if 2 <= i < 6:
                            load_state(H + i - 2)
                        if i == H - 1:
                            store_state(i)

            def add_loop(first, last):
                n0 = o.n
                with pool.Fori(0, last - first) as it:
                    pool.wait_ge(sem("sq_ready"), it + (first + 1))
                    pool.wait_ge(sem("pool_steps"), it + n0)
                    pool.tensor_tensor(acc[:], acc[:], sq[:, 0, :], ALU.add).then_inc(sem("pool_steps"), 1)
                    pool.wait_ge(sem("pool_steps"), it + (n0 + 1))
                    pool.tensor_tensor(acc[:], acc[:], sq[:, 1, :], ALU.add).then_inc(sem("acc_added"), 1)
                    pool.wait_ge(sem("acc_added"), it + (first + 1))
                o.n = n0 + last - first

            pool.wait_ge(sem("on_ready"), H // 2)
            o.link(pool.memset(acc[:], 0.0))
            add_loop(8, 16)
            clear_sum(1)
            for c in range(FCH):
                with pool.Fori(0, KFC // 2) as it:
                    pool.wait_ge(sem("silu_ready"), it + (c * (KFC // 2) + 1))
                    pool.tensor_tensor(fsi[:], fsg[:], inv[:].unsqueeze(1).broadcast_to([P, 2, N]),
                                       ALU.mult).then_inc(sem("fsi_ready"), 1)
            add_loop(16, 24)
            clear_sum(2)
            add_loop(24, 32)

        @block.scalar
        def _(act):
            o = Steps(act, sem("scalar_steps"))

            def split_hi(u, r, nk, lap0=False):
                act.wait_ge(raw_landed[r], 16 * (u // RING + 1) if isinstance(u, int) else u * 4 + (16 - 4 * r))
                if not lap0:
                    act.wait_ge(multiplied, u - RING + 1)
                act.activation(whi[:, r, 0:nk, :], raw[:, r, 0:nk, :], ACT.Copy).then_inc(w_hi, 1)

            def copy(out, in_, scale=1.0):
                return act.activation(out, in_, ACT.Copy, scale=scale)

            def finish(x, n, j, gcol):
                if not (isinstance(n, int) and n == 0):
                    act.wait_ge(sem("acc_added"), n)
                act.activation(sq[:], x[:, bass.ds(j * 2, 2), :], ACT.Square).then_inc(sem("sq_ready"), 1)
                if gcol is None:
                    return
                for m in range(2):
                    act.activation(xhi[:, bass.ds(j * 2 + m, 1), :], x[:, bass.ds(j * 2 + m, 1), :], ACT.Copy,
                                   scale=par1[:, bass.ds(j * 2 + (m + gcol), 1)]).then_inc(sem("xhi_ready"), 1)

            def root(n):
                key = ("norm", n)
                wait_filled(act, key)
                if n in (0, 3):
                    o.step(act.activation(invt[:, 0:2], ps(key)[:, 1, 0:2], ACT.Ln, scale=1.0 / D, bias=cst[:, 0:1]))
                    ins = act.activation(invt[0:NSM, 2:3], ps(key)[0:NSM, 1, 2:3], ACT.Ln, scale=1.0 / D, bias=cst[0:NSM, 0:1])
                    o.step(ins) if n == 0 else drain(ins, key)
                if n < 3:
                    drain(act.activation(inv[:], ps(key)[:, 0, 0:N], ACT.Ln, scale=1.0 / D, bias=cst[:, 0:1]), key)
                wait_drained(act, key)
                if n in (0, 3):
                    o.step(act.activation(invt[:, 0:2], invt[:, 0:2], ACT.Exp, scale=-0.5))
                    act.activation(invt[0:NSM, 2:3], invt[0:NSM, 2:3], ACT.Exp, scale=-0.5).then_inc(sem("invt_ready"), 1)
                if n < 3:
                    act.activation(inv[:], inv[:], ACT.Exp, scale=-0.5).then_inc(sem("inv_ready"), 1)

            def inverse_root(out, in_, scale, bias):
                o.link(act.activation(out, in_, ACT.Ln, scale=scale, bias=bias))
                return act.activation(out, out, ACT.Exp, scale=-0.5)

            gates = 0

            def evac(p):
                nonlocal gates
                kind, i, _ = pairs[p]
                if kind in ("z", "gate"):
                    n = gates
                    gates += 1
                    act.wait_ge(evacuated, p + 1)
                    if n >= 2:
                        act.wait_ge(sem(f"stage_stored_{n % 2}"), 16 * (n // 2))
                    act.activation(stg[:, n % 2], g1[:], ACT.Silu if kind == "z" else ACT.Sigmoid).then_inc(sem("stage_written"), 1)
                elif kind == "glu":
                    act.wait_ge(evacuated, p + 1)
                    act.activation(g1[:], g1[:], ACT.Sigmoid).then_inc(sem("glu_sig"), 1)

            def first_taps(h):
                if h >= 2:
                    act.wait_ge(sem("silu_done"), 3 * (h - 1))
                else:
                    act.wait_ge(evacuated, pair_of["qkv", 11] + 1)
                    act.wait_ge(sem("states_ready"), NT // 2)
                    wait_filled(act, ("y", NT // 2 - 1))
                for g in range(3):
                    t = h + H * g
                    copy(cacc[:, h % 2, g, 0:NCV], qkv[:, t, 0:NCV], scale=par2[:, t:t + 1]).then_inc(sem("taps_ready"), 1)

            def silu_head(h):
                for g in range(3):
                    act.wait_ge(sem("conv_ready"), 3 * h + g + 1)
                    act.activation(qkv[:, h + H * g, 0:NCV], cacc[:, h % 2, g, 0:NCV], ACT.Silu).then_inc(sem("silu_done"), 1)

            def side(key):
                what, a = key[0], key[1:]
                if what == "const":
                    for at, w in ((G_MIX, g_mix), (G_FFN, g_ffn), (G_PLE, g_ple), (G_FINAL, g_final)):
                        src = w if w is g_final else w[0]
                        act.dma_start(par1n[at:at + KD, :], src.rearrange("(k p) -> k p", p=P)).then_inc(sem("par_landed"), 16)
                    for at, w in ((D5, s5_d), (BGLU, b_glu)):
                        act.dma_start(par1n[at:at + K5, :], w[0].rearrange("(k p) -> k p", p=P)).then_inc(sem("par_landed"), 16)
                    act.dma_start(par1n[ONW:ONW + 1, :], onorm_w).then_inc(sem("par_landed"), 16)
                    act.dma_start(par2n[:], conv_w[0].rearrange("j (k p) -> (j k) p", p=P)).then_inc(sem("par_landed"), 16)
                    for k, w in enumerate((s5_a_re, s5_a_im)):
                        act.dma_start(spar[:, k, :], w[0].rearrange("(t g) n -> t (g n)", g=2)).then_inc(sem("spar_landed"), 16)
                    act.dma_start(spar[:, 2, 0:2], s5_log_dt[0].rearrange("(t g) -> t g", g=2)).then_inc(sem("spar_landed"), 16)
                    act.dma_start(csn[:], state_conv[0].rearrange("b j c -> (b j) c")).then_inc(sem("csn_landed"), 16)
                    for r, h_ in enumerate((state_s5_re, state_s5_im)):
                        src = h_[0].rearrange("b (t g) n -> (b t) (g n)", g=2).rearrange("(k r) c -> r k c", k=2)
                        act.dma_start(h0n[:, r], src).then_inc(sem("h0_landed"), 16)
                    for r, b_ in enumerate((s5_b_re, s5_b_im)):
                        act.dma_start(bnat[:, r], b_[0].rearrange("(t g) n c -> (g n) t c", g=2)).then_inc(sem("bnat_landed"), 16)
                    act.dma_start(gab[:, 0:H], a_log.broadcast_to([P, H])).then_inc(sem("gab_landed"), 16)
                    act.dma_start(gab[:, H:2 * H], dt_bias.broadcast_to([P, H])).then_inc(sem("gab_landed"), 16)
                    act.dma_start(wba[:], w_in[0, :, OFF_Z:OFF_A].rearrange("(k p) c -> p k c", p=P)).then_inc(sem("wba_landed"), 16)
                elif what == "par":
                    wait_filled(act, key)
                    o.step(copy(par1[:], ps(key)[:, 0, 0:81]))
                    drain(copy(par2[:], ps(key)[:, 1, 0:CW * KC]), key)
                    wait_filled(act, ("cst",))
                    drain(copy(cstt[:].rearrange("p (k t) c -> p k (t c)", k=2), ps(("cst",))[:, :, 0:12 * 3 * NB]), ("cst",))
                    wait_drained(act, ("par",))
                elif what == "x":
                    j = a[0]
                    wait_filled(act, key)
                    drain(copy(xt0[:, 2 * j:2 * j + 2, :], ps(key)[:, :, 0:N]), key)
                    wait_drained(act, key)
                    finish(xt0, j, j, G_MIX)
                    if j == KD // 2 - 1:
                        for r, c_ in enumerate((s5_c_re, s5_c_im)):
                            src = c_[0].rearrange("(k g) c n -> (g c) k n", g=8)
                            for h in range(2):
                                act.dma_start(cnat[:, r, :, h, :], src).then_inc(sem("cnat_landed"), 16)
                        act.dma_start(scr_x, xt0[:]).then_inc(sem("x_stored"), 16)
                elif what == "s5a":
                    act.wait_ge(sem("spar_landed"), 48)
                    act.wait_ge(sem("cst_ready"), 1)
                    act.activation(sc5[:, 0, 0:2], spar[:, 2, 0:2], ACT.Exp).then_inc(sem("s5_scalar"), 1)
                elif what == "s5b":
                    act.wait_ge(sem("s5_vector"), 1)
                    act.activation(sc5[:, 3, :], sc5[:, 1, :], ACT.Exp).then_inc(sem("s5_scalar"), 1)
                    act.wait_ge(sem("s5_vector"), 2)
                    act.activation(sc5[:, 7, :], sc5[:, 5, :], ACT.Sin).then_inc(sem("s5_scalar"), 1)
                    act.activation(sc5[:, 8, :], sc5[:, 6, :], ACT.Sin, scale=-1.0, bias=cst[0:NT, 2:3]).then_inc(sem("s5_scalar"), 1)
                elif what == "norm":
                    root(a[0])
                    act.wait_ge(sem("wba_landed"), 16)
                    act.activation(wbhi[:], wba[:], ACT.Copy).then_inc(sem("wb_split"), 1)
                elif what == "s5par":
                    wait_filled(act, key)
                    drain(copy(sp5[:].rearrange("p a t -> p (a t)"), ps(key)[:, 0, 0:7 * NT]), key)
                elif what == "h0":
                    wait_filled(act, key)
                    drain(copy(h0s[:].rearrange("p r t b -> p r b t"), ps(key)[:, :, 0:NT * NB].rearrange("p r (b t) -> p r b t", b=NB)), key)
                elif what == "bb":
                    for r in range(2):
                        wait_filled(act, ("bbt", r))
                        drain(copy(bbt[:, r].rearrange("p (k t) c -> p k (t c)", k=2), ps(("bbt", r))[:]), ("bbt", r))
                elif what == "ba":
                    act.wait_ge(sem("gab_landed"), 32)
                    o.step(act.activation(gab[:, 0:H], gab[:, 0:H], ACT.Exp))
                    act.wait_ge(sem("ba_vector"), 1)
                    act.activation(sp3[:], sp3[:], ACT.Exp, scale=-1.0).then_inc(sem("ba_scalar"), 1)
                    act.wait_ge(sem("ba_scalar"), 1)
                    act.activation(sp3[:], sp3[:], ACT.Ln, bias=ones[:, 0:1]).then_inc(sem("ba_scalar"), 1)
                    act.activation(bet[:], ba[:, :, 0:H], ACT.Sigmoid).then_inc(sem("ba_scalar"), 1)
                elif what == "s5":
                    hq = a[0]
                    if hq == 0:
                        act.wait_ge(sem("phases_ready"), 1)
                        act.wait_ge(sem("start_ready"), 1)
                        act.wait_ge(sem("pads_done"), 1)
                    else:
                        act.wait_ge(sem("states_ready"), hq)
                        last_states(hq - 1)
                    for t in range(2):
                        k = 2 * hq + t
                        copy(mm[:, t, :], start[:], scale=sp5[:, 0, k:k + 1]).then_inc(sem("decay_ready"), 1)
                    for t in range(2):
                        wait_filled(act, ("bu", hq, t))
                        drain(copy(bu[:, :, t, :], ps(("bu", hq, t))[:, :, 0:N]), ("bu", hq, t))
                    if hq % 2 and hq >= 3:
                        gelu((hq - 3) // 2)
                elif what == "s5y":
                    act.wait_ge(sem("states_ready"), NT // 2)
                    last_states(NT // 2 - 1)
                    gelu(K5 - 1)
                elif what == "s5out":
                    wait_filled(act, ("hl",))
                    o.step(act.activation(hlo[0:NT, :, 0, :], ps(("hl",))[0:NT, :, 0:P], ACT.Copy))
                    drain(copy(hlo[:, :, 1:3, :], ps(("hl",))[:, :, P:3 * P].rearrange("p r (k c) -> p r k c", k=2)), ("hl",))
                elif what == "tail":
                    first_taps(0)
                    for j in range(3):
                        wait_filled(act, ("tail", j))
                        drain(copy(ttok[:, j * 1024:(j + 1) * 1024].rearrange("p (k c) -> p k c", k=2),
                                   ps(("tail", j))[0:27, :, :]), ("tail", j))
                elif what == "conv":
                    if a[0]:
                        silu_head(a[0] - 1)
                    if a[0] + 1 < H:
                        first_taps(a[0] + 1)
                elif what == "l2a":
                    j = a[0]
                    if j == 0:
                        silu_head(H - 1)
                        act.wait_ge(sem("silu_done"), 3 * H)
                    if j == 0:
                        src = qkv[:, 2 * H:3 * H, SEQP:NPAD].rearrange("p h (b l) -> p h b l", l=SEQS)[:, :, :, 0:NL]
                        copy(vsm[:].rearrange("p h (b l) -> p h b l", l=NL), src).then_inc(sem("vsm_ready"), 1)
                    if j:
                        wait_filled(act, ("l2", j - 1))
                    act.activation(sql[:, :, 0:NCV], qkv[:, 2 * j:2 * j + 2, 0:NCV], ACT.Square).then_inc(sem("l2sq_ready"), 1)
                elif what == "l2":
                    j = a[0]
                    wait_filled(act, key)
                    if j == 0:
                        act.wait_ge(sem("tail_stored"), 32)
                        act.wait_ge(sem("hl_stored"), 64)
                    q = j < H // 2
                    dst, scale, bias = (qt, float(P), cst[:, 1:2]) if q else (kt, 1.0, cst[:, 0:1])
                    t = slice(2 * (j % 4), 2 * (j % 4) + 2)
                    o.step(act.activation(dst[:, t, 0:NPR], ps(key)[:, :, 0:NPR], ACT.Ln, scale=scale, bias=bias))
                    v = ps(key)[:, :, SEQP:SEQP + NB * SEQS].rearrange("p t (b l) -> p t b l", l=SEQS)[:, :, :, 0:NL]
                    drain(act.activation(dst[:, t, NPR:N].rearrange("p t (b l) -> p t b l", l=NL), v, ACT.Ln, scale=scale,
                                         bias=bias), key)
                elif what == "l2e":
                    for j in range(H - 2, H):
                        wait_drained(act, ("l2", j))
                    dst = (qt, kt)[a[0]]
                    for k in range(2):
                        t = slice(4 * k, 4 * k + 4)
                        act.activation(dst[:, t, :], dst[:, t, :], ACT.Exp, scale=-0.5).then_inc(sem("norms_ready"), 1)
                elif what == "dg":
                    c = a[0]
                    n = CHUNKS[c][1]
                    act.wait_ge(sem("gdiff_ready"), H * (c + 1))
                    if c:
                        wait_filled(act, ("o", c - 1))
                    drain(act.activation(hsplit(eg[:, :, 0:n]), hview(("grow", c), c), ACT.Exp), ("grow", c))
                    act.activation(dt_[0:n, :, 0:n], dt_[0:n, :, 0:n], ACT.Exp).then_inc(sem("decay_exp"), 1)
                    act.activation(egc[0:n, :], gc[0:n, c, :], ACT.Exp).then_inc(sem("decay_exp"), 1)
                elif what == "dkv":
                    c = a[0]
                    n = CHUNKS[c][1]
                    wait_filled(act, ("kt", c))
                    drain(act.activation(hsplit(ktok[0:n]), ps(("kt", c))[0:n].rearrange("p k (h c) -> p k h c", h=4), ACT.Copy), ("kt", c))
                    wait_filled(act, ("vt", c))
                    for h in range(H):
                        ins = copy(vb[0:n, h, :], ps(("vt", c))[0:n, h // 4, (h % 4) * P:(h % 4 + 1) * P], scale=bet[0:n, c, h:h + 1])
                        o.step(ins) if h < H - 1 else drain(ins, ("vt", c))
                elif what == "m1" and a[1]:
                    c, k = a
                    n = CHUNKS[c][1]
                    wait_filled(act, key)
                    drain(act.activation(hsplit(m1[0:n, :, 0:n]), hview(key, c, rows=n), ACT.Copy), key)
                elif what == "vn":
                    n = CHUNKS[a[0]][1]
                    wait_filled(act, key)
                    drain(act.activation(hsplit(vn[0:n]), ps(key)[0:n].rearrange("p k (h c) -> p k h c", h=4), ACT.Copy), key)
                elif what == "o" and a[0] < 2:
                    c0, n = CHUNKS[a[0]]
                    wait_filled(act, key)
                    drain(act.activation(hsplit(qt[:, :, c0:c0 + n]), hview(key, a[0]), ACT.Copy), key)
                elif what == "sq":
                    if a[0] == 0:
                        act.wait_ge(sem("s_stored"), 16)
                    wait_filled(act, key)
                    drain(copy(sqt[:, a[0], :].rearrange("p (s b l) -> p s b l", s=2, l=NL),
                               ps(key)[:, 0, 0:P].rearrange("p (b s l) -> p s b l", s=2, l=NL)), key)
                elif what == "ysplit":
                    act.wait_ge(multiplied, pair_first[pair_of["gate", 15]] + 4)
                    act.wait_ge(sem("gelu_done"), K5)
                    for k in range(0, K5, UK):
                        act.activation(yhi[:, k:k + UK, :], yt[:, k:k + UK, :], ACT.Copy).then_inc(sem("yhi_ready"), 1)
                elif what == "ona":
                    j = a[0]
                    if j:
                        wait_filled(act, ("on", j - 1))
                    else:
                        wait_drained(act, ("o", 2))
                        act.wait_ge(sem("glu_done"), 4)
                    act.activation(sq[:], qt[:, 2 * j:2 * j + 2, :], ACT.Square).then_inc(sem("osq_ready"), 1)
                elif what == "on":
                    j = a[0]
                    wait_filled(act, key)
                    if j:
                        act.wait_ge(sem("on_ready"), j)
                    drain(inverse_root(g1[:], ps(key)[:, :, 0:N], 1.0 / P, cst[:, 0:1]), key)

            def last_states(hq):
                s = hq % 2
                o.step(copy(hl[:, :, 0, 2 * hq:2 * hq + 2], gg[:, s, :, :, NPR - 1]))
                copy(hl[:, :, 1:NB + 1, 2 * hq:2 * hq + 2].rearrange("p r b t -> p r t b"),
                     gg[:, s, :, :, NPR + NL - 1:N:NL]).then_inc(sem("last_states"), 1)

            def gelu(c):
                wait_drained(act, ("y", 2 * c + 1))
                act.activation(yt[:, c, :], yt[:, c, :], ACT.Gelu_apprx_tanh).then_inc(sem("gelu_done"), 1)

            prev = None
            for sides, us in slots:
                for n in [units.index(u) for u in us]:
                    p, j = units[n]
                    split_hi(n, n % RING, min(UK, pairs[p][2] - UK * j), n < RING)
                    if j == pair_units[p] - 1:
                        if prev is not None:
                            evac(prev)
                        prev = p
                for key in sides:
                    side(key)

            def finish_out(n, j, gcol):
                act.wait_ge(evacuated, n + (OUT_P - 7))
                finish(xt, n, j, gcol)

            def units_of(u0, js, nk=lambda j: UK):
                for j in js:
                    split_hi(u0 + j, j % RING, nk(j))

            units_of(OUT_U, range(4))
            evac(prev)
            with act.Fori(0, 3) as it:
                for b in range(2):
                    for j in range(4):
                        split_hi(OUT_U + 4 + 4 * b + it * 8 + j, j, UK)
                    finish_out(it * 2 + (8 + b), it * 2 + b, G_FFN)
            units_of(OUT_U + 28, range(4))
            finish_out(14, 6, G_FFN)

            def silu(c, i):
                act.wait_ge(evacuated, i * 2 + (FFN_P[c] + 1))
                act.activation(fsg[:], fg1[:], ACT.Silu).then_inc(sem("silu_ready"), 1)

            def hidden(c, i):
                act.wait_ge(evacuated, i * 2 + (FFN_P[c] + 2))
                act.activation(mhi[:, bass.ds(i * 2, 2), :], fmd[:], ACT.Copy).then_inc(sem("mhi_ready"), 1)

            nk_down = lambda j: min(UK, KFC - UK * (j % DU))
            HF = KFC // 2
            for c in range(FCH):
                units_of(FFN_U[c], range(4))
                if c == 0:
                    finish_out(15, 7, G_FFN)
                units_of(FFN_U[c] + 4, range(4))
                if c == 0:
                    root(1)
                silu(c, 0)
                units_of(FFN_U[c] + 8, range(4))
                hidden(c, 0)
                with act.Fori(0, HF - 2) as it:
                    for j in range(4):
                        split_hi(FFN_U[c] + 12 + it * 8 + j, j, UK)
                    silu(c, it + 1)
                    for j in range(4):
                        split_hi(FFN_U[c] + 16 + it * 8 + j, j, UK)
                    hidden(c, it + 1)
                units_of(FFN_U[c] + 8 * HF - 4, range(4))
                silu(c, HF - 1)
                units_of(DOWN_U[c], range(DU), nk_down)
                hidden(c, HF - 1)
                n0 = 16

                def down_pair(it, b):
                    for j in range(DU):
                        jj = DU + b * DU + j
                        split_hi(DOWN_U[c] + jj + it * 2 * DU, jj % RING, nk_down(j))
                    if c == FCH - 1:
                        act.wait_ge(evacuated, it * 2 + (DOWN_P[c] + 1 + b))
                        finish(xt, it * 2 + (n0 + b), it * 2 + b, G_PLE)

                with act.Fori(0, 3) as it:
                    for b in range(2):
                        down_pair(it, b)
                for j in range(DU):
                    jj = 7 * DU + j
                    split_hi(DOWN_U[c] + jj, jj % RING, nk_down(j))
                if c == FCH - 1:
                    act.wait_ge(evacuated, DOWN_P[c] + 7)
                    finish(xt, 22, 6, G_PLE)

            def gate_sig(i):
                act.wait_ge(evacuated, PLE_P + i + 1)
                act.activation(fsg[:], fg1[:], ACT.Sigmoid).then_inc(sem("psig_ready"), 1)

            def final_x(i):
                act.wait_ge(sem("xf_ready"), i + 1)
                finish(xt, i + 24, i, None)
                for m in range(2):
                    act.activation(xg[:, bass.ds(i * 2 + m, 1), :], xt[:, bass.ds(i * 2 + m, 1), :], ACT.Copy,
                                   scale=par1[:, bass.ds(i * 2 + (m + G_FINAL), 1)]).then_inc(sem("xg_ready"), 1)

            wait_drained(act, ("pt",))
            act.activation(phi[:], pf[:], ACT.Copy).then_inc(sem("phi_ready"), 1)
            for i in range(8):
                u = PLE_U + 5 * i
                for j in range(3):
                    split_hi(u + j, (5 * i + j) % RING, UK)
                    if i == 1 and j == 1:
                        root(2)
                if i:
                    gate_sig(i - 1)
                split_hi(u + 3, (5 * i + 3) % RING, UK)
                if i:
                    final_x(i - 1)
                else:
                    act.wait_ge(evacuated, PLE_P)
                    finish(xt, 23, 7, G_PLE)
                split_hi(u + 4, (5 * i + 4) % RING, 2)
            gate_sig(7)
            final_x(7)
            root(3)
            act.wait_ge(sem("invt_ready"), 2)
            for t in range(3):
                n = CHUNKS[t][1]
                key = ("fin", 2 * t)
                wait_filled(act, key)
                if t == 2:
                    act.wait_ge(sem("y_stored_0"), 16)
                drain(act.activation(yo[0:n, t % 2, 0:D // 2].rearrange("p (k c) -> p k c", k=2), ps(key)[0:n], ACT.Copy,
                                     scale=invt[0:n, t:t + 1]), key)

        @block.vector
        def _(dve):
            o = Steps(dve, sem("vector_steps"))

            def both(t):
                return t[:].unsqueeze(1).broadcast_to([P, 2, N])

            def split_lo(u, r, nk):
                dve.wait_ge(w_hi, u + 1)
                dve.tensor_tensor(wlo[:, r, 0:nk, :], raw[:, r, 0:nk, :], whi[:, r, 0:nk, :].bitcast(F32),
                                  ALU.subtract).then_inc(w_lo, 1)

            def lows(x, n, j, gcol):
                for m in range(2):
                    dve.wait_ge(sem("xhi_ready"), n * 2 + (m + 1))
                    dve.scalar_tensor_tensor(out=xlo[:, bass.ds(j * 2 + m, 1), :], in0=x[:, bass.ds(j * 2 + m, 1), :],
                                             scalar=par1[:, bass.ds(j * 2 + (m + gcol), 1)],
                                             in1=xhi[:, bass.ds(j * 2 + m, 1), :].bitcast(F32),
                                             op0=ALU.mult, op1=ALU.subtract).then_inc(sem("xlo_ready"), 1)

            def norm(n):
                dve.wait_ge(sem("inv_ready"), n + 1)

            gates = 0

            def stored_gate(kind, i):
                n = [u for u, _ in uses].index((kind, i))
                dve.wait_ge(sem(f"gate_landed_{n % 2}"), 16 * (n // 2 + 1))
                return gr[:, n % 2]

            def evac(p):
                nonlocal gates
                kind, i, _ = pairs[p]
                dve.wait_ge(multiplied, pair_first[p] + pair_units[p])
                src = pg[:, p % 2, :, 0:N]
                if kind == "u":
                    dve.tensor_tensor(yt[:, 2 * i:2 * i + 2, :], src, both(inv), ALU.mult).then_inc(evacuated, 1)
                elif kind == "qkv":
                    if i == 0:
                        dve.wait_ge(sem("x_stored"), 16)
                    t = slice(2 * i, 2 * i + 2)
                    o.step(dve.tensor_tensor(qkv[:, t, CW - 1:SEQP], pg[:, p % 2, :, 0:NPR],
                                             inv[:, 0:NPR].unsqueeze(1).broadcast_to([P, 2, NPR]), ALU.mult))
                    dst = qkv[:, t, SEQP:NPAD].rearrange("p t (b l) -> p t b l", l=SEQS)[:, :, :, CW - 1:SEQS]
                    dve.tensor_tensor(dst, pg[:, p % 2, :, NPR:N].rearrange("p t (b l) -> p t b l", l=NL),
                                      inv[:, NPR:N].rearrange("p (b l) -> p b l", l=NL).unsqueeze(1).broadcast_to([P, 2, NB, NL]),
                                      ALU.mult).then_inc(evacuated, 1)
                elif kind in ("z", "gate"):
                    if gates:
                        dve.wait_ge(sem("stage_written"), gates)
                    gates += 1
                    dve.tensor_tensor(g1[:], src, both(inv), ALU.mult).then_inc(evacuated, 1)
                elif kind == "glu":
                    dve.wait_ge(sem("stage_written"), 20)
                    o.settle()
                    for m in range(2):
                        k = BGLU + 2 * i + m
                        ins = dve.tensor_scalar(g1[:, m, :], src[:, m, :], par1[:, k:k + 1], None, ALU.add)
                        o.step(ins) if m == 0 else ins.then_inc(evacuated, 1)
                elif kind == "wa":
                    dve.tensor_tensor(mixa[:, 2 * i:2 * i + 2, :], src, stored_gate("wa", i), ALU.mult).then_inc(evacuated, 1)
                elif kind == "wb":
                    if i == 0:
                        for s in range(2):
                            dve.wait_ge(sem(f"st_stored_{s}"), 16 * (H // 4))
                    o.settle()
                    dve.tensor_tensor(t1[:], src, stored_gate("wb", i), ALU.mult).then_inc(evacuated, 1)
                    dve.wait_ge(evacuated, p + 1)
                    t = slice(2 * i, 2 * i + 2)
                    o.link(dve.tensor_tensor(t1[:], t1[:], mixa[:, t, :], ALU.add))
                    o.link(dve.tensor_copy(mxhi[:, t, :], t1[:]))
                    dve.tensor_tensor(mxlo[:, t, :], t1[:], mxhi[:, t, :].bitcast(F32), ALU.subtract).then_inc(sem("mix_ready"), 1)
                    dve.wait_ge(sem("mix_ready"), i + 1)

            def late(p):
                kind, i, _ = pairs[p]
                if kind == "glu":
                    t = slice(2 * i, 2 * i + 2)
                    dve.wait_ge(sem("glu_sig"), i + 1)
                    o.settle()
                    o.link(dve.tensor_tensor(tg[:], yt[:, t, :], g1[:], ALU.mult))
                    o.link(dve.tensor_copy(ghi[:, t, :], tg[:]))
                    dve.tensor_tensor(glo[:, t, :], tg[:], ghi[:, t, :].bitcast(F32), ALU.subtract).then_inc(sem("glu_done"), 1)
                    dve.wait_ge(sem("glu_done"), i + 1)

            def s5_scalars():
                dve.wait_ge(sem("s5_scalar"), 1)
                ar, ai = spar[:, 0, :], spar[:, 1, :]
                row = [sc5[:, k, :] for k in range(16)]
                dtb = sc5[:, 0, 0:2].unsqueeze(2).broadcast_to([NT, 2, ST])

                def g(v):
                    return v.rearrange("t (g n) -> t g n", g=2)
                o.step(dve.tensor_tensor(g(row[2]), g(ai), dtb, ALU.mult))
                dve.tensor_tensor(g(row[1]), g(ar), dtb, ALU.mult).then_inc(sem("s5_vector"), 1)
                dve.wait_ge(sem("s5_vector"), 1)
                o.link(dve.tensor_scalar(row[4], row[2], 1.0 / (2 * math.pi), MAGIC, ALU.mult, ALU.add))
                o.link(dve.tensor_scalar(row[4], row[4], MAGIC, None, ALU.subtract))
                cur = row[2]
                for k, part in enumerate(TWO_PI_PARTS):
                    dst = row[12 + k % 2]
                    o.link(dve.scalar_tensor_tensor(out=dst, in0=row[4], scalar=-part, in1=cur, op0=ALU.mult, op1=ALU.add))
                    cur = dst
                o.link(dve.tensor_scalar(row[5], cur, 3.1415925, -3.1415925, ALU.min, ALU.max))
                dve.scalar_tensor_tensor(out=row[6], in0=row[5], scalar=-1.0, in1=row[5], op0=ALU.mult, op1=ALU.max).then_inc(sem("s5_vector"), 1)

            def s5_lambda():
                ar, ai = spar[:, 0, :], spar[:, 1, :]
                row = [sc5[:, k, :] for k in range(16)]
                dve.wait_ge(sem("s5_scalar"), 4)
                o.step(dve.tensor_tensor(row[9], row[3], row[8], ALU.mult))
                o.step(dve.tensor_tensor(row[10], row[3], row[7], ALU.mult))
                o.step(dve.tensor_tensor(row[13], ar, ar, ALU.mult))
                o.link(dve.tensor_tensor(row[14], ai, ai, ALU.mult))
                o.step(dve.tensor_tensor(row[13], row[13], row[14], ALU.add))
                o.link(dve.tensor_scalar(row[15], row[9], -1.0, None, ALU.add))
                o.step(dve.reciprocal(row[13], row[13]))
                o.step(dve.tensor_tensor(row[1], row[15], ar, ALU.mult))
                o.step(dve.tensor_tensor(row[2], row[10], ai, ALU.mult))
                o.step(dve.tensor_tensor(row[4], row[10], ar, ALU.mult))
                o.link(dve.tensor_tensor(row[14], row[15], ai, ALU.mult))
                o.step(dve.tensor_tensor(row[1], row[1], row[2], ALU.add))
                o.link(dve.tensor_tensor(row[4], row[4], row[14], ALU.subtract))
                o.step(dve.tensor_tensor(row[11], row[1], row[13], ALU.mult))
                dve.tensor_tensor(row[12], row[4], row[13], ALU.mult).then_inc(sem("s5_vector"), 1)

            def b_discrete():
                dve.wait_ge(sem("bnat_landed"), 32)
                dve.wait_ge(sem("start_ready"), 1)
                wait_drained(dve, ("s5par",))
                cr = sp5[:, 5, :].unsqueeze(2).broadcast_to([P, NT, 16])
                ci = sp5[:, 6, :].unsqueeze(2).broadcast_to([P, NT, 16])
                br, bi = bnat[:, 0], bnat[:, 1]
                t3 = bmix[:, 0].rearrange("p t h c -> p (t h c)")[:, 0:NT * 16].rearrange("p (t c) -> p t c", c=16)
                o.step(dve.tensor_tensor(bt1[:], br, cr, ALU.mult))
                o.step(dve.tensor_tensor(bt2[:], bi, ci, ALU.mult))
                o.link(dve.tensor_tensor(t3, br, ci, ALU.mult))
                o.link(dve.tensor_tensor(bt1[:], bt1[:], bt2[:], ALU.subtract))
                o.link(dve.tensor_tensor(bt2[:], bi, cr, ALU.mult))
                o.link(dve.tensor_tensor(bt2[:], bt2[:], t3, ALU.add))
                for r, b in enumerate((bt1, bt2)):
                    for h in range(2):
                        ins = dve.tensor_scalar(bmix[:, r, :, h, :], b[:], half[:, h:h + 1], None, ALU.mult)
                        o.step(ins) if (r, h) != (1, 1) else ins.then_inc(sem("bmix_ready"), 1)

            def s5_tiles(hq):
                s = hq % 2
                ur, ui, gr_, gi = uu[:, s, 0], uu[:, s, 1], gg[:, s, 0], gg[:, s, 1]
                br, bi, tr, ti = bu[:, 0], bu[:, 1], tt[:, 0], tt[:, 1]

                def op(out, a, b, how, but=None):
                    if but is not None:
                        o.settle(but)
                    o.step(dve.tensor_tensor(out, a, b, how))

                dve.wait_ge(sem("phases_ready"), hq + 1)
                for t in range(2):
                    wait_drained(dve, ("bu", hq, t))
                o.link(dve.tensor_tensor(bu[:, :, :, NPR:N:NL], bu[:, :, :, NPR:N:NL], a0[:, :, 2 * hq:2 * hq + 2, :], ALU.add))
                op(tr, ur, br, ALU.mult)
                op(ti, ui, bi, ALU.mult)
                if hq >= 2:
                    wait_filled(dve, ("y", hq - 2))
                    dve.wait_ge(sem("last_states"), hq - 1)
                op(gi, ur, bi, ALU.mult)
                op(br, ui, br, ALU.mult, 2)
                op(gr_, tr, ti, ALU.add, 2)
                op(gi, gi, br, ALU.subtract, 1)
                if hq:
                    y_half(hq - 1)
                dve.wait_ge(sem("decay_ready"), 2 * hq + 2)
                for k, (out, g) in enumerate(((tr, gr_), (ti, gi))):
                    o.settle(1)
                    o.step(dve.tensor_tensor_scan(out.rearrange("p t n -> p (t n)"), mm[:].rearrange("p t n -> p (t n)"),
                                                  g.rearrange("p t n -> p (t n)"), 0.0, ALU.mult, ALU.add))
                op(br, ur, tr, ALU.mult, 1)
                op(gi, ur, ti, ALU.mult, 1)
                op(bi, ui, ti, ALU.mult)
                op(tr, ui, tr, ALU.mult, 2)
                op(gr_, br, bi, ALU.subtract, 1)
                o.settle(1)
                dve.tensor_tensor(gi, gi, tr, ALU.add).then_inc(sem("states_ready"), 1)
                dve.wait_ge(sem("states_ready"), hq + 1)

            def y_half(hq):
                c, r = hq // 2, slice(64 * (hq % 2), 64 * (hq % 2) + 64)
                wait_filled(dve, ("y", hq))
                ins = dve.scalar_tensor_tensor(out=yt[r, c, :], in0=yt[r, c, :], scalar=par1[r, D5 + c:D5 + c + 1],
                                               in1=ps(("y", hq))[r, 0, 0:N], op0=ALU.mult, op1=ALU.add)
                drain(ins, ("y", hq))

            def level_mask(c, k):
                n = CHUNKS[c][1]
                m = lvl[0:n, k, 0:n].unsqueeze(1).broadcast_to([n, H, n])
                dve.tensor_tensor(ltm[0:n, :, 0:n], lt[0:n, :, 0:n], m, ALU.mult).then_inc(sem("ltm_ready"), 1)

            def side(key):
                what, a = key[0], key[1:]
                if what == "const":
                    dve.memset(acc[:], 0.0).then_inc(sem("acc_cleared"), 1)
                    dve.wait_ge(sem("acc_cleared"), 1)
                elif what == "x":
                    j = a[0]
                    dve.wait_ge(sem("sq_ready"), j + 1)
                    o.link(dve.tensor_tensor(acc[:], acc[:], sq[:, 0, :], ALU.add))
                    dve.tensor_tensor(acc[:], acc[:], sq[:, 1, :], ALU.add).then_inc(sem("acc_added"), 1)
                    dve.wait_ge(sem("acc_added"), j + 1)
                    lows(xt0, j, j, G_MIX)
                elif what == "norm":
                    norm(0)
                elif what == "s5a":
                    s5_scalars()
                elif what == "s5b":
                    s5_lambda()
                elif what == "bmix":
                    b_discrete()
                    dve.wait_ge(sem("wb_split"), 1)
                    dve.tensor_tensor(wblo[:], wba[:], wbhi[:].bitcast(F32), ALU.subtract).then_inc(sem("wb_split"), 1)
                elif what == "ct":
                    for r in range(2):
                        key = ("ct", r)
                        wait_filled(dve, key)
                        dst = ct[:, r].rearrange("p k (g h c) -> p (k g) h c", h=2, c=16)
                        src = ps(key)[:].rearrange("p k (g h c) -> p (k g) h c", h=2, c=16)
                        for h in range(2):
                            ins = dve.tensor_scalar(dst[:, :, h, :], src[:, :, h, :], half[:, h:h + 1], -1.0 if r else 1.0,
                                                    ALU.mult, ALU.mult)
                            o.step(ins) if h == 0 else drain(ins, key)
                elif what == "ba":
                    o.link(dve.memset(ba[:], 0.0))
                    wait_filled(dve, key)
                    drain(dve.tensor_copy(bafm[:], ps(key)[0:2 * H, 0, 0:N]), key)
                    dve.wait_ge(sem("invt_ready"), 1)
                    key = ("bat",)
                    wait_filled(dve, key)
                    for c in range(3):
                        n = CHUNKS[c][1]
                        ins = dve.tensor_scalar(ba[0:n, c, :], ps(key)[0:n, 0, 16 * c:16 * c + 16], invt[0:n, c:c + 1], None, ALU.mult)
                        o.step(ins) if c < 2 else drain(ins, key)
                    wait_drained(dve, key)
                    dve.wait_ge(sem("gab_landed"), 32)
                    av = ba[:, :, H:2 * H]
                    o.link(dve.tensor_tensor(av, av, gab[:, H:2 * H].unsqueeze(1).broadcast_to([P, 3, H]), ALU.add))
                    dve.scalar_tensor_tensor(out=sp3[:], in0=av, scalar=-1.0, in1=av, op0=ALU.mult, op1=ALU.max).then_inc(sem("ba_vector"), 1)
                    dve.wait_ge(sem("ba_scalar"), 3)
                    o.link(dve.scalar_tensor_tensor(out=sp3[:], in0=av, scalar=0.0, in1=sp3[:], op0=ALU.max, op1=ALU.add))
                    dve.scalar_tensor_tensor(out=gt[:], in0=sp3[:], scalar=-1.0, in1=gab[:, 0:H].unsqueeze(1).broadcast_to([P, 3, H]),
                                             op0=ALU.mult, op1=ALU.mult).then_inc(sem("g_ready"), 1)
                    dve.wait_ge(sem("x_stored"), 16)
                    wait_drained(dve, ("cst",))
                    o.step(dve.memset(qkv[:, :, 0:CW - 1], 0.0))
                    dst = qkv[:, :, SEQP:NPAD].rearrange("p t (b l) -> p t b l", l=SEQS)[:, :, :, 0:CW - 1]
                    dve.tensor_copy(dst, cstt[:].rearrange("p t (b j) -> p t b j", j=CW - 1)).then_inc(sem("pads_done"), 1)
                    dve.wait_ge(sem("pads_done"), 1)
                elif what == "s5":
                    s5_tiles(a[0])
                elif what == "s5y":
                    y_half(NT // 2 - 1)
                elif what == "tailc":
                    dve.wait_ge(evacuated, pair_of["qkv", 11] + 1)
                    wait_filled(dve, ("y", NT // 2 - 1))
                    dve.wait_ge(sem("last_states"), NT // 2)
                    o.settle()
                    o.step(dve.tensor_copy(tail[:, :, 0:3], qkv[:, :, SEQP - 3:SEQP]))
                    src = qkv[:, :, SEQP:NPAD].rearrange("p t (b l) -> p t b l", l=SEQS)[:, :, :, NL:SEQS]
                    dve.tensor_copy(tail[:, :, 3:27].rearrange("p t (b j) -> p t b j", j=3), src).then_inc(sem("tails_ready"), 1)
                elif what == "conv":
                    h = a[0]
                    if h == 0:
                        dve.wait_ge(sem("tails_ready"), 1)
                    dve.wait_ge(sem("taps_ready"), 3 * (h + 1))
                    for j in range(1, CW):
                        for g in range(3):
                            t, s = h + H * g, cacc[:, h % 2, g, 0:NCV]
                            w = par2[:, j * KC + t:j * KC + t + 1]
                            ins = dve.scalar_tensor_tensor(out=s, in0=qkv[:, t, j:j + NCV], scalar=w, in1=s,
                                                           op0=ALU.mult, op1=ALU.add)
                            o.step(ins) if j < CW - 1 else ins.then_inc(sem("conv_ready"), 1)
                        o.settle()
                elif what == "l2e":
                    dst, t0 = ((qt, 0), (kt, H))[a[0]]
                    for k in range(2):
                        t, src = slice(4 * k, 4 * k + 4), slice(t0 + 4 * k, t0 + 4 * k + 4)
                        dve.wait_ge(sem("norms_ready"), 2 * a[0] + k + 1)
                        o.step(dve.tensor_tensor(dst[:, t, 0:NPR], dst[:, t, 0:NPR], qkv[:, src, 0:NPR], ALU.mult))
                        v = dst[:, t, NPR:N].rearrange("p t (b l) -> p t b l", l=NL)
                        x = qkv[:, src, SEQP:NPAD].rearrange("p t (b l) -> p t b l", l=SEQS)[:, :, :, 0:NL]
                        dve.tensor_tensor(v, v, x, ALU.mult).then_inc(sem("qk_normed"), 1)
                elif what == "dg":
                    c = a[0]
                    dve.wait_ge(sem("masks_ready"), 1)
                    c0, n = CHUNKS[c]
                    wait_filled(dve, ("gcum", c))
                    drain(dve.tensor_copy(gc[0:n, c, :], ps(("gcum", c))[0:n, 0, 0:H]), ("gcum", c))
                    wait_drained(dve, ("gcum", c))
                    wait_filled(dve, ("grow", c))
                    if c:
                        wait_drained(dve, ("qk", c - 1))
                    for h in range(H):
                        dve.tensor_scalar(dt_[0:n, h, 0:n], ps(("grow", c))[0:n, h // 4, (h % 4) * n:(h % 4) * n + n],
                                          gc[0:n, c, h:h + 1], 0.0, ALU.subtract, ALU.min).then_inc(sem("gdiff_ready"), 1)
                    wait_filled(dve, ("brow", c))
                    if c:
                        wait_drained(dve, ("tb", c - 1, LEVELS[c - 1] - 1))
                    drain(dve.tensor_tensor(hsplit(kb[:, :, 0:n]), hsplit(kt[:, :, c0:c0 + n]), hview(("brow", c), c), ALU.mult),
                          ("brow", c))
                    dve.wait_ge(sem("decay_exp"), 2 * (c + 1))
                    m = (cum if c < 2 else cums)[0:n, 0:n].unsqueeze(1).broadcast_to([n, H, n])
                    o.link(dve.tensor_tensor(dt_[0:n, :, 0:n], dt_[0:n, :, 0:n], m, ALU.mult))
                    o.step(dve.scalar_tensor_tensor(out=nbe[0:n, c, :], in0=egc[0:n, :], scalar=-1.0, in1=bet[0:n, c, :],
                                                    op0=ALU.mult, op1=ALU.mult))
                    if c < 2:
                        o.step(dve.tensor_copy(dl[0:n, :], dt_[0:n, :, n - 1]))
                        o.step(dve.tensor_copy(egl[:, :, 0], eg[:, :, n - 1]))
                    else:
                        o.step(dve.tensor_reduce(dl[0:n, :], dt_[0:n, :, NL - 1:n:NL], AX.X, ALU.add))
                        o.step(dve.tensor_copy(egl[:], eg[:, :, NL - 1:n:NL]))
                    o.settle()
                elif what == "dkk":
                    c = a[0]
                    c0, n = CHUNKS[c]
                    wait_filled(dve, ("kk", c))
                    drain(dve.tensor_tensor(hsplit(lt[0:n, :, 0:n]), hview(("kk", c), c, rows=n), hsplit(dt_[0:n, :, 0:n]), ALU.mult), ("kk", c))
                    wait_filled(dve, ("qk", c))
                    if c:
                        wait_drained(dve, ("o", c - 1))
                    drain(dve.tensor_tensor(hsplit(qkd[0:n, :, 0:n]), hview(("qk", c), c, rows=n), hsplit(dt_[0:n, :, 0:n]), ALU.mult), ("qk", c))
                    if c < 2:
                        out, gv, qv = eg[:, :, 0:n], eg[:, :, 0:n], qt[:, :, c0:c0 + n]
                    else:
                        out = kq[:].rearrange("p h b (s l) -> p h b s l", s=2)[:, :, :, 1, :]
                        gv, qv = (x.rearrange("p h (b l) -> p h b l", l=NL) for x in (eg[:, :, 0:n], qt[:, :, c0:c0 + n]))
                    dve.tensor_tensor(out, gv, qv, ALU.mult).then_inc(sem("qg_ready"), 1)
                    wait_drained(dve, ("kt", c))
                    dve.tensor_tensor(ktok[0:n], ktok[0:n], dl[0:n, :].unsqueeze(2).broadcast_to([n, H, P]), ALU.mult).then_inc(sem("kd_ready"), 1)
                    dve.wait_ge(sem("lt_ready"), c + 1)
                    level_mask(c, 0)
                elif what == "m1" and a[1] == 0:
                    c = a[0]
                    n = CHUNKS[c][1]
                    wait_filled(dve, key)
                    dve.wait_ge(sem("t_started"), c + 1)
                    o.step(dve.tensor_tensor(tmt[0:n, :, 0:n], tmt[0:n, :, 0:n], ltm[0:n, :, 0:n], ALU.subtract))
                    drain(dve.tensor_tensor(hsplit(tm[0:n, :, 0:n]), hsplit(tm[0:n, :, 0:n]), hview(key, c, rows=n), ALU.subtract), key)
                    o.settle()
                    level_mask(c, 1)
                elif what == "tab":
                    c, k = a
                    n = CHUNKS[c][1]
                    if k + 1 < LEVELS[c]:
                        wait_filled(dve, ("m1", c, k))
                        level_mask(c, k + 1)
                    for nm, t in (("ta", tm), ("tb", tmt)):
                        if nm == "ta" and k == LEVELS[c] - 1:
                            continue
                        kk = (nm, c, k)
                        wait_filled(dve, kk)
                        drain(dve.tensor_tensor(hsplit(t[0:n, :, 0:n]), hsplit(t[0:n, :, 0:n]), hview(kk, c, rows=n), ALU.subtract), kk)
                elif what == "ks":
                    c = a[0]
                    n = CHUNKS[c][1]
                    wait_filled(dve, key)
                    for h in range(H):
                        ins = dve.scalar_tensor_tensor(out=vb[0:n, h, :], in0=ps(key)[0:n, h // 4, (h % 4) * P:(h % 4 + 1) * P],
                                                       scalar=nbe[0:n, c, h:h + 1], in1=vb[0:n, h, :], op0=ALU.mult, op1=ALU.add)
                        o.step(ins) if h < H - 1 else drain(ins, key)
                elif what == "o" and a[0] == 2:
                    wait_filled(dve, key)
                    v = sqt[:].rearrange("p h (k c) -> p h k c", k=2)[:, :, 1, :]
                    drain(dve.tensor_tensor(hsplit(qt[:, :, NPR:N]), hview(key, 2), hsplit(v), ALU.add), key)
                elif what == "s":
                    c = a[0]
                    wait_filled(dve, key)
                    if c == 0:
                        drain(dve.tensor_copy(hsplit(s_[:]), ps(key)[:].rearrange("p k (h e) -> p k h e", h=4)), key)
                    else:
                        for h in range(H):
                            ins = dve.scalar_tensor_tensor(out=s_[:, h, :], in0=s_[:, h, :], scalar=egl[:, h, 0:1],
                                                           in1=ps(key)[:, h // 4, (h % 4) * P:(h % 4 + 1) * P], op0=ALU.mult, op1=ALU.add)
                            o.step(ins) if h < H - 1 else drain(ins, key)
                elif what == "su":
                    i = a[0]
                    h, st = (i + 4) % H, st_ring[i % 4]
                    dve.wait_ge(sem(f"st_landed_{i % 4}"), 16 * (2 if i < 4 else 3))
                    o.link(dve.tensor_tensor(st[:], st[:], egl[:, h, :].unsqueeze(2).broadcast_to([P, NB, P]), ALU.mult))
                    wait_filled(dve, key)
                    drain(dve.tensor_tensor(hsplit(st[:]), hsplit(st[:]), ps(key)[:].rearrange("p k (b e) -> p k b e", b=4), ALU.add), key)
                elif what == "ysplit":
                    for k in range(0, K5, UK):
                        t = slice(k, k + UK)
                        dve.wait_ge(sem("yhi_ready"), k // UK + 1)
                        dve.tensor_tensor(ylo[:, t, :], yt[:, t, :], yhi[:, t, :].bitcast(F32), ALU.subtract).then_inc(sem("ylo_ready"), 1)
                elif what == "on":
                    j = a[0]
                    wait_drained(dve, key)
                    for m in range(2):
                        o.step(dve.scalar_tensor_tensor(out=t1[:, m, :], in0=qt[:, 2 * j + m, :], scalar=par1[:, ONW:ONW + 1],
                                                        in1=g1[:, m, :], op0=ALU.mult, op1=ALU.mult))
                    z = stored_gate("on", j)
                    o.settle()
                    o.link(dve.tensor_tensor(t1[:], t1[:], z, ALU.mult))
                    t = slice(2 * j, 2 * j + 2)
                    o.link(dve.tensor_copy(dhi[:, t, :], t1[:]))
                    dve.tensor_tensor(dlo[:, t, :], t1[:], dhi[:, t, :].bitcast(F32), ALU.subtract).then_inc(sem("on_ready"), 1)
                    dve.wait_ge(sem("on_ready"), j + 1)

            prev = None
            for sides, us in slots:
                for n in [units.index(u) for u in us]:
                    p, j = units[n]
                    nk, last = min(UK, pairs[p][2] - UK * j), pair_units[p] - 1
                    if j == last and last >= 3 and prev is not None:
                        evac(prev)
                    split_lo(n, n % RING, nk)
                    if j == 0 and p >= 2 and pairs[p - 2][0:2] != ("glu", 3):
                        late(p - 2)
                    if j == last:
                        if last < 3 and prev is not None:
                            evac(prev)
                            if pairs[prev][0:2] == ("glu", 3):
                                late(prev)
                        prev = p
                for key in sides:
                    side(key)

            def add_x(gp, par, j):
                xs = xt[:, bass.ds(j * 2, 2), :]
                dve.tensor_tensor(xs, xs, pg[:, par, :, 0:N], ALU.add).then_inc(evacuated, 1)

            def splits(u0, js, nk=lambda j: UK):
                for j in js:
                    split_lo(u0 + j, j % RING, nk(j))

            splits(OUT_U, range(3))
            evac(prev)
            splits(OUT_U, [3])
            dve.wait_ge(sem("xt_landed"), 16)
            splits(OUT_U + 4, range(3))
            dve.wait_ge(multiplied, OUT_U + 4)
            add_x(OUT_P, 0, 0)
            splits(OUT_U + 4, [3])
            with dve.Fori(0, 3) as it:
                for b in range(2):
                    split_lo(OUT_U + 8 + 4 * b + it * 8, 0, UK)
                    lows(xt, it * 2 + (8 + b), it * 2 + b, G_FFN)
                    split_lo(OUT_U + 9 + 4 * b + it * 8, 1, UK)
                    split_lo(OUT_U + 10 + 4 * b + it * 8, 2, UK)
                    dve.wait_ge(multiplied, OUT_U + 8 + 4 * b + it * 8)
                    add_x(None, 1 - b, it * 2 + (1 + b))
                    split_lo(OUT_U + 11 + 4 * b + it * 8, 3, UK)

            HF = KFC // 2
            both_inv = both(inv)

            def gate_out(k):
                dve.wait_ge(multiplied, k)
                dve.tensor_tensor(fg1[:], pg[:, 0, :, 0:N], both_inv, ALU.mult).then_inc(evacuated, 1)

            def up_out(k, n):
                dve.wait_ge(multiplied, k)
                dve.wait_ge(sem("fsi_ready"), n)
                dve.tensor_tensor(fmd[:], pg[:, 1, :, 0:N], fsi[:], ALU.mult).then_inc(evacuated, 1)

            def hidden_lo(n, i):
                dve.wait_ge(sem("mhi_ready"), n)
                dve.tensor_tensor(mlo[:, bass.ds(i * 2, 2), :], fmd[:], mhi[:, bass.ds(i * 2, 2), :].bitcast(F32),
                                  ALU.subtract).then_inc(sem("mlo_ready"), 1)

            nk_down = lambda j: min(UK, KFC - UK * (j % DU))
            for c in range(FCH):
                U, n0 = FFN_U[c], c * HF
                if c == 0:
                    split_lo(U, 0, UK)
                    lows(xt, 14, 6, G_FFN)
                    splits(U, [1, 2])
                    dve.wait_ge(multiplied, OUT_U + 32)
                    add_x(None, 1, 7)
                    splits(U, [3])
                    split_lo(U + 4, 0, UK)
                    lows(xt, 15, 7, G_FFN)
                    splits(U + 4, [1, 2])
                    norm(1)
                else:
                    splits(U, range(3))
                    dve.wait_ge(multiplied, U)
                    add_x(None, 1, 7)
                    splits(U, [3])
                    splits(U + 4, range(3))
                gate_out(U + 4)
                splits(U + 4, [3])
                with dve.Fori(0, HF - 1) as it:
                    k = it * 8
                    split_lo(k + (U + 8), 0, UK)
                    split_lo(k + (U + 9), 1, UK)
                    split_lo(k + (U + 10), 2, UK)
                    up_out(k + (U + 8), it + (n0 + 1))
                    split_lo(k + (U + 11), 3, UK)
                    split_lo(k + (U + 12), 0, UK)
                    hidden_lo(it + (n0 + 1), it)
                    split_lo(k + (U + 13), 1, UK)
                    split_lo(k + (U + 14), 2, UK)
                    gate_out(k + (U + 12))
                    split_lo(k + (U + 15), 3, UK)
                W = DOWN_U[c]
                splits(W, range(3))
                up_out(W, n0 + HF)
                splits(W, [3])
                hidden_lo(n0 + HF, HF - 1)
                splits(W, range(4, DU), nk_down)
                if c == 0:
                    wait_filled(dve, ("pt",))
                    drain(dve.tensor_copy(pf[:], ps(("pt",))[:, :, 0:N]), ("pt",))
                    wait_drained(dve, ("pt",))

                def down_pair(it, b):
                    for j in range(DU):
                        jj = DU + b * DU + j
                        if c == FCH - 1 and j == 1 and b == 1:
                            lows(xt, it * 2 + 16, it * 2, G_PLE)
                        if j == 3:
                            dve.wait_ge(multiplied, it * (2 * DU) + (W + DU + b * DU))
                            add_x(None, b, it * 2 + b)
                        split_lo(it * (2 * DU) + (W + jj), jj % RING, nk_down(j))

                with dve.Fori(0, 3) as it:
                    down_pair(it, 0)
                    down_pair(it, 1)
                    if c == FCH - 1:
                        lows(xt, it * 2 + 17, it * 2 + 1, G_PLE)
                for j in range(DU):
                    jj = 7 * DU + j
                    if j == 3:
                        dve.wait_ge(multiplied, W + 7 * DU)
                        add_x(None, 0, 6)
                    split_lo(W + jj, jj % RING, nk_down(j))

            def ple_gate_out(i):
                dve.wait_ge(multiplied, PLE_U + 5 * i + 4)
                dve.tensor_tensor(fg1[:], pg[:, i % 2, :, 0:N], both_inv, ALU.mult).then_inc(evacuated, 1)

            def ple_out(i):
                key = ("emb", i)
                dve.wait_ge(multiplied, PLE_U + 5 * i + 5)
                dve.wait_ge(sem("psig_ready"), i + 1)
                o.settle()
                drain(dve.tensor_tensor(fmd[:], ps(key)[:, :, 0:N], fsg[:], ALU.mult), key)
                wait_drained(dve, key)
                xs = xt[:, 2 * i:2 * i + 2, :]
                dve.tensor_tensor(xs, xs, fmd[:], ALU.add).then_inc(sem("xf_ready"), 1)
                dve.wait_ge(sem("xf_ready"), i + 1)

            dve.wait_ge(sem("phi_ready"), 1)
            dve.tensor_tensor(plo[:], pf[:], phi[:].bitcast(F32), ALU.subtract).then_inc(sem("plo_ready"), 1)
            for i in range(8):
                u = PLE_U + 5 * i

                def s(j):
                    split_lo(u + j, (5 * i + j) % RING, UK if j < 4 else 2)
                s(0)
                if i == 0:
                    lows(xt, 22, 6, G_PLE)
                s(1)
                s(2) if i == 0 else None
                if i == 0:
                    dve.wait_ge(multiplied, PLE_U)
                    add_x(None, 1, 7)
                    s(3)
                    lows(xt, 23, 7, G_PLE)
                    s(4)
                else:
                    if i == 1:
                        norm(2)
                    ple_gate_out(i - 1)
                    s(2)
                    ple_out(i - 1)
                    s(3)
                    s(4)
            ple_gate_out(7)
            ple_out(7)
            dve.wait_ge(sem("invt_ready"), 2)
            for t in range(3):
                n = CHUNKS[t][1]
                key = ("fin", 2 * t + 1)
                wait_filled(dve, key)
                if t == 2:
                    dve.wait_ge(sem("y_stored_0"), 16)
                drain(dve.tensor_scalar(yo[0:n, t % 2, 1024:2048].rearrange("p (k c) -> p k c", k=2), ps(key)[0:n],
                                        invt[0:n, t:t + 1], None, ALU.mult), key)

        @block.tensor
        def _(pe):
            def begin(key):
                r, i, _ = fill_at[key]
                if i:
                    pe.wait_ge(drained[r], i)
                return ps(key)

            def end(ins, key):
                ins.then_inc(filled[fill_at[key][0]], 1)

            def unit(u, r, par, k0, nk, first, last, hi, lo, out=None):
                out = pg[:, par] if out is None else out
                pe.wait_ge(w_lo, u + 1)
                for m in range(2):
                    for k in range(nk):
                        wh, wl = whi[:, r, k, m * P:(m + 1) * P], wlo[:, r, k, m * P:(m + 1) * P]
                        a_hi, a_lo = hi[:, k0 + k, :], lo[:, k0 + k, :]
                        for part, (w, a) in enumerate(((wh, a_hi), (wh, a_lo), (wl, a_hi))):
                            ins = pe.matmul(out[:, m, 0:N], w, a, start=first and k == 0 and part == 0,
                                            stop=last and k == nk - 1 and part == 2)
                ins.then_inc(multiplied, 1)

            def token_transposes(out, cols, src):
                for c, (c0, n) in enumerate(CHUNKS):
                    ins = pe.transpose(out[:, c0:c0 + n], src[0:n, c, cols], ident[0:n, 0:n])
                return ins

            def norm(i):
                pe.wait_ge(sem("acc_added"), 8 * (i + 1))
                key = ("norm", i)
                out = begin(key)
                if i < 3:
                    ins = pe.matmul(out[:, 0, 0:N], ones[:], acc[:], start=True, stop=True)
                if i in (0, 3):
                    for c, (c0, n) in enumerate(CHUNKS):
                        ins = pe.matmul(out[0:n, 1, c:c + 1], acc[:, c0:c0 + n], ones[:, 0:1], start=True, stop=True)
                end(ins, key)

            def per_head(key, n, lhs, rhs, rows=None):
                out = begin(key)
                for h in range(H):
                    ins = pe.matmul(out[0:rows or P, h // 4, (h % 4) * n:(h % 4) * n + n], lhs(h), rhs(h), start=True, stop=True)
                end(ins, key)

            def side(key):
                what, a = key[0], key[1:]
                if what == "par":
                    pe.wait_ge(sem("par_landed"), 16 * 8)
                    pe.wait_ge(sem("ident_ready"), 1)
                    out = begin(key)
                    pe.transpose(out[:, 0, 0:81], par1n[:], ident[0:81, 0:81])
                    end(pe.transpose(out[:, 1, 0:CW * KC], par2n[:], ident[0:CW * KC, 0:CW * KC]), key)
                    pe.wait_ge(sem("csn_landed"), 16)
                    key = ("cst",)
                    out = begin(key)
                    for t in range(KC):
                        c = (t % 12) * 3 * NB
                        ins = pe.transpose(out[:, t // 12, c:c + 3 * NB], csn[:, t * P:(t + 1) * P], ident[0:3 * NB, 0:3 * NB])
                    end(ins, key)
                elif what == "x":
                    if a[0] == 0:
                        pe.wait_ge(sem("x_landed"), 48)
                    out = begin(key)
                    for m in range(2):
                        t = 2 * a[0] + m
                        ins = token_transposes(out[:, m], slice(t * P, (t + 1) * P), xtok)
                    end(ins, key)
                elif what == "norm":
                    norm(0)
                elif what == "s5par":
                    pe.wait_ge(sem("s5_vector"), 3)
                    out = begin(key)
                    for i, k in enumerate((3, 8, 7, 9, 10, 11, 12)):
                        ins = pe.transpose(out[:, 0, i * NT:(i + 1) * NT], sc5[:, k, :], ident[0:NT, 0:NT])
                    end(ins, key)
                elif what == "h0":
                    pe.wait_ge(sem("h0_landed"), 32)
                    out = begin(key)
                    for r in range(2):
                        for k in range(2):
                            ins = pe.transpose(out[:, r, k * P:(k + 1) * P], h0n[:, r, k, :], ident[:])
                    end(ins, key)
                elif what == "bb":
                    pe.wait_ge(sem("bmix_ready"), 1)
                    for r in range(2):
                        key = ("bbt", r)
                        out = begin(key)
                        for k in range(K5):
                            ins = pe.transpose(out[:, k // 4, (k % 4) * P:(k % 4 + 1) * P],
                                               bmix[:, r, 4 * k:4 * k + 4].rearrange("p t h c -> p (t h c)"), ident[:])
                        end(ins, key)
                elif what == "ct":
                    pe.wait_ge(sem("cnat_landed"), 64)
                    for r in range(2):
                        key = ("ct", r)
                        out = begin(key)
                        for k in range(K5):
                            ins = pe.transpose(out[:, k // 4, (k % 4) * P:(k % 4 + 1) * P],
                                               cnat[:, r, k].rearrange("p h n -> p (h n)"), ident[:])
                        end(ins, key)
                elif what == "ba":
                    pe.wait_ge(sem("wb_split"), 2)
                    pe.wait_ge(sem("xlo_ready"), KD)
                    out = begin(key)
                    for k in range(KD):
                        for part, (w, x) in enumerate(((wbhi, xhi), (wbhi, xlo), (wblo, xhi))):
                            ins = pe.matmul(out[0:2 * H, 0, 0:N], w[:, k, :], x[:, k, :], start=k == 0 and part == 0,
                                            stop=k == KD - 1 and part == 2)
                    end(ins, key)
                    wait_drained(pe, key)
                    key = ("bat",)
                    out = begin(key)
                    for c, (c0, n) in enumerate(CHUNKS):
                        ins = pe.transpose(out[0:n, 0, 16 * c:16 * c + 16], bafm[:, c0:c0 + n], ident[0:2 * H, 0:2 * H])
                    end(ins, key)
                elif what == "s5" and a[0]:
                    readout(a[0] - 1)
                elif what == "s5y":
                    readout(NT // 2 - 1)
                elif what == "s5out":
                    pe.wait_ge(sem("last_states"), NT // 2)
                    key = ("hl",)
                    out = begin(key)
                    for r in range(2):
                        pe.transpose(out[0:NT, r, 0:P], hl[:, r, 0, :], ident[:])
                        for k in range(2):
                            ins = pe.transpose(out[:, r, (k + 1) * P:(k + 2) * P],
                                               hl[:, r, 1 + 4 * k:5 + 4 * k, :].rearrange("p b t -> p (b t)"), ident[:])
                    end(ins, key)
                elif what == "tail":
                    pe.wait_ge(sem("tails_ready"), 1)
                    for j in range(3):
                        key = ("tail", j)
                        out = begin(key)
                        for t in range(8):
                            ins = pe.transpose(out[0:27, t // 4, (t % 4) * P:(t % 4 + 1) * P], tail[:, 8 * j + t, :], ident[:])
                        end(ins, key)
                elif what == "l2":
                    j = a[0]
                    pe.wait_ge(sem("l2sq_ready"), j + 1)
                    out = begin(key)
                    for m in range(2):
                        ins = pe.matmul(out[:, m, 0:NCV], ones[:], sql[:, m, 0:NCV], start=True, stop=True)
                    end(ins, key)
                elif what == "dg":
                    c = a[0]
                    n = CHUNKS[c][1]
                    tri = (cum if c < 2 else cums)[0:n, 0:n]
                    pe.wait_ge(sem("g_ready"), 1)
                    pe.wait_ge(sem("masks_ready"), 1)
                    key = ("gcum", c)
                    end(pe.matmul(begin(key)[0:n, 0, 0:H], tri, gt[0:n, c, :], start=True, stop=True), key)
                    per_head(("grow", c), n, lambda h: gt[0:n, c, h:h + 1].to_broadcast([n, P]), lambda h: tri)
                    per_head(("brow", c), n, lambda h: bet[0:n, c, h:h + 1].to_broadcast([n, P]), lambda h: ident[0:n, 0:n])
                elif what == "dkv":
                    c = a[0]
                    c0, n = CHUNKS[c]
                    pe.wait_ge(sem("qk_normed"), 4)
                    pe.wait_ge(sem("vsm_ready"), 1)
                    for nm in ("kt", "vt"):
                        key = (nm, c)
                        out = begin(key)
                        for h in range(H):
                            if nm == "kt":
                                src = kt[:, h, c0:c0 + n]
                            elif c < 2:
                                src = qkv[:, 2 * H + h, c0:c0 + n]
                            else:
                                src = vsm[:, h, :]
                            ins = pe.transpose(out[0:n, h // 4, (h % 4) * P:(h % 4 + 1) * P], src, ident[:])
                        end(ins, key)
                elif what == "dkk":
                    c = a[0]
                    c0, n = CHUNKS[c]
                    wait_drained(pe, ("brow", c))
                    per_head(("kk", c), n, lambda h: kt[:, h, c0:c0 + n], lambda h: kb[:, h, 0:n], n)
                    per_head(("qk", c), n, lambda h: kt[:, h, c0:c0 + n], lambda h: qt[:, h, c0:c0 + n], n)
                elif what == "m1":
                    c, k = a
                    n = CHUNKS[c][1]
                    pe.wait_ge(sem("ltm_ready"), sum(LEVELS[:c]) + k + 1)
                    if k > 1:
                        wait_drained(pe, ("ta", c, k - 1))
                    elif k == 1:
                        wait_drained(pe, ("m1", c, 0))
                    else:
                        pe.wait_ge(sem("t_started"), c + 1)
                    per_head(key, n, lambda h: ltm[0:n, h, 0:n], lambda h: tm[0:n, h, 0:n], n)
                elif what == "tab":
                    c, k = a
                    n = CHUNKS[c][1]
                    wait_drained(pe, ("m1", c, k))
                    if k > 1:
                        wait_drained(pe, ("tb", c, k - 1))
                    if k < LEVELS[c] - 1:
                        per_head(("ta", c, k), n, lambda h: tmt[0:n, h, 0:n], lambda h: m1[0:n, h, 0:n], n)
                    per_head(("tb", c, k), n, lambda h: m1[0:n, h, 0:n], lambda h: tmt[0:n, h, 0:n], n)
                elif what == "sq":
                    h = a[0]
                    pe.wait_ge(sem("qg_ready"), 3)
                    pe.wait_ge(sem("lt_ready"), 3)
                    pe.wait_ge(sem(f"st_landed_{h % 4}"), 16 * (h // 4 + 1))
                    out, st = begin(key), st_ring[h % 4]
                    for b in range(NB):
                        ins = pe.matmul(out[:, 0, b * 2 * NL:(b + 1) * 2 * NL], st[:, b, :], kq[:, h, b, :], start=True, stop=True)
                    end(ins, key)
                elif what == "ks":
                    c = a[0]
                    c0, n = CHUNKS[c]
                    if c == 1:
                        wait_drained(pe, ("s", 0))
                        out = begin(key)
                        for h in range(H):
                            ins = pe.matmul(out[0:n, h // 4, (h % 4) * P:(h % 4 + 1) * P], kt[:, h, c0:c0 + n], s_[:, h, :], start=True, stop=True)
                        end(ins, key)
                    else:
                        wait_drained(pe, ("sq", H - 1))
                        wait_drained(pe, ("sq", H - 2))
                        out = begin(key)
                        for h in range(H):
                            ins = pe.transpose(out[0:n, h // 4, (h % 4) * P:(h % 4 + 1) * P], sqt[:, h, 0:NSM], ident[:])
                        end(ins, key)
                elif what == "vn":
                    c = a[0]
                    n = CHUNKS[c][1]
                    wait_drained(pe, ("tb", c, LEVELS[c] - 1))
                    wait_drained(pe, ("vt", c))
                    if c:
                        wait_drained(pe, ("ks", c))
                    per_head(key, P, lambda h: tmt[0:n, h, 0:n], lambda h: vb[0:n, h, :], n)
                elif what == "o":
                    c = a[0]
                    n = CHUNKS[c][1]
                    wait_drained(pe, ("vn", c))
                    wait_drained(pe, ("qk", c))
                    pe.wait_ge(sem("qg_ready"), c + 1)
                    out = begin(key)
                    for h in range(H):
                        cols = slice((h % 4) * n, (h % 4) * n + n)
                        ins = pe.matmul(out[:, h // 4, cols], vn[0:n, h, :], qkd[0:n, h, 0:n], start=True, stop=c != 1)
                        if c == 1:
                            ins = pe.matmul(out[:, h // 4, cols], s_[:, h, :], eg[:, h, 0:n], start=False, stop=True)
                    end(ins, key)
                elif what == "s":
                    c = a[0]
                    pe.wait_ge(sem("kd_ready"), c + 1)
                    n = CHUNKS[c][1]
                    per_head(key, P, lambda h: ktok[0:n, h, :], lambda h: vn[0:n, h, :])
                elif what == "su":
                    i = a[0]
                    pe.wait_ge(sem("kd_ready"), 3)
                    pe.wait_ge(sem("vnb_ready"), i + 1)
                    out = begin(key)
                    for k in range(2):
                        ins = pe.matmul(out[:, k, :], ktok[0:NSM, (i + 4) % H, :],
                                        vnb[:, i % 2, 4 * k:4 * k + 4, :].rearrange("j b e -> j (b e)"), start=True, stop=True)
                    end(ins, key)
                elif what == "on":
                    j = a[0]
                    pe.wait_ge(sem("osq_ready"), j + 1)
                    out = begin(key)
                    for m in range(2):
                        ins = pe.matmul(out[:, m, 0:N], ones[:], sq[:, m, :], start=True, stop=True)
                    end(ins, key)

            def drive(hq):
                pe.wait_ge(evacuated, hq // 4 + 1)
                for t in range(2):
                    key = ("bu", hq, t)
                    c, q = (2 * hq + t) // 4, (2 * hq + t) % 4
                    rows = slice(32 * q, 32 * q + 32)
                    out = begin(key)
                    for r in range(2):
                        ins = pe.matmul(out[:, r, 0:N], bbt[rows, r, c, :], yt[rows, c, :], start=True, stop=True)
                    end(ins, key)

            def readout(hq):
                key = ("y", hq)
                pe.wait_ge(sem("states_ready"), hq + 1)
                if hq == 0:
                    wait_drained(pe, ("ct", 1))
                out = begin(key)
                for t in range(2):
                    c, q = (2 * hq + t) // 4, (2 * hq + t) % 4
                    for r in range(2):
                        ins = pe.matmul(out[32 * q:32 * q + 32, 0, 0:N], ct[:, r, c, 32 * q:32 * q + 32], gg[:, hq % 2, r, t, :],
                                        start=r == 0, stop=r == 1)
                end(ins, key)

            operands = {"u": (xhi, xlo), "qkv": (xhi, xlo), "z": (xhi, xlo), "gate": (xhi, xlo), "glu": (yhi, ylo),
                        "wa": (ghi, glo), "wb": (dhi, dlo)}
            for s, (sides, us) in enumerate(slots):
                for key in sides:
                    side(key)
                for n in [units.index(u) for u in us]:
                    if units[n] == us[-1] and s + 1 < len(slots) and slots[s + 1][0] and slots[s + 1][0][0][0] == "s5":
                        drive(slots[s + 1][0][0][1])
                    p, j = units[n]
                    kind, i, kts = pairs[p]
                    nk = min(UK, kts - UK * j)
                    if j == 0 and p >= 2:
                        pe.wait_ge(evacuated, p - 1)
                    if p == 0:
                        pe.wait_ge(sem("xlo_ready"), UK * (j + 1))
                    if kind == "glu" and i == 0:
                        pe.wait_ge(sem("ylo_ready"), j + 1)
                    if kind == "wa" and i == 0:
                        pe.wait_ge(sem("glu_done"), 2 * (j + 1))
                    if kind == "wb" and i == 0:
                        pe.wait_ge(sem("on_ready"), 2 * (j + 1))
                    unit(n, n % RING, p % 2, UK * j, nk, j == 0, j == pair_units[p] - 1, *operands[kind])

            def pair(u0, p0, du, kts, hi, lo, par, ready=None):
                pe.wait_ge(evacuated, p0 - 1)
                nu = -(-kts // UK)
                for j in range(nu):
                    if ready is not None:
                        ready(j)
                    jj = du + j
                    unit(u0 + j, jj % RING, par, UK * j, min(UK, kts - UK * j), j == 0, j == nu - 1, hi, lo)

            def out_pair(it, b, ready=None):
                pair(it * 8 + (OUT_U + 4 * b), it * 2 + (OUT_P + b), 4 * b, KD, mxhi, mxlo, b, ready)

            out_pair(0, 0, lambda j: pe.wait_ge(sem("mix_ready"), 2 * (j + 1)))
            out_pair(0, 1)
            with pe.Fori(1, 4) as it:
                out_pair(it, 0)
                out_pair(it, 1)
            for c in range(FCH):
                def gate_up(it, b, ready=None):
                    pair(it * 8 + (FFN_U[c] + 4 * b), it * 2 + (FFN_P[c] + b), 4 * b, KD, xhi, xlo, b, ready)

                def ffn_in(j):
                    pe.wait_ge(sem("xlo_ready"), KD + 4 * (j + 1))
                gate_up(0, 0, ffn_in if c == 0 else None)
                if c == 0:
                    norm(1)
                gate_up(0, 1)
                with pe.Fori(1, KFC // 2) as it:
                    gate_up(it, 0)
                    gate_up(it, 1)

                def down(it, b, ready=None):
                    pair(it * (2 * DU) + (DOWN_U[c] + DU * b), it * 2 + (DOWN_P[c] + b), DU * b, KFC, mhi, mlo, b, ready)
                down(0, 0, lambda j: pe.wait_ge(sem("mlo_ready"), c * (KFC // 2) + min(2 * (j + 1), KFC // 2)))
                if c == 0:
                    pe.wait_ge(sem("p_landed"), 48)
                    key = ("pt",)
                    out = begin(key)
                    for m in range(2):
                        ins = token_transposes(out[:, m], slice(m * P, (m + 1) * P), ptok)
                    end(ins, key)
                down(0, 1)
                with pe.Fori(1, 4) as it:
                    down(it, 0)
                    down(it, 1)

            for i in range(KD // 2):
                u = PLE_U + 5 * i
                pair(u, PLE_P + i, 5 * i, KD, xhi, xlo, i % 2,
                     (lambda j: pe.wait_ge(sem("xlo_ready"), 2 * KD + 4 * (j + 1))) if i == 0 else None)
                if i == 0:
                    pe.wait_ge(sem("plo_ready"), 1)
                key = ("emb", i)
                out = begin(key)
                unit(u + 4, (5 * i + 4) % RING, None, 0, PLE // P, True, True, phi, plo, out)
                if i == 0:
                    norm(2)
            pe.wait_ge(sem("xg_ready"), KD)
            norm(3)
            for f in range(6):
                key = ("fin", f)
                c0, n = CHUNKS[f // 2]
                out = begin(key)
                for t in range(8):
                    ins = pe.transpose(out[0:n, t // 4, (t % 4) * P:(t % 4 + 1) * P], xg[:, 8 * (f % 2) + t, c0:c0 + n], ident[:])
                end(ins, key)


_INS = ["x_prompt", "x_sample", "state_conv", "state_delta", "state_s5_re", "state_s5_im", "p_prompt", "p_sample",
        "g_mix", "w_in", "conv_w", "a_log", "dt_bias", "onorm_w", "s5_a_re", "s5_a_im", "s5_b_re", "s5_b_im",
        "s5_c_re", "s5_c_im", "s5_d", "s5_log_dt", "w_glu", "b_glu", "w_a", "w_b", "w_out", "g_ffn", "w_gate",
        "w_up", "w_down", "g_ple", "w_ple", "w_ple_gate", "g_final"]
_OUTS = [("y_prompt", (1, NPR, D)), ("y_sample", (NB, NL, D)), ("conv_prompt", (1, 1, CW - 1, CCH)),
         ("delta_prompt", (1, 1, H, P, P)), ("s5_re_prompt", (1, 1, 64, ST)), ("s5_im_prompt", (1, 1, 64, ST)),
         ("conv_sample", (1, NB, CW - 1, CCH)), ("delta_sample", (1, NB, H, P, P)),
         ("s5_re_sample", (1, NB, 64, ST)), ("s5_im_sample", (1, NB, 64, ST))]


def kernel(**inputs):
    import numpy as np
    import concourse.bacc as bacc
    from concourse.bass_utils import run_bass_kernel_spmd

    nc = bacc.Bacc("TRN2", target_bir_lowering=False, num_devices=1)
    arrays, args = {}, []
    for name in _INS:
        a = np.ascontiguousarray(inputs[name])
        arrays[f"in_{name}"] = a
        args.append(nc.dram_tensor(f"in_{name}", a.shape, mybir.dt.from_np(a.dtype), kind="ExternalInput").ap())
    for name, shape in _OUTS:
        args.append(nc.dram_tensor(f"out_{name}", shape, F32, kind="ExternalOutput").ap())
    hybrid_layer(nc, *args)
    r = run_bass_kernel_spmd(nc, [arrays], core_ids=[0])
    return tuple(r.results[0][f"out_{name}"] for name, _ in _OUTS)
```
